# Optimizing a Trainium2 kernel written in Bass

```python
import math
import jax, jax.numpy as jnp
from jax import lax
import numpy as np

D_MODEL = 1024
BATCH = 1
SEQ = 1024
DEPTH = 1

MEM_LEN = 256
EPS = 1e-6
ROPE_BASE = 10000.0

RET_HEADS = 8
RET_QK_WIDTH = D_MODEL // 2
RET_V_WIDTH = D_MODEL
RET_DK = RET_QK_WIDTH // RET_HEADS
RET_DV = RET_V_WIDTH // RET_HEADS
CHUNK = 128

S5_WIDTH = D_MODEL
S5_GROUP = 16
S5_GROUPS = S5_WIDTH // S5_GROUP
S5_STATE = 64

D_MIX = RET_V_WIDTH + S5_WIDTH
IN_COLS = 2 * RET_QK_WIDTH + 2 * RET_V_WIDTH + 2 * S5_WIDTH
SPLITS = (RET_QK_WIDTH, 2 * RET_QK_WIDTH, 2 * RET_QK_WIDTH + RET_V_WIDTH,
          2 * RET_QK_WIDTH + 2 * RET_V_WIDTH, 2 * RET_QK_WIDTH + 2 * RET_V_WIDTH + S5_WIDTH)

XA_HEADS = 4
XA_DH = D_MODEL // XA_HEADS


def rms_norm(x, g):
    xf = x.astype(jnp.float32)
    y = xf * lax.rsqrt(jnp.mean(xf * xf, axis=-1, keepdims=True) + EPS)
    return (y * g.astype(jnp.float32)).astype(x.dtype)

def rotary(x, positions):
    half = x.shape[-1] // 2
    inv = ROPE_BASE ** (-jnp.arange(half, dtype=jnp.float32) / half)
    ang = positions.astype(jnp.float32)[:, :, None, None] * inv
    cos, sin = jnp.cos(ang), jnp.sin(ang)
    x1, x2 = x[..., :half], x[..., half:]
    return jnp.concatenate([x1 * cos - x2 * sin, x1 * sin + x2 * cos], axis=-1)

def retention(q, k, v, gn_g):
    B, L, H, DK = q.shape
    DV = v.shape[-1]
    nC = L // CHUNK
    q = q.astype(jnp.float32)
    k = k.astype(jnp.float32) * DK ** -0.5
    v = v.astype(jnp.float32)
    log_g = jnp.log1p(-jnp.exp2(-5.0 - jnp.arange(H, dtype=jnp.float32)))
    qc = q.reshape(B, nC, CHUNK, H, DK)
    kc = k.reshape(B, nC, CHUNK, H, DK)
    vc = v.reshape(B, nC, CHUNK, H, DV)
    j = jnp.arange(CHUNK, dtype=jnp.float32)
    diff = j[:, None] - j[None, :]
    decay = jnp.where(diff[None] >= 0.0,
                      jnp.exp(log_g[:, None, None] * jnp.maximum(diff, 0.0)[None]), 0.0)
    scores = jnp.einsum('bnihd,bnjhd->bnhij', qc, kc) * decay
    inner = jnp.einsum('bnhij,bnjhe->bnihe', scores, vc)
    k_w = jnp.exp(log_g[None, :] * (CHUNK - 1.0 - j)[:, None])
    kv = jnp.einsum('bnjhd,jh,bnjhe->bnhde', kc, k_w, vc)
    chunk_decay = jnp.exp(log_g * CHUNK)[None, :, None, None]

    def step(R, kv_n):
        return chunk_decay * R + kv_n, R

    _, R_prev = lax.scan(step, jnp.zeros((B, H, DK, DV), jnp.float32), jnp.moveaxis(kv, 1, 0))
    R_prev = jnp.moveaxis(R_prev, 0, 1)
    q_w = jnp.exp(log_g[None, :] * (j + 1.0)[:, None])
    cross = jnp.einsum('bnihd,ih,bnhde->bnihe', qc, q_w, R_prev)
    o = (inner + cross).reshape(B, L, H, DV)
    mu = jnp.mean(o, axis=-1, keepdims=True)
    var = jnp.mean(jnp.square(o - mu), axis=-1, keepdims=True)
    o = ((o - mu) * lax.rsqrt(var + EPS)).reshape(B, L, H * DV)
    return o * gn_g.astype(jnp.float32)

def s5_branch(u, a_re, a_im, log_dt, b_re, b_im, c_re, c_im, d, glu_w, glu_b):
    Bsz, L, W = u.shape
    f32 = jnp.float32
    uf = u.astype(f32)
    ug = uf.reshape(Bsz, L, S5_GROUPS, S5_GROUP)
    dt = jnp.exp(log_dt.astype(f32))[:, None]
    ar, ai = a_re.astype(f32), a_im.astype(f32)
    mag = jnp.exp(ar * dt)
    abar_re = mag * jnp.cos(ai * dt)
    abar_im = mag * jnp.sin(ai * dt)
    den = ar * ar + ai * ai
    nr, ni = abar_re - 1.0, abar_im
    f_re = (nr * ar + ni * ai) / den
    f_im = (ni * ar - nr * ai) / den
    br, bi = b_re.astype(f32), b_im.astype(f32)
    bb_re = f_re[..., None] * br - f_im[..., None] * bi
    bb_im = f_re[..., None] * bi + f_im[..., None] * br
    bu_re = jnp.einsum('blgp,gnp->blgn', ug, bb_re)
    bu_im = jnp.einsum('blgp,gnp->blgn', ug, bb_im)
    a_seq_re = jnp.broadcast_to(abar_re[None, None], (1, L, S5_GROUPS, S5_STATE))
    a_seq_im = jnp.broadcast_to(abar_im[None, None], (1, L, S5_GROUPS, S5_STATE))

    def combine(e1, e2):
        a1r, a1i, b1r, b1i = e1
        a2r, a2i, b2r, b2i = e2
        return (a2r * a1r - a2i * a1i,
                a2r * a1i + a2i * a1r,
                a2r * b1r - a2i * b1i + b2r,
                a2r * b1i + a2i * b1r + b2i)

    _, _, xr, xi = lax.associative_scan(combine, (a_seq_re, a_seq_im, bu_re, bu_im), axis=1)
    y = (jnp.einsum('blgn,gpn->blgp', xr, c_re.astype(f32))
         - jnp.einsum('blgn,gpn->blgp', xi, c_im.astype(f32)))
    y = y.reshape(Bsz, L, W) + d.astype(f32) * uf
    y = jax.nn.gelu(y)
    y = y * jax.nn.sigmoid(y @ glu_w.astype(f32) + glu_b.astype(f32))
    return y

def first_inputs(seed: int = 0) -> dict:
    key = jax.random.key(seed)
    ks = jax.random.split(key, 24)
    f32 = jnp.float32

    def nrm(k, shape, scale):
        return jax.random.normal(k, shape, f32) * scale

    Ld = DEPTH
    G, N, P = S5_GROUPS, S5_STATE, S5_GROUP
    x = nrm(ks[0], (BATCH, SEQ, D_MODEL), 1.0)
    mem = nrm(ks[1], (BATCH, MEM_LEN, D_MODEL), 1.0)
    positions = jnp.broadcast_to(jnp.arange(SEQ, dtype=jnp.int32)[None, :], (BATCH, SEQ))
    norm1_g = 1.0 + nrm(ks[2], (Ld, D_MODEL), 0.02)
    w_in = nrm(ks[3], (Ld, D_MODEL, IN_COLS), D_MODEL ** -0.5)
    ret_gn_g = 1.0 + nrm(ks[4], (Ld, RET_V_WIDTH), 0.02)
    n_idx = jnp.arange(N, dtype=f32)
    s5_a_re = -0.5 + nrm(ks[5], (Ld, G, N), 0.01)
    s5_a_im = math.pi * n_idx[None, None, :] + nrm(ks[6], (Ld, G, N), 0.01)
    s5_log_dt = jax.random.uniform(ks[7], (Ld, G), f32, math.log(1e-3), math.log(1e-1))
    s5_b_re = nrm(ks[8], (Ld, G, N, P), (2.0 * P) ** -0.5)
    s5_b_im = nrm(ks[9], (Ld, G, N, P), (2.0 * P) ** -0.5)
    s5_c_re = nrm(ks[10], (Ld, G, P, N), N ** -0.5)
    s5_c_im = nrm(ks[11], (Ld, G, P, N), N ** -0.5)
    s5_d = nrm(ks[12], (Ld, S5_WIDTH), 0.5)
    s5_glu_w = nrm(ks[13], (Ld, S5_WIDTH, S5_WIDTH), S5_WIDTH ** -0.5)
    s5_glu_b = nrm(ks[14], (Ld, S5_WIDTH), 0.01)
    w_out = nrm(ks[15], (Ld, D_MIX, D_MODEL), D_MIX ** -0.5)
    norm2_g = 1.0 + nrm(ks[16], (Ld, D_MODEL), 0.02)
    norm_mem_g = 1.0 + nrm(ks[17], (Ld, D_MODEL), 0.02)
    xa_wq = nrm(ks[18], (Ld, D_MODEL, D_MODEL), D_MODEL ** -0.5)
    xa_wk = nrm(ks[19], (Ld, D_MODEL, D_MODEL), D_MODEL ** -0.5)
    xa_wv = nrm(ks[20], (Ld, D_MODEL, D_MODEL), D_MODEL ** -0.5)
    xa_wo = nrm(ks[21], (Ld, D_MODEL, D_MODEL), D_MODEL ** -0.5)
    norm_f_g = 1.0 + nrm(ks[22], (D_MODEL,), 0.02)
    return {'x': x, 'mem': mem, 'positions': positions, 'norm1_g': norm1_g, 'w_in': w_in,
            'ret_gn_g': ret_gn_g, 's5_a_re': s5_a_re, 's5_a_im': s5_a_im, 's5_log_dt': s5_log_dt,
            's5_b_re': s5_b_re, 's5_b_im': s5_b_im, 's5_c_re': s5_c_re, 's5_c_im': s5_c_im,
            's5_d': s5_d, 's5_glu_w': s5_glu_w, 's5_glu_b': s5_glu_b, 'w_out': w_out,
            'norm2_g': norm2_g, 'norm_mem_g': norm_mem_g, 'xa_wq': xa_wq, 'xa_wk': xa_wk,
            'xa_wv': xa_wv, 'xa_wo': xa_wo, 'norm_f_g': norm_f_g}

def first_block(x, mem, positions, norm1_g, w_in, ret_gn_g, s5_a_re, s5_a_im, s5_log_dt,
              s5_b_re, s5_b_im, s5_c_re, s5_c_im, s5_d, s5_glu_w, s5_glu_b, w_out,
              norm2_g, norm_mem_g, xa_wq, xa_wk, xa_wv, xa_wo, norm_f_g):
    B, L, _ = x.shape
    M = mem.shape[1]
    for l in range(DEPTH):
        h = rms_norm(x, norm1_g[l])
        proj = h @ w_in[l]
        q, k, v, g_ret, u, g_s5 = jnp.split(proj, SPLITS, axis=-1)
        q = rotary(q.reshape(B, L, RET_HEADS, RET_DK), positions)
        k = rotary(k.reshape(B, L, RET_HEADS, RET_DK), positions)
        v = v.reshape(B, L, RET_HEADS, RET_DV)
        ret = retention(q, k, v, ret_gn_g[l]).astype(x.dtype) * jax.nn.silu(g_ret)
        ssm = s5_branch(u, s5_a_re[l], s5_a_im[l], s5_log_dt[l], s5_b_re[l], s5_b_im[l],
                        s5_c_re[l], s5_c_im[l], s5_d[l], s5_glu_w[l],
                        s5_glu_b[l]).astype(x.dtype) * jax.nn.silu(g_s5)
        x = x + jnp.concatenate([ret, ssm], axis=-1) @ w_out[l]
        h2 = rms_norm(x, norm2_g[l])
        m = rms_norm(mem, norm_mem_g[l])
        qa = (h2 @ xa_wq[l]).reshape(B, L, XA_HEADS, XA_DH)
        ka = (m @ xa_wk[l]).reshape(B, M, XA_HEADS, XA_DH)
        va = (m @ xa_wv[l]).reshape(B, M, XA_HEADS, XA_DH)
        s = jnp.einsum('blhd,bmhd->bhlm', qa, ka).astype(jnp.float32) * XA_DH ** -0.5
        p = jax.nn.softmax(s, axis=-1).astype(va.dtype)
        o = jnp.einsum('bhlm,bmhd->blhd', p, va).reshape(B, L, XA_HEADS * XA_DH)
        x = x + o @ xa_wo[l]
    return rms_norm(x, norm_f_g)


MIX_WIDTH = D_MODEL
N_MIXERS = 4
GROUP_WIDTH = MIX_WIDTH // N_MIXERS
HEADS_PER_GROUP = 4
HEAD_DIM = GROUP_WIDTH // HEADS_PER_GROUP
SGU_CHUNK = 128
SC_WIDTH = 3
DN_CONV_WIDTH = 4
DN_CHUNK = 64
GLA_CHUNK = 64
GLA_GATE_RANK = 16
GLA_GATE_TEMP = 16.0
D_FF = ((8 * D_MODEL // 3 + 255) // 256) * 256

_G = GROUP_WIDTH
_H = HEADS_PER_GROUP
IN_SPLITS = (_G, _G,
             _G, _G, _G,
             _G, _G, _G, _H, _H, _G,
             _G, _G, _G, GLA_GATE_RANK, _G)
IN_COLS_2 = sum(IN_SPLITS)


def rmsnorm(x, w):
    xf = x.astype(jnp.float32)
    y = xf * lax.rsqrt(jnp.mean(xf * xf, axis=-1, keepdims=True) + EPS)
    return (y * w.astype(jnp.float32)).astype(x.dtype)

def layernorm(x, w, b):
    xf = x.astype(jnp.float32)
    mu = jnp.mean(xf, axis=-1, keepdims=True)
    var = jnp.mean(jnp.square(xf - mu), axis=-1, keepdims=True)
    y = (xf - mu) * lax.rsqrt(var + EPS)
    return (y * w.astype(jnp.float32) + b.astype(jnp.float32)).astype(x.dtype)

def l2norm(t):
    return t * lax.rsqrt(jnp.sum(t * t, axis=-1, keepdims=True) + EPS)

def causal_dwconv(x, w):
    k_width, ch = w.shape
    return lax.conv_general_dilated(
        x, w[:, None, :].astype(x.dtype), window_strides=(1,),
        padding=[(k_width - 1, 0)], dimension_numbers=('NWC', 'WIO', 'NWC'),
        feature_group_count=ch)

def to_heads(t):
    b, s, _ = t.shape
    return t.reshape(b, s, HEADS_PER_GROUP, HEAD_DIM).astype(jnp.float32)

def to_chunks(t, c):
    b, s = t.shape[:2]
    t = t.reshape(b, s // c, c, *t.shape[2:])
    return jnp.moveaxis(t, 3, 1)

def from_chunks(t):
    b, h, n, c, d = t.shape
    return jnp.moveaxis(t, 1, 3).reshape(b, n * c, h, d)

def sgu_mixer(u, v, ln_w, ln_b, w_s, b_s):
    bsz, s, g = u.shape
    n = s // SGU_CHUNK
    u = jax.nn.gelu(u)
    v = layernorm(jax.nn.gelu(v), ln_w, ln_b)
    vc = v.reshape(bsz, n, SGU_CHUNK, HEADS_PER_GROUP, HEAD_DIM)
    mask = jnp.tril(jnp.ones((SGU_CHUNK, SGU_CHUNK), dtype=bool))
    ws = jnp.where(mask, w_s, 0.0).astype(v.dtype)
    mixed = jnp.einsum('hts,bnshd->bnthd', ws, vc) + b_s.T.astype(v.dtype)[None, None, :, :, None]
    return u * mixed.reshape(bsz, s, g)

def short_conv_mixer(gate_b, gate_c, h, w_conv):
    return gate_b * causal_dwconv(gate_c * h, w_conv)

def chunk_gated_delta_rule(q, k, v, g, beta):
    bsz, s, h, dk = q.shape
    dv = v.shape[-1]
    c = DN_CHUNK
    q, k, v = to_chunks(q, c), to_chunks(k, c), to_chunks(v, c)
    g, beta = to_chunks(g, c), to_chunks(beta, c)
    q = q * dk ** -0.5
    gc = jnp.cumsum(g, axis=-1)
    causal = jnp.tril(jnp.ones((c, c), dtype=bool))
    strict = jnp.tril(jnp.ones((c, c), dtype=bool), k=-1)
    decay = jnp.exp(jnp.where(causal, gc[..., :, None] - gc[..., None, :], -jnp.inf))
    kb = k * beta[..., None]
    low = jnp.where(strict, jnp.einsum('bhncd,bhnsd->bhncs', kb, k) * decay, 0.0)
    rhs = jnp.concatenate([v * beta[..., None], kb * jnp.exp(gc)[..., None]], axis=-1)
    sol = lax.linalg.triangular_solve(low, rhs, left_side=True, lower=True, unit_diagonal=True)
    u, w = sol[..., :dv], sol[..., dv:]
    attn = jnp.einsum('bhncd,bhnsd->bhncs', q, k) * decay
    qg = q * jnp.exp(gc)[..., None]
    k_dec = k * jnp.exp(gc[..., -1:] - gc)[..., None]
    chunk_dec = jnp.exp(gc[..., -1])

    def step(state, inp):
        qg_n, w_n, u_n, attn_n, kd_n, dec_n = inp
        v_new = u_n - jnp.einsum('bhcd,bhde->bhce', w_n, state)
        o = jnp.einsum('bhcd,bhde->bhce', qg_n, state) + jnp.einsum('bhcs,bhse->bhce', attn_n, v_new)
        state = state * dec_n[..., None, None] + jnp.einsum('bhcd,bhce->bhde', kd_n, v_new)
        return state, o

    s0 = jnp.zeros((bsz, h, dk, dv), jnp.float32)
    xs = tuple(jnp.moveaxis(t, 2, 0) for t in (qg, w, u, attn, k_dec, chunk_dec))
    _, o = lax.scan(step, s0, xs)
    return from_chunks(jnp.moveaxis(o, 0, 2))

def deltanet_mixer(q, k, v, a, b, z, conv_w, a_log, dt_bias, norm_w):
    bsz, s, _ = q.shape
    qkv = jax.nn.silu(causal_dwconv(jnp.concatenate([q, k, v], axis=-1), conv_w))
    q, k, v = jnp.split(qkv, 3, axis=-1)
    q, k, v = l2norm(to_heads(q)), l2norm(to_heads(k)), to_heads(v)
    g = -jnp.exp(a_log.astype(jnp.float32)) * jax.nn.softplus(a.astype(jnp.float32) + dt_bias.astype(jnp.float32))
    beta = jax.nn.sigmoid(b.astype(jnp.float32))
    o = chunk_gated_delta_rule(q, k, v, g, beta)
    o = rmsnorm(o, norm_w) * jax.nn.silu(to_heads(z))
    return o.reshape(bsz, s, GROUP_WIDTH).astype(z.dtype)

def chunk_gla(q, k, v, log_a):
    bsz, s, h, dk = q.shape
    dv = v.shape[-1]
    c = GLA_CHUNK
    q, k, v, log_a = (to_chunks(t, c) for t in (q, k, v, log_a))
    q = q * dk ** -0.5
    gcum = jnp.cumsum(log_a, axis=3)
    g_mid = gcum[:, :, :, c // 2:c // 2 + 1, :]
    qa = q * jnp.exp(gcum - g_mid)
    ka = k * jnp.exp(g_mid - gcum)
    causal = jnp.tril(jnp.ones((c, c), dtype=bool))
    attn = jnp.where(causal, jnp.einsum('bhncd,bhnsd->bhncs', qa, ka), 0.0)
    o_intra = jnp.einsum('bhncs,bhnse->bhnce', attn, v)
    qg = q * jnp.exp(gcum)
    k_last = k * jnp.exp(gcum[:, :, :, -1:, :] - gcum)
    chunk_dec = jnp.exp(gcum[:, :, :, -1, :])

    def step(state, inp):
        qg_n, kl_n, v_n, dec_n = inp
        o = jnp.einsum('bhcd,bhde->bhce', qg_n, state)
        state = state * dec_n[..., :, None] + jnp.einsum('bhcd,bhce->bhde', kl_n, v_n)
        return state, o

    s0 = jnp.zeros((bsz, h, dk, dv), jnp.float32)
    xs = tuple(jnp.moveaxis(t, 2, 0) for t in (qg, k_last, v, chunk_dec))
    _, o_inter = lax.scan(step, s0, xs)
    return from_chunks(o_intra + jnp.moveaxis(o_inter, 0, 2))

def gla_mixer(q, k, v, g_lr, z, w_gate2, gate_bias, norm_w):
    bsz, s, _ = q.shape
    pre = jnp.einsum('btr,rg->btg', g_lr, w_gate2.astype(g_lr.dtype)).astype(jnp.float32) + gate_bias.astype(jnp.float32)
    log_a = jax.nn.log_sigmoid(pre) / GLA_GATE_TEMP
    o = chunk_gla(to_heads(q), to_heads(k), to_heads(v), to_heads(log_a))
    o = rmsnorm(o, norm_w) * jax.nn.silu(to_heads(z))
    return o.reshape(bsz, s, GROUP_WIDTH).astype(z.dtype)

def swiglu(h, w_gate_up, w_down):
    gu = h @ w_gate_up
    gate, up = jnp.split(gu, 2, axis=-1)
    return (jax.nn.silu(gate) * up) @ w_down

def second_inputs(seed: int = 0) -> dict:
    key = jax.random.key(seed)
    ks = jax.random.split(key, 24)
    f32 = jnp.float32

    def nrm(k, shape, scale):
        return jax.random.normal(k, shape, f32) * scale

    def gain(k, shape):
        return 1.0 + 0.02 * jax.random.normal(k, shape, f32)

    dt = jnp.exp(jax.random.uniform(ks[11], (DEPTH, HEADS_PER_GROUP), f32, np.log(1e-3), np.log(1e-1)))
    return {
        "x": jax.random.normal(ks[0], (BATCH, SEQ, D_MODEL), f32),
        "norm1_w": gain(ks[1], (DEPTH, D_MODEL)),
        "w_in": nrm(ks[2], (DEPTH, D_MODEL, IN_COLS_2), D_MODEL ** -0.5),
        "sgu_ln_w": gain(ks[3], (DEPTH, GROUP_WIDTH)),
        "sgu_ln_b": nrm(ks[4], (DEPTH, GROUP_WIDTH), 0.02),
        "sgu_w_spatial": nrm(ks[5], (DEPTH, HEADS_PER_GROUP, SGU_CHUNK, SGU_CHUNK), SGU_CHUNK ** -0.5),
        "sgu_b_spatial": gain(ks[6], (DEPTH, HEADS_PER_GROUP, SGU_CHUNK)),
        "sc_conv_w": nrm(ks[7], (DEPTH, SC_WIDTH, GROUP_WIDTH), SC_WIDTH ** -0.5),
        "dn_conv_w": nrm(ks[8], (DEPTH, DN_CONV_WIDTH, 3 * GROUP_WIDTH), DN_CONV_WIDTH ** -0.5),
        "dn_a_log": jnp.log(jax.random.uniform(ks[9], (DEPTH, HEADS_PER_GROUP), f32, 1.0, 16.0)),
        "dn_dt_bias": dt + jnp.log(-jnp.expm1(-dt)),
        "dn_norm_w": gain(ks[10], (DEPTH, HEAD_DIM)),
        "gla_w_gate2": nrm(ks[12], (DEPTH, GLA_GATE_RANK, GROUP_WIDTH), GLA_GATE_RANK ** -0.5),
        "gla_gate_bias": nrm(ks[13], (DEPTH, GROUP_WIDTH), 0.1),
        "gla_norm_w": gain(ks[14], (DEPTH, HEAD_DIM)),
        "w_out": nrm(ks[15], (DEPTH, MIX_WIDTH, D_MODEL), MIX_WIDTH ** -0.5),
        "norm2_w": gain(ks[16], (DEPTH, D_MODEL)),
        "w_gate_up": nrm(ks[17], (DEPTH, D_MODEL, 2 * D_FF), D_MODEL ** -0.5),
        "w_down": nrm(ks[18], (DEPTH, D_FF, D_MODEL), D_FF ** -0.5),
        "final_norm_w": gain(ks[19], (D_MODEL,)),
    }

def second_block(x, norm1_w, w_in, sgu_ln_w, sgu_ln_b, sgu_w_spatial, sgu_b_spatial, sc_conv_w,
              dn_conv_w, dn_a_log, dn_dt_bias, dn_norm_w, gla_w_gate2, gla_gate_bias, gla_norm_w,
              w_out, norm2_w, w_gate_up, w_down, final_norm_w):
    split_idx = [int(i) for i in np.cumsum(IN_SPLITS)[:-1]]
    for l in range(DEPTH):
        h = rmsnorm(x, norm1_w[l])
        p = h @ w_in[l]
        (a_u, a_v, b_b, b_c, b_h, c_q, c_k, c_v, c_a, c_b, c_z,
         d_q, d_k, d_v, d_g, d_z) = jnp.split(p, split_idx, axis=-1)
        y_a = sgu_mixer(a_u, a_v, sgu_ln_w[l], sgu_ln_b[l], sgu_w_spatial[l], sgu_b_spatial[l])
        y_b = short_conv_mixer(b_b, b_c, b_h, sc_conv_w[l])
        y_c = deltanet_mixer(c_q, c_k, c_v, c_a, c_b, c_z, dn_conv_w[l], dn_a_log[l], dn_dt_bias[l], dn_norm_w[l])
        y_d = gla_mixer(d_q, d_k, d_v, d_g, d_z, gla_w_gate2[l], gla_gate_bias[l], gla_norm_w[l])
        mix = jnp.concatenate([y_a, y_b.astype(x.dtype), y_c, y_d], axis=-1)
        x = x + (mix @ w_out[l]).astype(x.dtype)
        x = x + swiglu(rmsnorm(x, norm2_w[l]), w_gate_up[l], w_down[l]).astype(x.dtype)
    return rmsnorm(x, final_norm_w)


_first_inputs = second_inputs


def second_inputs(seed=0):
    import zlib

    import numpy as np

    out = dict(_first_inputs(seed))
    spreads = {}
    factors = {'sgu_ln_w': 8.0,
     'sgu_ln_b': 8.0,
     'sgu_b_spatial': 8.0,
     'dn_norm_w': 8.0,
     'gla_gate_bias': 4.631,
     'gla_norm_w': 8.0,
     'norm2_w': 4.624,
     'final_norm_w': 2.838}
    for name, (base, spread) in spreads.items():
        noise = np.random.default_rng([zlib.crc32(name.encode()), seed]).standard_normal(out[name].shape)
        drawn = base * np.exp(spread * noise) if base else spread * noise
        out[name] = __import__('jax').numpy.asarray(drawn.astype(out[name].dtype))
    for name, factor in factors.items():
        out[name] = (out[name] * factor).astype(out[name].dtype)
    return out


_narrow_inputs = second_inputs


def second_inputs(seed=0):

    out = dict(_narrow_inputs(seed))
    wider = {'sgu_ln_w': 6.64,
     'sgu_ln_b': 6.79,
     'sgu_b_spatial': 4.19,
     'dn_norm_w': 4.36,
     'gla_norm_w': 4.67,
     'final_norm_w': 3.19}
    for name, times in wider.items():
        mean = out[name].mean()
        out[name] = (mean + times * (out[name] - mean)).astype(out[name].dtype)
    return out


def setup_inputs(seed=0):
    out = dict(first_inputs(seed))
    for name, value in second_inputs(seed + 1).items():
        if name != "x":
            out[name + "_2"] = value
    return out


def reference(
    x, mem, positions, norm1_g, w_in, ret_gn_g, s5_a_re, s5_a_im, s5_log_dt, s5_b_re, s5_b_im,
    s5_c_re, s5_c_im, s5_d, s5_glu_w, s5_glu_b, w_out, norm2_g, norm_mem_g, xa_wq, xa_wk, xa_wv,
    xa_wo, norm_f_g, norm1_w_2, w_in_2, sgu_ln_w_2, sgu_ln_b_2, sgu_w_spatial_2,
    sgu_b_spatial_2, sc_conv_w_2, dn_conv_w_2, dn_a_log_2, dn_dt_bias_2, dn_norm_w_2,
    gla_w_gate2_2, gla_gate_bias_2, gla_norm_w_2, w_out_2, norm2_w_2, w_gate_up_2, w_down_2,
    final_norm_w_2,
):
    x = first_block(
        x, mem, positions, norm1_g, w_in, ret_gn_g, s5_a_re, s5_a_im, s5_log_dt, s5_b_re,
        s5_b_im, s5_c_re, s5_c_im, s5_d, s5_glu_w, s5_glu_b, w_out, norm2_g, norm_mem_g, xa_wq,
        xa_wk, xa_wv, xa_wo, norm_f_g,
    )
    return second_block(
        x, norm1_w_2, w_in_2, sgu_ln_w_2, sgu_ln_b_2, sgu_w_spatial_2, sgu_b_spatial_2,
        sc_conv_w_2, dn_conv_w_2, dn_a_log_2, dn_dt_bias_2, dn_norm_w_2, gla_w_gate2_2,
        gla_gate_bias_2, gla_norm_w_2, w_out_2, norm2_w_2, w_gate_up_2, w_down_2,
        final_norm_w_2,
    )


_drawn_inputs = setup_inputs


def setup_inputs(seed=0):
    import zlib

    import numpy as np

    out = dict(_drawn_inputs(seed))
    spreads = {}
    factors = {'ret_gn_g': 3.233,
     's5_a_re': 8.0,
     's5_b_re': 3.42,
     's5_b_im': 3.397,
     's5_c_re': 3.347,
     's5_c_im': 3.45,
     's5_glu_w': 2.692,
     's5_glu_b': 8.0,
     'norm2_g': 8.0,
     'norm_mem_g': 8.0}
    for name, (base, spread) in spreads.items():
        noise = np.random.default_rng([zlib.crc32(name.encode()), seed]).standard_normal(out[name].shape)
        drawn = base * np.exp(spread * noise) if base else spread * noise
        out[name] = __import__('jax').numpy.asarray(drawn.astype(out[name].dtype))
    for name, factor in factors.items():
        out[name] = (out[name] * factor).astype(out[name].dtype)
    return out
```

```python
import math
from contextlib import ExitStack

import numpy as np

import concourse.bass as bass
from concourse import mybir

F32 = mybir.dt.float32
F32R = mybir.dt.float32r
I32 = mybir.dt.int32
ALU = mybir.AluOpType
ACT = mybir.ActivationFunctionType
AX = mybir.AxisListType

P = 128
D = 1024
L = 1024
TT = L // P
KT = D // P
MEM = 256
EPS = 1e-6
HALF = 512

RH, RDK, RDV = 8, 64, 128
SG, SP_, SN = 64, 16, 64
SC = 8
NCH = L // SC
PAIRS = SG // 2
XH, XD = 4, 256
GW, GH, GD = 256, 4, 64
FF = 2816
FFB = FF // 256

TWO_PI = 2 * math.pi
PI_A = 6.28125
PI_B = 0.0019350051879882812
PI_C = TWO_PI - PI_A - PI_B
ROUND = 12582912.0
PI_SAFE = 3.1415925

C_AU, C_AV, C_CA, C_CB, C_CZ, C_DG, C_DQ, C_DK, C_DV, C_DZ, C_TOK = (
    0, 256, 512, 516, 520, 776, 792, 1048, 1304, 1560, 1816)


PTOK0 = (C_AU, C_CA, C_DQ, C_DV)


SHARED = {}
for later, earlier, total in (e.split() for e in (
        "gt s5b_t 8, pre s5b_mm 8, cum s5y_t 8, tr s5y_mm 8, a s5y_tt 8, kv s5_bt_t 16, q_t sg_mm 8, av sg_t 8,"
        "turn s5_r 1, gtc s5b_ut 8, ex s5y_ut 8, ln s5y_yo 8, ee s5_bt 16, trc s5_cp 4, q sg_gl 8, zs sg_root 8,"
        "root sg_hi 9, hi s5_act 4, zero s5_prm 1, ab s5b_s 8, la s5b_ur 8, kg s5y_ur 8, at s5y_ys 16, s s5_xpw 16,"
        "ms sg_var 8, on sg_vn 8, og sg_y 16, lo s5_small 4, in0 s5y_in0 192, in1 s5y_in1 192,"
        "par s5b_in 256").split(",")):
    SHARED["gl_" + later] = (earlier, int(total))
for later, earlier, total in (e.split() for e in (
        "gm r_turn 8, dec r_sc 8, tr r_o 8, la r_kv 8, c1 r_back 8, ex r_qkt 8, rt r_root 8, trc r_hi 8, e1 r_trig 2,"
        "ag r_scr 8, ss r_var 8, kk r_on 8, s r_rst 25, lt r_g 16, ct r_ang 1, in0 rq_in 128, in1 rv_in 128,"
        "par rc_in 32").split(",")):
    SHARED["dn_" + later] = (earlier, int(total))
for later, earlier, total in (e.split() for e in (
        "sg_w xa_s 8, sg_mm xa_t 8, sg_t xa_o 8, sg_gl xa_pt 8, sg_root xa_hi 8, sg_hi xa_e 32, sg_wt xa_nm 8,"
        "sg_var xa_p 8, sg_vn xa_lo 8, sg_y r_ab 16, sg_lo r_rot 8, su_in0 xa_q0 64, su_in1 xa_q1 64,"
        "sg_in xa_kv 32").split(",")):
    SHARED[later] = (earlier, int(total))


def shape_constants():
    i = np.arange(P)
    row, col = i[:, None], i[None, :]
    same = (row // 64) == (col // 64)
    f = np.float32
    tabs = {"ident": np.eye(P, dtype=f)}
    tabs["upto"] = (same & (row <= col)).astype(f)
    tabs["later"] = (same & (row > col)).astype(f)
    tabs["before"] = (same & (row < col)).astype(f)
    tabs["frommid"] = tabs["upto"] - (same & (row % 64 <= 32)).astype(f)
    tabs["first"] = np.broadcast_to(row < 64, (P, P)).astype(f)
    tabs["second"] = np.broadcast_to(row >= 64, (P, P)).astype(f)
    tabs["causal"] = (row <= col).astype(f)
    for b in (1, 2, 4, 8, 16, 32):
        m = ((row // (2 * b)) == (col // (2 * b))) & (col % (2 * b) >= b) & (row % (2 * b) < b)
        tabs[f"join{b}"] = m.astype(f)
    base = np.concatenate([tabs[k] for k in tabs], axis=1)
    names = list(tabs)
    gam = 1.0 - 2.0 ** (-5.0 - np.arange(RH))
    mask = np.where(row <= col, 1.0, 0.0)
    by_parity = np.r_[0:RH:2, 1:RH:2]
    rmask = mask[:, None, :] * (gam ** -128.0)[by_parity][None, :, None]
    qw = gam[None, :] ** (i[:, None] + 1.0)
    kw = gam[None, :] ** (127.0 - i[:, None]) * RDK ** -0.5
    dec = np.empty((P, RH // 2))
    dec[:64] = gam[0::2] ** 128.0
    dec[64:] = gam[1::2] ** 128.0
    inv = (np.float32(10000.0) ** (-np.arange(32, dtype=f) / f(32))).astype(f)
    inv = np.broadcast_to(inv[None, :], (P, 32))
    ret = np.concatenate([rmask.reshape(P, -1), qw, kw, dec, inv], axis=1).astype(f)
    place = np.zeros((SP_, P + SP_), f)
    place[np.arange(SP_), P - SP_ + np.arange(SP_)] = 1.0
    place[np.arange(SP_), P + np.arange(SP_)] = 1.0
    return base.astype(f), names, ret, place


def build(nc, I, out):
    dram = {}

    def scratch(name, shape):
        dram[name] = nc.dram_tensor(name, shape, F32, kind="Internal").ap()
        return dram[name]

    qk_d = scratch("qk_d", (L, D))
    v_d = scratch("v_d", (L, D))
    u_d = scratch("u_d", (L, D))
    gret_d = scratch("gret_d", (D, L))
    gs5_d = scratch("gs5_d", (D, L))
    bct_d = scratch("bct_d", (P, PAIRS, 2, P))
    toep_d = scratch("toep_d", (P, SC, SG * SP_))
    cc_d = scratch("cc_d", (P, PAIRS, 2, P))
    yt_d = scratch("yt_d", (D, L))
    st_d = scratch("st_d", (D, L))
    qa_d = scratch("qa_d", (D, L))
    x1_d = scratch("x1_d", (L, D))
    x2_d = scratch("x2_d", (L, D))
    ptok_d = scratch("ptok_d", (L, C_TOK))
    pch_d = scratch("pch_d", (1536, L))
    ka_d = scratch("ka_d", (D, MEM))
    va_d = scratch("va_d", (MEM, D))

    ctx = ExitStack()
    ctx.enter_context(nc.allow_non_contiguous_dma(reason="small parameters, once"))
    where = {}
    top = [16640]

    def region(name, size):
        where[name] = top[0]
        top[0] += size

    for name, size in (("const", 7168), ("small", 3072), ("x", 33024), ("ophi", 32768), ("oplo", 32768),
                       ("whi", 32768), ("wlo", 32768), ("raw", 16384), ("stage", 20480)):
        region(name, size)
    assert top[0] <= 229344, top[0]
    used = {}

    def at(name, reg, off, shape, dt=F32):
        size = int(np.prod(shape[1:])) * 4
        limit = {"const": 7168, "small": 3072, "x": 33024, "ophi": 32768, "oplo": 32768, "whi": 32768,
                 "wlo": 32768, "raw": 16384, "stage": 20480}[reg]
        assert off + size <= limit, (name, off, size, limit)
        return nc.alloc_sbuf_tensor_at(name, list(shape), dt, offset=where[reg] + off)

    class Signal:
        def __init__(self, hw, base):
            self.hw, self.base, self.count = hw, base, 0

        def __call__(self, value):
            return self.hw, self.base + value

        def by(self, n):
            self.count += n
            return self.hw, n

    sems = {}

    def sem(name):
        if name not in sems:
            if name in SHARED:
                before, total = SHARED[name]
                earlier = sem(before)
                sems[name] = Signal(earlier.hw, earlier.base + total)
            else:
                sems[name] = Signal(ctx.enter_context(nc.semaphore(name)), 0)
        return sems[name]

    PS = ctx.enter_context(nc.psum_tensor("PS", [P, 8, HALF], F32))
    _, names, _, _ = shape_constants()
    CONST = at("CONST", "const", 0, [P, len(names) * P])
    K = {n: CONST[:, j * P:(j + 1) * P] for j, n in enumerate(names)}
    ident = K["ident"]
    X = at("X", "x", 0, [P, TT, D])
    OP_HI = at("OP_HI", "ophi", 0, [P, KT, L], F32R)
    OP_LO = at("OP_LO", "oplo", 0, [P, KT, L], F32R)
    W_HI = at("W_HI", "whi", 0, [P, 2, KT, HALF], F32R)
    W_LO = at("W_LO", "wlo", 0, [P, 2, KT, HALF], F32R)
    RAW = at("RAW", "raw", 0, [P, 2, 4, HALF])
    OST = at("OST", "stage", 0, [P, 4, HALF])
    XN = at("XN", "stage", 8192, [P, 2, D])
    GROW = at("GROW", "stage", 16384, [P, D])
    st = at("st", "small", 0, [P, 64])
    bcol = at("bcol", "small", 256, [P, 16])
    halfpi = at("halfpi", "small", 512, [P, 1])

    def together(*stages):
        nexts = [[next(s), n, s] for n, s in enumerate(stages)]
        while nexts:
            first = min(nexts, key=lambda x: (x[0], x[1]))
            first[0] = next(first[2], None)
            if first[0] is None:
                nexts.remove(first)

    def alone(stage):
        for _ in stage:
            pass

    class Chain:
        def __init__(self, eng, s):
            self.eng, self.s, self.n = eng, s, 0

        def __call__(self, ins):
            ins.then_inc(*self.s.by(1))
            self.n += 1
            self.eng.wait_ge(*self.s(self.n))
    class Gemm:
        pass

    gemms, blocks, halves = {}, [], []
    raw_total = [0, 0]
    count = [0]

    def add_gemm(name, weight, col_blocks, major, tiles, row0=0, engine="act"):
        g = Gemm()
        g.name, g.major, g.tiles, g.engine = name, major, tiles, engine
        g.first_block, g.first = len(blocks), count[0]
        g.units = []
        g.cols = col_blocks
        for segs in col_blocks:
            b = len(blocks)
            width = sum(n for _, n in segs)
            if major == "tok":
                units = [(b, t, 0, width) for t in range(tiles)]
            else:
                step = min(HALF, tiles)
                units = [(b, c, h, step) for c in range(width // P) for h in range(tiles // step)]
            g.units += units
            count[0] += len(units)
            blocks.append((width, count[0]))
            for half in range(2):
                r = len(halves)
                raw_total[r % 2] += 16 * len(segs)
                halves.append((weight, row0 + half * HALF, segs, b, half, raw_total[r % 2], width))
        g.end = count[0]
        gemms[name] = g

    def cols(a, b):
        return [[(c, min(HALF, b - c))] for c in range(a, b, HALF)]

    w_in, w_out = I["w_in"][0], I["w_out"][0]
    add_gemm("xk", I["xa_wk"][0], cols(0, D), "ch", MEM)
    add_gemm("xv", I["xa_wv"][0], cols(0, D), "tok", MEM // P)
    add_gemm("u", w_in, cols(3072, 4096), "tok", TT)
    add_gemm("qk", w_in, cols(0, 1024), "tok", TT)
    add_gemm("v", w_in, cols(1024, 2048), "tok", TT)
    add_gemm("gret", w_in, cols(2048, 3072), "ch", L)
    add_gemm("gs5", w_in, cols(4096, 5120), "ch", L)
    add_gemm("glu", I["s5_glu_w"][0], cols(0, D), "ch", L)
    add_gemm("out_ret", w_out, cols(0, D), "tok", TT, row0=0, engine="dve")
    add_gemm("out_s5", w_out, cols(0, D), "tok", TT, row0=D, engine="dve")
    add_gemm("xq", I["xa_wq"][0], cols(0, D), "ch", L)
    add_gemm("xo", I["xa_wo"][0], cols(0, D), "tok", TT, engine="dve")
    w_in2 = I["w_in_2"][0]
    add_gemm("ptok", w_in2, [[(0, 512)], [(2048, 264), (3080, 16)], [(2312, 512)], [(2824, 256), (3096, 256)]],
             "tok", TT)
    add_gemm("pch", w_in2, cols(512, 2048), "ch", L)
    add_gemm("out2", I["w_out_2"][0], cols(0, D), "tok", TT, engine="dve")

    raw_in = [sem("raw_in0"), sem("raw_in1")]
    w_split = sem("w_split")
    w_hi = sem("w_hi")
    mm_done = sem("mm_done")
    bank_act = sem("bank_act")
    bank_dve = sem("bank_dve")
    ost_out = [sem(f"ost_out{i}") for i in range(4)]

    act_total, dve_total = [0], [0]
    for g in gemms.values():
        g.free0_act, g.free0_dve = act_total[0], dve_total[0]
        (act_total if g.engine == "act" else dve_total)[0] += len(g.units)
        g.free1_act, g.free1_dve = act_total[0], dve_total[0]

    issued = [0]

    def sp_weights(sp, upto):
        alone(sp_weights_steps(sp, upto, 0))

    def sp_weights_steps(sp, upto, block0):
        while issued[0] < min(upto, len(halves)):
            r = issued[0]
            yield 8 * (halves[r][3] - block0 - 2) + 0.05
            weight, row, segs, _, _, _, _ = halves[r]
            if r >= 2:
                sp.wait_ge(*w_split(r - 1))
            c = 0
            for c0, n in segs:
                sp.dma_start(RAW[:, r % 2, :, c:c + n],
                             weight[row:row + HALF, c0:c0 + n].rearrange("(k p) n -> p k n", p=P))\
                  .then_inc(*raw_in[r % 2].by(16))
                c += n
            issued[0] += 1

    def weights_before(name):
        return 2 * gemms[name].first_block + 6

    def pool_split_all(pool):
        for r, (_, _, _, b, half, arrived, width) in enumerate(halves):
            pool.wait_ge(*raw_in[r % 2](arrived))
            if b >= 2 and half == 0:
                pool.wait_ge(*mm_done(blocks[b - 2][1]))
            if b == gemms["out2"].first_block + 1 and half == 0:
                pool.wait_ge(*fin_g.lo(TT))
            raw = RAW[:, r % 2, :, 0:width]
            hi = W_HI[:, b % 2, 4 * half:4 * half + 4, 0:width]
            nc.gpsimd.tensor_scalar(hi, raw, 1.0, 1.0, ALU.mult, ALU.mult).then_inc(*w_hi.by(1))
            pool.wait_ge(*w_hi(r + 1))
            nc.gpsimd.tensor_tensor(W_LO[:, b % 2, 4 * half:4 * half + 4, 0:width], raw, hi.bitcast(F32),
                                    ALU.subtract).then_inc(*w_split.by(1))

    def pe_gemm(pe, name, ready=()):
        alone(pe_gemm_steps(pe, name, ready))

    def pe_gemm_steps(pe, name, ready=()):
        g = gemms[name]
        for s, v in ready:
            pe.wait_ge(*s(v))
        if g.engine == "act" and g.free0_dve:
            pe.wait_ge(*bank_dve(g.free0_dve))
        if g.engine == "dve" and g.free0_act:
            pe.wait_ge(*bank_act(g.free0_act))
        mine, base = (bank_act, g.free0_act) if g.engine == "act" else (bank_dve, g.free0_dve)
        last = -1
        for n, (b, a, h, width) in enumerate(g.units):
            yield n
            if b != last:
                pe.wait_ge(*w_split(2 * b + 2))
                last = b
            if base + n - 3 > 0:
                pe.wait_ge(*mine(base + n - 3))
            bank = (g.first + n) % 4
            slot = b % 2
            for i, (act_part, w_part) in enumerate(((OP_HI, W_HI), (OP_HI, W_LO), (OP_LO, W_HI))):
                for k in range(KT):
                    start, stop = i == 0 and k == 0, i == 2 and k == KT - 1
                    if g.major == "tok":
                        ins = nc.tensor.matmul(PS[:, bank, 0:width], act_part[:, k, a * P:(a + 1) * P],
                                               w_part[:, slot, k, 0:width], start=start, stop=stop)
                    else:
                        ins = nc.tensor.matmul(PS[:, bank, 0:width], w_part[:, slot, k, a * P:(a + 1) * P],
                                               act_part[:, k, h * HALF:h * HALF + width], start=start, stop=stop)
            ins.then_inc(*mm_done.by(1))

    stores = [0]

    def act_gemm_store(act, name, dst, func=ACT.Copy):
        alone(act_gemm_store_steps(act, name, dst, func))

    def act_gemm_store_steps(act, name, dst, func=ACT.Copy):
        g = gemms[name]
        for n, (b, a, h, width) in enumerate(g.units):
            yield n + 0.9
            s = stores[0]
            act.wait_ge(*mm_done(g.first + n + 1))
            if s >= 4:
                act.wait_ge(*ost_out[s % 4](16 * (s // 4)))
            act.activation(OST[:, s % 4, 0:width], PS[:, (g.first + n) % 4, 0:width], func)\
               .then_inc(*bank_act.by(1))
            act.wait_ge(*bank_act(g.free0_act + n + 1))
            places = dst(b - g.first_block, a, h, width)
            act.dma_start(places, OST[:, s % 4, 0:width]).then_inc(*ost_out[s % 4].by(16))
            stores[0] += 1

    store_ends, total = {}, 0
    for name in ("xk", "xv", "u", "qk", "v", "gret", "gs5", "xq", "ptok", "pch"):
        total += len(gemms[name].units)
        store_ends[name] = total

    def wait_stores(eng, name):
        n = store_ends[name]
        for i in range(4):
            if (n - i + 3) // 4 > 0:
                eng.wait_ge(*ost_out[i](16 * ((n - i + 3) // 4)))

    def dve_gemm_add(dve, name):
        g = gemms[name]
        for n, (b, a, h, width) in enumerate(g.units):
            c = (b - g.first_block) * HALF
            dve.wait_ge(*mm_done(g.first + n + 1))
            nc.vector.tensor_tensor(X[:, a, c:c + width], X[:, a, c:c + width],
                                    PS[:, (g.first + n) % 4, 0:width], ALU.add).then_inc(*bank_dve.by(1))

    sq_done, st_a, st_b = sem("sq_done"), sem("st_a"), sem("st_b")
    xn_full, xn_turned = sem("xn_full"), sem("xn_turned")
    op_hi_done, op_lo_done = sem("op_hi_done"), sem("op_lo_done")
    x_in, grow_in = sem("x_in"), sem("grow_in")
    norms = []
    JUNK = XN[:, :, :]

    def norm_base(q):
        return sum(norms[:q])

    def act_norm_stats(act, q, ready=(), tiles=TT):
        for s, v in ready:
            act.wait_ge(*s(v))
        base = norm_base(q)
        if base:
            act.wait_ge(*xn_turned(turned_base(q)))
        for t in range(tiles):
            ins = act.activation(XN[:, t % 2, :], X[:, t, :], ACT.Square, accum_out=st[:, t:t + 1])
            ins.then_inc(*sq_done.by(1))
            act.wait_ge(*sq_done(base + t + 1))
        act.wait_ge(*st_a(q + 1))
        act.activation(st[:, 16:16 + tiles], st[:, 8:8 + tiles], ACT.Sqrt).then_inc(*st_b.by(1))

    def dve_norm_rstd(dve, q, tiles=TT):
        dve.wait_ge(*sq_done(norm_base(q) + tiles))
        nc.vector.tensor_scalar(st[:, 8:8 + tiles], st[:, 0:tiles], 1.0 / D, EPS, ALU.mult, ALU.add)\
            .then_inc(*st_a.by(1))
        dve.wait_ge(*st_b(q + 1))
        return nc.vector.reciprocal(st[:, 24:24 + tiles], st[:, 16:16 + tiles])

    def dve_norm_split(dve, q, chain, tiles=TT):
        base = turned_base(q)
        chain(dve_norm_rstd(dve, q, tiles))
        dve.wait_ge(*grow_in(16 * (q + 1)))

        def lo(t):
            dve.wait_ge(*op_hi_done(base + t + 1))
            p = turn_bank(base + t)
            nc.vector.tensor_tensor(OP_LO[:, :, t * P:(t + 1) * P], PS_T(p),
                                    OP_HI[:, :, t * P:(t + 1) * P].bitcast(F32), ALU.subtract)\
                .then_inc(*op_lo_done.by(1))

        for t in range(tiles):
            if t >= 2:
                dve.wait_ge(*xn_turned(base + t - 1))
            nc.vector.scalar_tensor_tensor(XN[:, t % 2, :], X[:, t, :], st[:, 24 + t:25 + t], GROW[:, :],
                                           ALU.mult, ALU.mult).then_inc(*xn_full.by(1))
            if t:
                lo(t - 1)
        lo(tiles - 1)

    def turn_bank(n):
        return 4 + 2 * (n % 2)

    def PS_T(p):
        return PS[:, p:p + 2, :].rearrange("p b (c t) -> p (b c) t", t=P)

    def pe_norm(pe, q, tiles=TT):
        base = turned_base(q)
        if q == 0:
            pe.wait_ge(*consts_in(16))
        for t in range(tiles):
            pe.wait_ge(*xn_full(base + t + 1))
            if base + t >= 2:
                pe.wait_ge(*op_lo_done(base + t - 1))
            for c in range(KT):
                ins = nc.tensor.transpose(PS_T(turn_bank(base + t))[:, c, :], XN[:, t % 2, c * P:(c + 1) * P],
                                          ident)
            ins.then_inc(*xn_turned.by(1))

    def act_norm_hi(act, q, free=(), tiles=TT):
        base = turned_base(q)
        for s, v in free:
            act.wait_ge(*s(v))
        for t in range(tiles):
            act.wait_ge(*xn_turned(base + t + 1))
            act.activation(OP_HI[:, :, t * P:(t + 1) * P], PS_T(turn_bank(base + t)), ACT.Copy)\
               .then_inc(*op_hi_done.by(1))

    norms += [MEM // P, TT, TT, TT, TT, TT, TT]
    turned = [0, 1, 2, 4, 5]
    turned_by = {}

    def turned_base(q):
        return sum(norms[j] for j in turned if j < q)

    for q_ in range(7):
        turned_by[q_] = turned_base(q_)
    gains = ["norm_mem_g", "norm1_g", "norm2_g", "norm_f_g", "norm1_w_2", "norm2_w_2", "final_norm_w_2"]
    consts_in = sem("consts_in")

    def sp_gain(sp, q, ready=()):
        for s, v in ready:
            sp.wait_ge(*s(v))
        row = I[gains[q]]
        row = row[0:1, :] if len(row.shape) == 2 else row.rearrange("(a n) -> a n", a=1)
        sp.dma_start(GROW[:, :], row.to_broadcast([P, D])).then_inc(*grow_in.by(16))

    PW = at("PW", "stage", 0, [32, 24, P])
    PRM = at("PRM", "stage", 12288, [P, 8, PAIRS])
    DD = at("DD", "stage", 13312, [SP_, SG, SP_])
    PLACE = at("PLACE", "stage", 17408, [SP_, P + SP_])
    DCOL = at("DCOL", "stage", 18432, [SP_, SG])
    A8T = at("A8T", "small", 1024, [P, 2, 2, PAIRS])
    BNAT = at("BNAT", "x", 0, [P, 2, PAIRS, SP_])
    T12 = at("T12", "x", 4096, [P, 2, 2, PAIRS, SP_])
    T34 = at("T34", "x", 12288, [P, 2, 2, PAIRS, SP_])
    CNAT = at("CNAT", "x", 20480, [P, 8, 2, SN])
    CP = at("CP", "x", 24576, [P, 2, PAIRS, SP_])
    RSB = at("RSB", "x", 28672, [P, SG * SP_])
    XPW = at("XPW", "ophi", 0, [P, 2, PAIRS, SC, SP_])
    CPW = at("CPW", "oplo", 0, [P, 2, PAIRS, SC, SP_])
    BT = at("BT", "whi", 0, [P, PAIRS, 2, P])
    ZER = at("ZER", "wlo", 0, [P, SG * SP_])

    s5_in = sem("s5_in")
    s5_small = sem("s5_small")
    s5_act = sem("s5_act")
    s5_prm_t = sem("s5_prm_t")
    s5_prm = sem("s5_prm")
    s5_cp_t = sem("s5_cp_t")
    s5_cp = sem("s5_cp")
    s5_xpw = sem("s5_xpw")
    s5_cpw = sem("s5_cpw")
    s5_dd = sem("s5_dd")
    s5_r = sem("s5_r")
    s5_rsb = sem("s5_rsb")
    s5_bt_t = sem("s5_bt_t")
    s5_bt = sem("s5_bt")
    s5_out = sem("s5_out")
    PRE_LOADS = 12

    def sp_s5_tables(sp):
        sp.dma_start(CONST[:, :], I["c_base"]).then_inc(*consts_in.by(16))
        loads = [
            (PW[:, 0, :], I["s5_a_re"][0].rearrange("(q b) s -> q (b s)", b=2)),
            (PW[:, 1, :], I["s5_a_im"][0].rearrange("(q b) s -> q (b s)", b=2)),
            (PW[:, 2, 0:2], I["s5_log_dt"].rearrange("a (q b) -> (a q) b", b=2)),
            (BNAT[0:P, 0, :, :], I["s5_b_re"][0].rearrange("(q b) s c -> (b s) q c", b=2)),
            (BNAT[0:P, 1, :, :], I["s5_b_im"][0].rearrange("(q b) s c -> (b s) q c", b=2)),
            (CNAT[:, :, 0, :], I["s5_c_re"][0].rearrange("(t g) c s -> (g c) t s", g=8)),
            (CNAT[:, :, 1, :], I["s5_c_im"][0].rearrange("(t g) c s -> (g c) t s", g=8)),
            (DCOL[:, :], I["s5_d"].rearrange("a (g c) -> (a c) g", c=SP_)),
            (PLACE[:, :], I["c_place"]),
        ]
        for dst, src in loads:
            sp.dma_start(dst, src).then_inc(*s5_in.by(16))
        sp.wait_ge(*s5_rsb(3))
        for i in range(SC):
            rows = SP_ * (i + 1)
            sp.dma_start(toep_d[0:rows, i, :], RSB[P - rows:P, :]).then_inc(*s5_out.by(16))
            if i < SC - 1:
                sp.dma_start(toep_d[rows:P, i, :], ZER[rows:P, :]).then_inc(*s5_out.by(16))
        sp.wait_ge(*s5_bt(16))
        sp.dma_start(bct_d, BT[:, :, :, :]).then_inc(*s5_out.by(16))
        sp.wait_ge(*s5_cpw(4 * SC))
        for c in range(2):
            sp.dma_start(cc_d[:, :, c, :], CPW[:, c, :, :, :].rearrange("p q i c -> p q (i c)"))\
              .then_inc(*s5_out.by(16))
    S5_STORES = 16 * (2 * SC - 1 + 1 + 2)
    S5_LOADED = 16 * 9

    def reduce_angle(chain, angle, r, n):
        V = nc.vector
        chain(V.tensor_scalar(n, angle, 1.0 / TWO_PI, ROUND, ALU.mult, ALU.add))
        chain(V.tensor_scalar(n, n, ROUND, None, ALU.subtract))
        chain(V.scalar_tensor_tensor(r, n, -PI_A, angle, ALU.mult, ALU.add))
        chain(V.scalar_tensor_tensor(r, n, -PI_B, r, ALU.mult, ALU.add))
        chain(V.scalar_tensor_tensor(r, n, -PI_C, r, ALU.mult, ALU.add))
        chain(V.tensor_scalar(r, r, PI_SAFE, -PI_SAFE, ALU.min, ALU.max))

    def dve_s5_tables(dve, chain):
        V = nc.vector
        w = lambda k: PW[:, k, :]
        MUL, ADD, SUB = ALU.mult, ALU.add, ALU.subtract

        def tt(o, a, b, op):
            chain(V.tensor_tensor(o, a, b, op))

        V.memset(halfpi[:, :], math.pi / 2).then_inc(*s5_small.by(1))
        V.memset(ZER[:, :], 0.0).then_inc(*s5_rsb.by(1))
        dve.wait_ge(*s5_in(S5_LOADED))
        dve.wait_ge(*s5_act(1))
        chain(V.tensor_copy(w(4).rearrange("q (b s) -> q b s", b=2), PW[:, 3, 0:2].unsqueeze(2).to_broadcast([32, 2, SN])))
        tt(w(5), w(0), w(4), MUL)
        tt(w(6), w(1), w(4), MUL)
        reduce_angle(chain, w(6), w(7), w(8))
        chain(V.scalar_tensor_tensor(w(9), w(7), -1.0, w(7), MUL, ALU.max))
        V.tensor_copy(w(10), w(9)).then_inc(*s5_small.by(1))
        dve.wait_ge(*s5_act(4))
        tt(w(14), w(11), w(13), MUL)
        tt(w(15), w(11), w(12), MUL)
        tt(w(3), w(0), w(0), MUL)
        tt(w(4), w(1), w(1), MUL)
        tt(w(3), w(3), w(4), ADD)
        chain(V.reciprocal(w(5), w(3)))
        chain(V.tensor_scalar(w(6), w(14), -1.0, None, ADD))
        tt(w(7), w(6), w(0), MUL)
        tt(w(8), w(15), w(1), MUL)
        tt(w(7), w(7), w(8), ADD)
        tt(w(16), w(7), w(5), MUL)
        tt(w(7), w(15), w(0), MUL)
        tt(w(8), w(6), w(1), MUL)
        tt(w(7), w(7), w(8), SUB)
        tt(w(17), w(7), w(5), MUL)
        re, im = 14, 15
        for k in range(3):
            tt(w(7), w(re), w(re), MUL)
            tt(w(8), w(im), w(im), MUL)
            tt(w(9), w(re), w(im), MUL)
            re, im = (18, 19) if k % 2 == 0 else (20, 21)
            tt(w(re), w(7), w(8), SUB)
            chain(V.tensor_scalar(w(im), w(9), 2.0, None, MUL))
        V.tensor_copy(w(22), w(re)).then_inc(*s5_small.by(1))
        V.tensor_copy(w(23), w(im)).then_inc(*s5_small.by(1))
        dve.wait_ge(*s5_prm_t(1))
        chain(V.tensor_copy(PRM[:, 0:6, :], PS[:, 4, 0:192].rearrange("p (k q) -> p k q", k=6)))
        chain(V.tensor_scalar(PRM[:, 6, :], PRM[:, 1, :], -1.0, None, MUL))
        for o, t, k in ((0, 0, 4), (1, 1, 4), (1, 0, 5)):
            chain(V.tensor_copy(A8T[:, o, t, :], PRM[:, k, :]))
        V.tensor_scalar(A8T[:, 0, 1, :], PRM[:, 5, :], -1.0, None, MUL).then_inc(*s5_prm.by(1))
        chain(V.tensor_copy(DD[:, :, :], PLACE[:, P:P + SP_].unsqueeze(1).to_broadcast([SP_, SG, SP_])))
        V.tensor_tensor(DD[:, :, :], DD[:, :, :], DCOL[:, :].unsqueeze(2).to_broadcast([SP_, SG, SP_]), MUL)\
            .then_inc(*s5_dd.by(1))
        dve.wait_ge(*s5_dd(1))
        shape = [P, 2, PAIRS, SP_]

        def spread(k):
            return PRM[:, k, :].unsqueeze(1).unsqueeze(3).to_broadcast(shape)

        src = BNAT[:, :, :, :]
        fac = (2, 3)
        for e in range(SC):
            j = SC - 1 - e
            chain(V.tensor_tensor(T12[:, 0], src, spread(fac[0]), MUL))
            chain(V.tensor_tensor(T12[:, 1], src, spread(fac[1]), MUL))
            V.tensor_tensor(XPW[:, 0, :, j, :], T12[:, 0, 0], T12[:, 1, 1], SUB).then_inc(*s5_xpw.by(1))
            V.tensor_tensor(XPW[:, 1, :, j, :], T12[:, 0, 1], T12[:, 1, 0], ADD).then_inc(*s5_xpw.by(1))
            dve.wait_ge(*s5_xpw(2 * e + 2))
            src, fac = XPW[:, :, :, j, :], (0, 1)
        dve.wait_ge(*s5_r(1))
        for par in range(2):
            V.tensor_copy(RSB[:, :].rearrange("p (q b c) -> p q b c", b=2, c=SP_)[:, :, par, :],
                          PS[:, 4 + par, :].rearrange("p (q c) -> p q c", c=SP_)).then_inc(*s5_rsb.by(1))

    def pool_s5_tables(pool, chain):
        G = nc.gpsimd
        pool.wait_ge(*s5_prm(1))
        pool.wait_ge(*s5_cp(4))
        shape = [P, 2, PAIRS, SP_]

        def spread(k):
            return PRM[:, k, :].unsqueeze(1).unsqueeze(3).to_broadcast(shape)

        src = CP[:, :, :, :]
        for i in range(SC):
            G.tensor_tensor(T34[:, 0], src, spread(0), ALU.mult).then_inc(*s5_cpw.by(1))
            G.tensor_tensor(T34[:, 1], src, spread(6), ALU.mult).then_inc(*s5_cpw.by(1))
            pool.wait_ge(*s5_cpw(4 * i + 2))
            G.tensor_tensor(CPW[:, 0, :, i, :], T34[:, 0, 0], T34[:, 1, 1], ALU.subtract).then_inc(*s5_cpw.by(1))
            G.tensor_tensor(CPW[:, 1, :, i, :], T34[:, 0, 1], T34[:, 1, 0], ALU.add).then_inc(*s5_cpw.by(1))
            pool.wait_ge(*s5_cpw(4 * i + 4))
            src = CPW[:, :, :, i, :]

    def act_s5_tables(act):
        act.wait_ge(*s5_in(S5_LOADED))
        act.activation(PW[:, 3, 0:2], PW[:, 2, 0:2], ACT.Exp).then_inc(*s5_act.by(1))
        act.wait_ge(*s5_small(2))
        act.activation(PW[:, 11, :], PW[:, 5, :], ACT.Exp).then_inc(*s5_act.by(1))
        act.activation(PW[:, 12, :], PW[:, 7, :], ACT.Sin).then_inc(*s5_act.by(1))
        act.activation(PW[:, 13, :], PW[:, 10, :], ACT.Sin, scale=-1.0, bias=halfpi[0:32, :]).then_inc(*s5_act.by(1))
        act.wait_ge(*s5_cp_t(1))
        for c in range(2):
            for par in range(2):
                src = PS[64 * c:64 * c + 64, 6:8, :].rearrange("p b (t g e q) -> p (b t) g e q", t=4, g=4, e=2)
                act.activation(CP[64 * par:64 * par + 64, c, :, :].rearrange("p (t g) q -> p t g q", g=4),
                               src[:, :, :, par, :], ACT.Copy, scale=1.0 if c == 0 else -1.0).then_inc(*s5_cp.by(1))
        for n in range(16):
            act.wait_ge(*s5_bt_t(n + 1))
            act.activation(BT[:, 2 * n:2 * n + 2, :, :].rearrange("p q c s -> p (q c s)"), PS[:, 6 + n % 2, :],
                           ACT.Copy).then_inc(*s5_bt.by(1))

    def pe_s5_tables(pe):
        T = nc.tensor
        pe.wait_ge(*consts_in(16))
        pe.wait_ge(*s5_in(S5_LOADED))
        for t in range(8):
            ins = T.transpose(PS[:, 6 + t // 4, (t % 4) * P:(t % 4 + 1) * P],
                              CNAT[:, t, :, :].rearrange("p c s -> p (c s)"), ident)
        ins.then_inc(*s5_cp_t.by(1))
        pe.wait_ge(*s5_small(4))
        for n, k in enumerate((14, 15, 16, 17, 22, 23)):
            ins = T.transpose(PS[:, 4, 32 * n:32 * n + 32], PW[:, k, :], ident[0:32, 0:32])
        ins.then_inc(*s5_prm_t.by(1))
        pe.wait_ge(*s5_prm(1))
        pe.wait_ge(*s5_xpw(2 * SC))
        pe.wait_ge(*s5_cp(4))
        pe.wait_ge(*s5_dd(1))
        for g in range(SG):
            q, lo = g // 2, 64 * (g % 2)
            o = PS[:, 4 + g % 2, 16 * q:16 * q + 16]
            for c in range(2):
                T.matmul(o, XPW[lo:lo + 64, c, q, :, :].rearrange("p j c -> p (j c)"), CP[lo:lo + 64, c, q, :],
                         start=c == 0, stop=False)
            ins = T.matmul(o, PLACE[:, 0:P], DD[:, g, :], start=False, stop=True)
        ins.then_inc(*s5_r.by(1))
        for n in range(16):
            if n >= 2:
                pe.wait_ge(*s5_bt(n - 1))
            for m in range(4):
                q, c = 2 * n + m // 2, m % 2
                ins = T.transpose(PS[:, 6 + n % 2, m * P:(m + 1) * P],
                                  XPW[:, c, q, :, :].rearrange("p j c -> p (j c)"), ident)
            ins.then_inc(*s5_bt_t.by(1))

    SCAN = at("SCAN", "x", 0, [P, 2, PAIRS, NCH + 1])
    U8 = at("U8", "stage", 0, [P, SC, P])
    BCTq = at("BCTq", "stage", 4096, [P, 4, 2, P])
    UTq = at("UTq", "stage", 8192, [P, 8, P])
    URq = at("URq", "stage", 12288, [P, 8, P])
    SM = at("SM", "small", 1536, [P, 2, 2, PAIRS])
    SS = at("SS", "small", 2048, [P, 2, PAIRS])

    s5b_in, s5b_t, s5b_ut, s5b_mm, s5b_s = (sem(n) for n in ("s5b_in", "s5b_t", "s5b_ut", "s5b_mm", "s5b_s"))
    s5b_ur = sem("s5b_ur")
    scan_step = sem("scan_step")

    def sp_s5_in(sp):
        wait_stores(sp, "u")
        sp.wait_ge(*s5_out(S5_STORES))
        for q in range(8):
            if q:
                sp.wait_ge(*s5b_mm(q))
                sp.wait_ge(*s5b_ur(q))
            sp.dma_start(U8[:, :, :], u_d.rearrange("(n j) c -> n j c", j=SC)[:, :, q * P:(q + 1) * P])\
              .then_inc(*s5b_in.by(16))
            sp.dma_start(BCTq[:, :, :, :], bct_d[:, 4 * q:4 * q + 4, :, :]).then_inc(*s5b_in.by(16))

    def pe_s5_in(pe):
        T = nc.tensor
        for q in range(8):
            pe.wait_ge(*s5b_in(32 * (q + 1)))
            pe.wait_ge(*s5b_ur(q + 1))
            if q:
                pe.wait_ge(*s5b_ut(q))
            for g in range(8):
                ins = T.transpose(PS_T(4)[:, g, :], URq[:, g, :], ident)
            ins.then_inc(*s5b_t.by(1))
            pe.wait_ge(*s5b_ut(q + 1))
            if q:
                pe.wait_ge(*s5b_s(q))
            for c in range(2):
                for g in range(8):
                    lo = 64 * (g % 2)
                    ins = T.matmul(PS[lo:lo + 64, 6 + c, (g // 2) * P:(g // 2 + 1) * P],
                                   BCTq[:, g // 2, c, lo:lo + 64], UTq[:, g, :], start=True, stop=True)
            ins.then_inc(*s5b_mm.by(1))

    def act_s5_in(act):
        for q in range(8):
            act.wait_ge(*s5b_t(q + 1))
            if q:
                act.wait_ge(*s5b_mm(q))
            act.activation(UTq[:, :, :], PS_T(4), ACT.Copy).then_inc(*s5b_ut.by(1))

    def dve_s5_in(dve):
        nc.vector.memset(SCAN[:, :, :, 0:1], 0.0).then_inc(*scan_step.by(1))

        def regroup(q):
            dve.wait_ge(*s5b_in(32 * (q + 1)))
            if q:
                dve.wait_ge(*s5b_t(q))
            nc.vector.tensor_copy(URq[:, :, :].rearrange("n g (j c) -> n g j c", j=SC),
                                  U8[:, :, :].rearrange("n j (g c) -> n g j c", g=8)).then_inc(*s5b_ur.by(1))

        regroup(0)
        for q in range(8):
            if q + 1 < 8:
                regroup(q + 1)
            dve.wait_ge(*s5b_mm(q + 1))
            nc.vector.tensor_copy(SCAN[:, :, 4 * q:4 * q + 4, 1:NCH + 1],
                                  PS[:, 6:8, :].rearrange("p c (q n) -> p c q n", q=4)).then_inc(*s5b_s.by(1))

    def dve_s5_scan(dve):
        V = nc.vector
        dve.wait_ge(*s5b_s(8))
        UN = 4
        with dve.Fori(0, NCH // UN) as m:
            for k in range(UN):
                col = m * UN + k
                base = m * (3 * UN) + 3 * k + 1
                dve.wait_ge(*scan_step(base))
                cur = SCAN[:, :, :, bass.ds(col, 1)].rearrange("p c q o -> p (c o) q")
                V.tensor_tensor(SM[:, :, :, :], A8T[:, :, :, :],
                                cur.unsqueeze(1).to_broadcast([P, 2, 2, PAIRS]), ALU.mult).then_inc(*scan_step.by(1))
                dve.wait_ge(*scan_step(base + 1))
                V.tensor_tensor(SS[:, :, :], SM[:, :, 0, :], SM[:, :, 1, :], ALU.add).then_inc(*scan_step.by(1))
                dve.wait_ge(*scan_step(base + 2))
                nxt = SCAN[:, :, :, bass.ds(col + 1, 1)].rearrange("p c q o -> p (c o) q")
                V.tensor_tensor(nxt, nxt, SS[:, :, :], ALU.add).then_inc(*scan_step.by(1))
    SCAN_END = 3 * NCH + 1

    UY = at("UY", "ophi", 0, [P, 2, SC, P])
    TY = at("TY", "ophi", 8192, [P, 2, SC, P])
    CY = at("CY", "ophi", 16384, [P, 2, 4, 2, P])
    UTy = at("UTy", "ophi", 24576, [P, 8, P])
    YS = at("YS", "ophi", 28672, [P, SC, 8, SP_])
    YO = at("YO", "oplo", 0, [P, 2, NCH, SC])

    URy = at("URy", "oplo", 8192, [P, 8, P])
    s5y_ur = sem("s5y_ur")
    s5y_in0, s5y_in1 = sem("s5y_in0"), sem("s5y_in1")
    s5y_t, s5y_ut, s5y_mm, s5y_ys, s5y_tt, s5y_yo, s5y_out = (
        sem(n) for n in ("s5y_t", "s5y_ut", "s5y_mm", "s5y_ys", "s5y_tt", "s5y_yo", "s5y_out0"))
    s5y_outs = (s5y_out, sem("s5y_out1"))

    def sp_s5_y(sp):
        sp.wait_ge(*mm_done(gemms["gs5"].end))
        for q in range(8):
            b = q % 2
            if q >= 2:
                sp.wait_ge(*s5y_mm(q - 1))
            s = s5y_in1 if b else s5y_in0
            sp.dma_start(UY[:, b], u_d.rearrange("(n j) c -> n j c", j=SC)[:, :, q * P:(q + 1) * P]).then_inc(*s.by(16))
            sp.dma_start(TY[:, b], toep_d[:, :, q * P:(q + 1) * P]).then_inc(*s.by(16))
            sp.dma_start(CY[:, b], cc_d[:, 4 * q:4 * q + 4, :, :]).then_inc(*s.by(16))

    def pe_s5_y(pe):
        T = nc.tensor
        pe.wait_ge(*scan_step(SCAN_END))
        pe.wait_ge(*bank_act(gemms["gs5"].free1_act))

        def turn_back(q):
            pe.wait_ge(*s5y_ys(2 * q + 2))
            if q:
                pe.wait_ge(*s5y_yo(q))
            for i in range(SC):
                ins = T.transpose(PS_T(6)[:, i, :], YS[:, i, :, :].rearrange("n g c -> n (g c)"), ident)
            ins.then_inc(*s5y_tt.by(1))

        for q in range(8):
            b = q % 2
            pe.wait_ge(*(s5y_in1 if b else s5y_in0)(48 * (q // 2 + 1)))
            pe.wait_ge(*s5y_ur(q + 1))
            if q:
                pe.wait_ge(*s5y_ut(q))
            for g in range(8):
                ins = T.transpose(PS_T(2)[:, g, :], URy[:, g, :], ident)
            ins.then_inc(*s5y_t.by(1))
            if q:
                turn_back(q - 1)
            pe.wait_ge(*s5y_ut(q + 1))
            if q:
                pe.wait_ge(*s5y_ys(2 * q))
            for g in range(8):
                lo = 64 * (g % 2)
                o = PS[:, 4 + g % 2, (g // 2) * P:(g // 2 + 1) * P]
                T.matmul(o, UTy[:, g, :], TY[:, b, :, 16 * g:16 * g + 16], start=True, stop=False)
                for c in range(2):
                    ins = T.matmul(o, SCAN[lo:lo + 64, c, 4 * q + g // 2, 0:NCH], CY[lo:lo + 64, b, g // 2, c, :],
                                   start=False, stop=c == 1)
            ins.then_inc(*s5y_mm.by(1))
        turn_back(7)

    def act_s5_y(act):
        for q in range(8):
            act.wait_ge(*s5y_t(q + 1))
            if q:
                act.wait_ge(*s5y_mm(q))
            act.activation(UTy[:, :, :], PS_T(2), ACT.Copy).then_inc(*s5y_ut.by(1))
            if q:
                y_gelu(act, q - 1)
        y_gelu(act, 7)

    def y_gelu(act, q):
        act.wait_ge(*s5y_tt(q + 1))
        if q >= 2:
            act.wait_ge(*s5y_outs[q % 2](16 * (q // 2)))
        act.activation(YO[:, q % 2].rearrange("c n i -> c i n"), PS_T(6), ACT.Gelu_apprx_tanh).then_inc(*s5y_yo.by(1))
        act.wait_ge(*s5y_yo(q + 1))
        act.dma_start(yt_d[q * P:(q + 1) * P, :], YO[:, q % 2].rearrange("c n i -> c (n i)"))\
           .then_inc(*s5y_outs[q % 2].by(16))

    def dve_s5_y(dve):
        def regroup(q):
            dve.wait_ge(*(s5y_in1 if q % 2 else s5y_in0)(48 * (q // 2 + 1)))
            if q:
                dve.wait_ge(*s5y_t(q))
            nc.vector.tensor_copy(URy[:, :, :].rearrange("n g (j c) -> n g j c", j=SC),
                                  UY[:, q % 2].rearrange("n j (g c) -> n g j c", g=8)).then_inc(*s5y_ur.by(1))

        regroup(0)
        for q in range(8):
            if q + 1 < 8:
                regroup(q + 1)
            dve.wait_ge(*s5y_mm(q + 1))
            if q:
                dve.wait_ge(*s5y_tt(q))
            for par in range(2):
                nc.vector.tensor_copy(YS[:, :, par::2, :].rearrange("n i g c -> n g i c"),
                                      PS[:, 4 + par, :].rearrange("n (g i c) -> n g i c", g=4, i=SC))\
                    .then_inc(*s5y_ys.by(1))

    PC = at("PC", "small", 2304, [P, 64])
    GLUB, GN, DNW, GLW, SCW, DNC = 0, 8, 16, 17, 18, 24
    pc_in = sem("pc_in")
    PC_LOADED = 16 * 8

    def sp_columns(sp):
        for dst, src in (
                (PC[:, GLUB:GLUB + 8], I["s5_glu_b"].rearrange("a (k p) -> p (a k)", p=P)),
                (PC[:, GN:GN + 8], I["ret_gn_g"].rearrange("a (k p) -> p (a k)", p=P)),
                (PC[0:64, DNW:DNW + 1], I["dn_norm_w_2"].rearrange("a p -> p a")),
                (PC[64:P, DNW:DNW + 1], I["dn_norm_w_2"].rearrange("a p -> p a")),
                (PC[0:64, GLW:GLW + 1], I["gla_norm_w_2"].rearrange("a p -> p a")),
                (PC[64:P, GLW:GLW + 1], I["gla_norm_w_2"].rearrange("a p -> p a")),
                (PC[:, SCW:SCW + 6], I["sc_conv_w_2"][0].rearrange("k (c p) -> p (k c)", p=P)),
                (PC[:, DNC:DNC + 24], I["dn_conv_w_2"][0].rearrange("k (c p) -> p (k c)", p=P))):
            sp.dma_start(dst, src).then_inc(*pc_in.by(16))

    LA = at("LA", "stage", 0, [P, 2, L])
    LG = at("LG", "stage", 8192, [P, 2, L])
    la_in = [sem("la_in0"), sem("la_in1")]
    la_mul, la_hi, la_lo = sem("la_mul"), sem("la_hi"), sem("la_lo")

    def sp_load_operand(sp, n, src, gate=None):
        for k in range(KT):
            b = k % 2
            if k >= 2:
                sp.wait_ge(*la_lo(KT * n + k - 1))
            sp.dma_start(LA[:, b, :], src[k * P:(k + 1) * P, :]).then_inc(*la_in[b].by(16))
            if gate is not None:
                sp.dma_start(LG[:, b, :], gate[k * P:(k + 1) * P, :]).then_inc(*la_in[b].by(16))

    def la_arrived(n, k):
        return 64 * n + (16 if n == 0 else 32) * (k // 2 + 1)

    def act_load_operand(act, n, gated):
        for k in range(KT):
            act.wait_ge(*la_in[k % 2](la_arrived(n, k)))
            if gated:
                act.wait_ge(*la_mul(k + 1))
            act.activation(OP_HI[:, k, :], LA[:, k % 2, :], ACT.Copy).then_inc(*la_hi.by(1))

    def dve_load_operand(dve, n, gated):
        for k in range(KT):
            if gated:
                dve.wait_ge(*la_in[k % 2](la_arrived(n, k)))
                nc.vector.tensor_tensor(LA[:, k % 2, :], LA[:, k % 2, :], LG[:, k % 2, :], ALU.mult)\
                    .then_inc(*la_mul.by(1))
            dve.wait_ge(*la_hi(KT * n + k + 1))
            nc.vector.tensor_tensor(OP_LO[:, k, :], LA[:, k % 2, :], OP_HI[:, k, :].bitcast(F32), ALU.subtract)\
                .then_inc(*la_lo.by(1))

    GA = at("GA", "x", 0, [P, 2, HALF])
    ZB = at("ZB", "x", 4096, [P, 2, HALF])
    YB = at("YB", "x", 8192, [P, HALF])
    glu_y, glu_z = sem("glu_y"), sem("glu_z")
    glu_out = [sem("glu_out0"), sem("glu_out1")]

    def act_glu(act):
        g = gemms["glu"]
        act.wait_ge(*pc_in(PC_LOADED))

        def store(n):
            b, a, h, _ = g.units[n]
            c = 4 * (b - g.first_block) + a
            act.wait_ge(*glu_z(n + 1))
            act.dma_start(st_d[c * P:(c + 1) * P, h * HALF:(h + 1) * HALF], ZB[:, n % 2, :])\
               .then_inc(*glu_out[n % 2].by(16))

        for n, (b, a, h, _) in enumerate(g.units):
            c = 4 * (b - g.first_block) + a
            act.wait_ge(*mm_done(g.first + n + 1))
            if n >= 2:
                act.wait_ge(*glu_z(n - 1))
            act.activation(GA[:, n % 2, :], PS[:, (g.first + n) % 4, :], ACT.Sigmoid,
                           bias=PC[:, GLUB + c:GLUB + c + 1]).then_inc(*bank_act.by(1))
            if n:
                store(n - 1)
        store(len(g.units) - 1)

    def dve_glu(dve):
        g = gemms["glu"]
        for n, (b, a, h, _) in enumerate(g.units):
            c = 4 * (b - g.first_block) + a
            s = slice(h * HALF, (h + 1) * HALF)
            if n:
                dve.wait_ge(*glu_z(n))
            nc.vector.tensor_tensor(YB[:, :], OP_HI[:, c, s].bitcast(F32), OP_LO[:, c, s].bitcast(F32), ALU.add)\
                .then_inc(*glu_y.by(1))
            dve.wait_ge(*glu_y(n + 1))
            dve.wait_ge(*bank_act(g.free0_act + n + 1))
            if n >= 2:
                dve.wait_ge(*glu_out[n % 2](16 * (n // 2)))
            nc.vector.tensor_tensor(ZB[:, n % 2, :], YB[:, :], GA[:, n % 2, :], ALU.mult).then_inc(*glu_z.by(1))

    NRC = RH * P + 2 * RH + RH // 2 + 32
    RC = at("RC", "x", 0, [P, NRC])
    RW = RC[:, RH * P:RH * P + 2 * RH]
    RDEC = RC[:, RH * P + 2 * RH:RH * P + 2 * RH + 4]
    RINV = RC[:, NRC - 32:NRC]
    COS = at("COS", "x", 4352, [P, TT, 32])
    SIN = at("SIN", "x", 5376, [P, TT, 32])
    POSI = at("POSI", "x", 6400, [P, TT], I32)
    POSF = at("POSF", "x", 6432, [P, TT])
    ANG = at("ANG", "x", 6656, [P, 3, TT, 32])
    RST = at("RST", "x", 9728, [P, 4, P])
    RTA = at("RTA", "x", 11776, [P, 2 * RH, 2, 32])
    RTB = at("RTB", "x", 15872, [P, 2 * RH, 2, 32])
    QKR = at("QKR", "x", 19968, [P, 2 * RH, 2, 32])
    QKT = at("QKT", "x", 24064, [P, 8, P])
    SCR = at("SCR", "x", 28160, [P, 2, 4, P])
    QKL = at("QKL", "stage", 0, [P, 2 * RH, 2, 32])
    VL = at("VL", "stage", 4096, [P, D])
    GRL = at("GRL", "stage", 8192, [P, 8, P])
    ONR = at("ONR", "stage", 12288, [P, RH, P])
    GOR = at("GOR", "stage", 16384, [P, RH, P])
    BNS = at("BNS", "small", 2560, [P, RH, 6])
    BNM = at("BNM", "small", 2752, [P, RH, 2])
    RRS = at("RRS", "small", 2816, [P, 3, RH])

    rc_in, rq_in, rv_in, rg_in = (sem(n) for n in ("rc_in", "rq_in", "rv_in", "rg_in"))
    r_ang, r_trig, r_ab, r_rot, r_turn, r_qkt, r_sc, r_scr, r_o, r_kv = (
        sem(n) for n in ("r_ang", "r_trig", "r_ab", "r_rot", "r_turn", "r_qkt", "r_sc", "r_scr", "r_o", "r_kv"))
    r_rst, r_var, r_root, r_on, r_back, r_g, r_hi, r_lo = (
        sem(n) for n in ("r_rst", "r_var", "r_root", "r_on", "r_back", "r_g", "r_hi", "r_lo"))

    def sp_retention(sp):
        for s in glu_out:
            sp.wait_ge(*s(16 * 8))
        sp.wait_ge(*glu_z(16))
        sp.dma_start(RC[:, :], I["c_ret"]).then_inc(*rc_in.by(16))
        sp.dma_start(POSI[:, :], I["positions"].rearrange("a (t p) -> p (a t)", p=P)).then_inc(*rc_in.by(16))
        for t in range(TT):
            rows = slice(t * P, (t + 1) * P)
            if t:
                sp.wait_ge(*r_ab(2 * t))
            sp.dma_start(QKL[:, :, :, :].rearrange("p h a b -> p (h a b)"), qk_d[rows, :]).then_inc(*rq_in.by(16))
            if t:
                sp.wait_ge(*r_kv(t))
            sp.dma_start(VL[:, :], v_d[rows, :]).then_inc(*rv_in.by(16))
            if t:
                sp.wait_ge(*r_g(2 * t - 1))
            sp.dma_start(GRL[:, :, :], gret_d.rearrange("(k p) t -> p k t", p=P)[:, :, rows]).then_inc(*rg_in.by(16))

    def pe_retention(pe):
        T = nc.tensor
        pe.wait_ge(*bank_act(gemms["glu"].free1_act))

        def turn_and_scores(t):
            pe.wait_ge(*r_rot(t + 1))
            if t >= 2:
                pe.wait_ge(*r_g(2 * t - 3))
            flat = QKR[:, :, :, :].rearrange("p h a b -> p (h a b)")
            for c in range(8):
                ins = T.transpose(PS_T(0)[:, c, :], flat[:, c * P:(c + 1) * P], ident)
            ins.then_inc(*r_turn.by(1))
            pe.wait_ge(*r_qkt(t + 1))
            if t:
                pe.wait_ge(*r_scr(t))
            for h in range(RH):
                lo, p = 64 * (h % 2), h // 2
                ins = T.matmul(PS[:, 2 + h % 2, p * P:(p + 1) * P], QKT[lo:lo + 64, 4 + p, :],
                               QKT[lo:lo + 64, p, :], start=True, stop=True)
            ins.then_inc(*r_sc.by(1))

        def outputs(t):
            pe.wait_ge(*r_scr(t + 1))
            pe.wait_ge(*rv_in(16 * (t + 1)))
            if t:
                pe.wait_ge(*r_rst(3 * t + 1))
                pe.wait_ge(*r_on(t))
            else:
                pe.wait_ge(*r_rst(1))
            for h in range(RH):
                lo, p = 64 * (h % 2), h // 2
                o = PS[:, 4 + h % 2, p * P:(p + 1) * P]
                T.matmul(o, SCR[:, h % 2, p, :], VL[:, h * P:(h + 1) * P], start=True, stop=False)
                ins = T.matmul(o, QKT[lo:lo + 64, p, :], RST[lo:lo + 64, p, :], start=False, stop=True)
            ins.then_inc(*r_o.by(1))

        def update(t):
            flat = QKR[:, :, :, :].rearrange("p h a b -> p (h a b)")
            for p in range(4):
                ins = T.matmul(PS[:, 6 + p // 2, (p % 2) * 256:(p % 2) * 256 + 256],
                               flat[:, HALF + p * P:HALF + (p + 1) * P], VL[:, p * 256:(p + 1) * 256],
                               start=True, stop=True)
            ins.then_inc(*r_kv.by(1))

        def turn_out(t):
            pe.wait_ge(*r_on(t + 1))
            if t + 1 < TT:
                pe.wait_ge(*r_qkt(t + 2))
            for h in range(RH):
                ins = T.transpose(PS_T(0)[:, h, :], ONR[:, h, :], ident)
            ins.then_inc(*r_back.by(1))

        turn_and_scores(0)
        for t in range(TT):
            outputs(t)
            update(t)
            if t + 1 < TT:
                turn_and_scores(t + 1)
            turn_out(t)

    def act_retention(act):
        act.wait_ge(*r_ang(1))
        act.activation(SIN[:, :, :], ANG[:, 1, :, :], ACT.Sin).then_inc(*r_trig.by(1))
        act.activation(COS[:, :, :], ANG[:, 2, :, :], ACT.Sin, scale=-1.0, bias=halfpi[:, :]).then_inc(*r_trig.by(1))

        def turned(t):
            act.wait_ge(*r_turn(t + 1))
            act.activation(QKT[:, :, :], PS_T(0), ACT.Copy).then_inc(*r_qkt.by(1))

        turned(0)
        for t in range(TT):
            if t + 1 < TT:
                act.wait_ge(*r_o(t + 1))
                turned(t + 1)
            act.wait_ge(*r_var(t + 1))
            act.activation(RRS[:, 1, :], RRS[:, 0, :], ACT.Sqrt).then_inc(*r_root.by(1))
            act.wait_ge(*r_g(2 * t + 2))
            act.activation(OP_HI[:, :, t * P:(t + 1) * P], GOR[:, :, :], ACT.Copy).then_inc(*r_hi.by(1))

    def dve_retention(dve, chain):
        V = nc.vector
        MUL, ADD, SUB = ALU.mult, ALU.add, ALU.subtract
        dve.wait_ge(*rc_in(32))
        V.memset(RST[:, :, :], 0.0).then_inc(*r_rst.by(1))
        chain(V.tensor_copy(POSF[:, :], POSI[:, :]))
        chain(V.tensor_tensor(ANG[:, 0, :, :], POSF[:, :].unsqueeze(2).to_broadcast([P, TT, 32]),
                              RINV.unsqueeze(1).to_broadcast([P, TT, 32]), MUL))
        reduce_angle(chain, ANG[:, 0, :, :], ANG[:, 1, :, :], ANG[:, 2, :, :])
        V.scalar_tensor_tensor(ANG[:, 2, :, :], ANG[:, 1, :, :], -1.0, ANG[:, 1, :, :], MUL, ALU.max)\
            .then_inc(*r_ang.by(1))
        dve.wait_ge(*r_trig(2))

        def rotate(t):
            dve.wait_ge(*rq_in(16 * (t + 1)))
            shape = [P, 2 * RH, 2, 32]
            cos = COS[:, t, :].unsqueeze(1).unsqueeze(1).to_broadcast(shape)
            sin = SIN[:, t, :].unsqueeze(1).unsqueeze(1).to_broadcast(shape)
            V.tensor_tensor(RTA[:, :, :, :], QKL[:, :, :, :], cos, MUL).then_inc(*r_ab.by(1))
            V.tensor_tensor(RTB[:, :, :, :], QKL[:, :, :, :], sin, MUL).then_inc(*r_ab.by(1))
            dve.wait_ge(*r_ab(2 * t + 2))
            if t:
                dve.wait_ge(*r_kv(t))
            chain(V.tensor_tensor(QKR[:, :, 0, :], RTA[:, :, 0, :], RTB[:, :, 1, :], SUB))
            chain(V.tensor_tensor(QKR[:, :, 1, :], RTB[:, :, 0, :], RTA[:, :, 1, :], ADD))
            flat = QKR[:, :, :, :].rearrange("p h a b -> p h (a b)")
            V.tensor_tensor(flat, flat, RW.unsqueeze(2).to_broadcast([P, 2 * RH, 64]), MUL).then_inc(*r_rot.by(1))

        rotate(0)
        for t in range(TT):
            dve.wait_ge(*r_sc(t + 1))
            if t:
                dve.wait_ge(*r_o(t))
            V.tensor_tensor(SCR[:, :, :, :].rearrange("p a b i -> p (a b i)"),
                            PS[:, 2:4, :].rearrange("p b n -> p (b n)"), RC[:, 0:RH * P], MUL).then_inc(*r_scr.by(1))
            if t + 1 < TT:
                rotate(t + 1)
            dve.wait_ge(*r_kv(t + 1))
            dve.wait_ge(*r_o(t + 1))
            kv = PS[:, 6:8, :].rearrange("p b (q e) -> p (b q) e", q=2)
            V.tensor_tensor(RST[:, :, :], RST[:, :, :], RDEC.unsqueeze(2).to_broadcast([P, 4, P]), MUL)\
                .then_inc(*r_rst.by(1))
            dve.wait_ge(*r_rst(3 * t + 2))
            V.tensor_tensor(RST[0:64, :, :], RST[0:64, :, :], kv[0:64, :, 0:P], ADD).then_inc(*r_rst.by(1))
            V.tensor_tensor(RST[64:P, :, :], RST[64:P, :, :], kv[64:P, :, P:2 * P], ADD).then_inc(*r_rst.by(1))
            for h in range(RH):
                V.bn_stats(BNS[:, h, :], PS[:, 4 + h % 2, (h // 2) * P:(h // 2 + 1) * P]).then_inc(*chain.s.by(1))
            chain.n += RH
            dve.wait_ge(*chain.s(chain.n))
            for h in range(RH):
                V.bn_aggr(BNM[:, h, :], BNS[:, h, :]).then_inc(*chain.s.by(1))
            chain.n += RH
            dve.wait_ge(*chain.s(chain.n))
            V.tensor_scalar(RRS[:, 0, :], BNM[:, :, 1], EPS, None, ADD).then_inc(*r_var.by(1))
            dve.wait_ge(*r_root(t + 1))
            chain(V.reciprocal(RRS[:, 2, :], RRS[:, 1, :]))
            if t:
                dve.wait_ge(*r_back(t))
            for h in range(RH):
                ins = V.tensor_scalar(ONR[:, h, :], PS[:, 4 + h % 2, (h // 2) * P:(h // 2 + 1) * P],
                                      BNM[:, h, 0:1], RRS[:, 2, h:h + 1], SUB, MUL)
            ins.then_inc(*r_on.by(1))
            dve.wait_ge(*r_back(t + 1))
            dve.wait_ge(*rg_in(16 * (t + 1)))
            if t:
                dve.wait_ge(*r_lo(t))
            V.tensor_tensor(GOR[:, :, :], PS_T(0), GRL[:, :, :], MUL).then_inc(*r_g.by(1))
            dve.wait_ge(*r_g(2 * t + 1))
            V.tensor_tensor(GOR[:, :, :], GOR[:, :, :], PC[:, GN:GN + 8].unsqueeze(2).to_broadcast([P, 8, P]),
                            MUL).then_inc(*r_g.by(1))
            dve.wait_ge(*r_hi(t + 1))
            V.tensor_tensor(OP_LO[:, :, t * P:(t + 1) * P], GOR[:, :, :],
                            OP_HI[:, :, t * P:(t + 1) * P].bitcast(F32), SUB).then_inc(*r_lo.by(1))

    KA = at("KA", "stage", 0, [P, KT, MEM])
    VA = at("VA", "stage", 8192, [P, 2, D])
    QTL = at("QTL", "x", 0, [P, 2, KT, P])
    PM = at("PM", "x", 8192, [P, XH, MEM])
    PT = at("PT", "x", 12288, [P, 8, P])
    XST = at("XST", "x", 16384, [P, 4, XH])
    xa_kv, xa_q = sem("xa_kv"), (sem("xa_q0"), sem("xa_q1"))
    xa_s, xa_nm, xa_e, xa_p, xa_t, xa_pt, xa_o, xa_hi, xa_lo = (
        sem(n) for n in ("xa_s", "xa_nm", "xa_e", "xa_p", "xa_t", "xa_pt", "xa_o", "xa_hi", "xa_lo"))
    SCALE = XD ** -0.5

    def sp_attention(sp):
        sp.dma_start(KA[:, :, :], ka_d.rearrange("(k p) m -> p k m", p=P)).then_inc(*xa_kv.by(16))
        sp.dma_start(VA[:, :, :], va_d.rearrange("(k p) n -> p k n", p=P)).then_inc(*xa_kv.by(16))
        for t in range(TT):
            if t >= 2:
                sp.wait_ge(*xa_s(t - 1))
            sp.dma_start(QTL[:, t % 2], qa_d.rearrange("(k p) t -> p k t", p=P)[:, :, t * P:(t + 1) * P])\
              .then_inc(*xa_q[t % 2].by(16))

    def pe_attention(pe):
        T = nc.tensor
        pe.wait_ge(*bank_act(gemms["xq"].free1_act))
        pe.wait_ge(*xa_kv(32))

        def scores(t):
            pe.wait_ge(*xa_q[t % 2](16 * (t // 2 + 1)))
            if t >= 2:
                pe.wait_ge(*xa_e(4 * (t - 1)))
            for h in range(XH):
                for k in range(2):
                    ins = T.matmul(PS[:, 2 * (t % 2) + h // 2, (h % 2) * MEM:(h % 2 + 1) * MEM],
                                   QTL[:, t % 2, 2 * h + k, :], KA[:, 2 * h + k, :], start=k == 0, stop=k == 1)
            ins.then_inc(*xa_s.by(1))

        scores(0)
        for t in range(TT):
            if t + 1 < TT:
                scores(t + 1)
            pe.wait_ge(*xa_p(t + 1))
            if t:
                pe.wait_ge(*xa_pt(t))
            for c in range(8):
                ins = T.transpose(PS_T(4)[:, c, :], PM[:, c // 2, (c % 2) * P:(c % 2 + 1) * P], ident)
            ins.then_inc(*xa_t.by(1))
            pe.wait_ge(*xa_pt(t + 1))
            if t:
                pe.wait_ge(*xa_lo(t))
            for c in range(8):
                for m in range(2):
                    ins = T.matmul(PS_T(6)[:, c, :], VA[:, m, c * P:(c + 1) * P], PT[:, 2 * (c // 2) + m, :],
                                   start=m == 0, stop=m == 1)
            ins.then_inc(*xa_o.by(1))

    def act_attention(act):
        for t in range(TT):
            act.wait_ge(*xa_nm(t + 1))
            if t:
                act.wait_ge(*xa_t(t))
            for h in range(XH):
                act.activation(PM[:, h, :], PS[:, 2 * (t % 2) + h // 2, (h % 2) * MEM:(h % 2 + 1) * MEM], ACT.Exp,
                               bias=XST[:, 1, h:h + 1], scale=SCALE, accum_out=XST[:, 2, h:h + 1]).then_inc(*xa_e.by(1))
            act.wait_ge(*xa_t(t + 1))
            if t:
                act.wait_ge(*xa_o(t))
            act.activation(PT[:, :, :], PS_T(4), ACT.Copy).then_inc(*xa_pt.by(1))
            act.wait_ge(*xa_o(t + 1))
            act.activation(OP_HI[:, :, t * P:(t + 1) * P], PS_T(6), ACT.Copy).then_inc(*xa_hi.by(1))

    def dve_attention(dve, chain):
        V = nc.vector
        for t in range(TT):
            dve.wait_ge(*xa_s(t + 1))
            chain(V.tensor_reduce(XST[:, 0, :], PS[:, 2 * (t % 2):2 * (t % 2) + 2, :]
                                  .rearrange("p b (h m) -> p (b h) m", h=2), AX.X, ALU.max))
            V.tensor_scalar(XST[:, 1, :], XST[:, 0, :], -SCALE, None, ALU.mult).then_inc(*xa_nm.by(1))
            dve.wait_ge(*xa_e(4 * (t + 1)))
            chain(V.reciprocal(XST[:, 3, :], XST[:, 2, :]))
            V.tensor_tensor(PM[:, :, :], PM[:, :, :], XST[:, 3, :].unsqueeze(2).to_broadcast([P, XH, MEM]),
                            ALU.mult).then_inc(*xa_p.by(1))
            dve.wait_ge(*xa_hi(t + 1))
            V.tensor_tensor(OP_LO[:, :, t * P:(t + 1) * P], PS_T(6),
                            OP_HI[:, :, t * P:(t + 1) * P].bitcast(F32), ALU.subtract).then_inc(*xa_lo.by(1))

    inplace = sem("inplace")
    x_out = sem("x_out")

    def dve_norm_inplace(dve, q, chain):
        chain(dve_norm_rstd(dve, q))
        dve.wait_ge(*grow_in(16 * (q + 1)))
        for t in range(TT):
            nc.vector.scalar_tensor_tensor(X[:, t, :], X[:, t, :], st[:, 24 + t:25 + t], GROW[:, :],
                                           ALU.mult, ALU.mult).then_inc(*inplace.by(1))

    def rows_of(ap):
        return ap.rearrange("(t p) d -> p t d", p=P)

    dqkv_d = scratch("dqkv_d", (L, 3 * GW))
    CB = at("CB", "x", 0, [P, 3, L])
    CTP = at("CTP", "x", 12288, [P, 2 + L])
    CAC = at("CAC", "x", 16416, [P, 2, L])
    CQ = at("CQ", "x", 24608, [P, 2, 1032])
    CSL = at("CSL", "stage", 0, [P, 2, L])
    OV = at("OV", "stage", 8192, [P, 2, TT, P])
    cq_in, cb_in, cv_zero, dc_acc, dc_s, dc_t, dc_ov = (
        sem(n) for n in ("cq_in0", "cb_in", "cv_zero", "dc_acc", "dc_s", "dc_t", "dc_ov"))
    cq_ins, dc_out = (cq_in, sem("cq_in1")), (sem("dc_out0"), sem("dc_out1"))
    sc_acc, sc_hi, sc_lo = sem("sc_acc"), sem("sc_hi"), sem("sc_lo")
    NDC = 3 * GW // P
    OPC_CONV = 2

    def sp_conv(sp):
        yield -2
        wait_stores(sp, "pch")
        for n in range(NDC):
            yield conv_time(n - 2) + 0.1
            if n >= 2:
                sp.wait_ge(*dc_acc(n - 1))
            sp.dma_start(CQ[:, n % 2, 3:3 + L], pch_d[3 * GW + n * P:3 * GW + (n + 1) * P, :]).then_inc(*cq_ins[n % 2].by(16))
        yield -0.45
        sp.wait_ge(*sg_lo(1))
        for n in range(2):
            if n:
                yield -0.149
                sp.wait_ge(*sc_acc(n))
            sp.dma_start(CB[:, :, :], pch_d[0:3 * GW, :].rearrange("(k c p) t -> c p k t", k=3, p=P)[n])\
              .then_inc(*cb_in.by(16))

    def conv_time(n):
        return -1 + 0.14 * n

    def dve_conv(dve, chain):
        V = nc.vector
        MUL, ADD = ALU.mult, ALU.add
        V.memset(CTP[:, 0:2], 0.0).then_inc(*cv_zero.by(1))
        V.memset(CQ[:, :, 0:3], 0.0).then_inc(*cv_zero.by(1))
        dve.wait_ge(*cv_zero(2))
        for n in range(NDC):
            w = lambda k: PC[:, DNC + k * NDC + n:DNC + k * NDC + n + 1]
            acc = CAC[:, n % 2, :]
            yield conv_time(n)
            dve.wait_ge(*cq_ins[n % 2](16 * (n // 2 + 1)))
            if n >= 2:
                dve.wait_ge(*dc_s(n - 1))
            chain(V.tensor_scalar(acc, CQ[:, n % 2, 0:L], w(0), None, MUL))
            for k in (1, 2):
                chain(V.scalar_tensor_tensor(acc, CQ[:, n % 2, k:k + L], w(k), acc, MUL, ADD))
            V.scalar_tensor_tensor(acc, CQ[:, n % 2, 3:3 + L], w(3), acc, MUL, ADD).then_inc(*dc_acc.by(1))
        yield -0.15
        dve.wait_ge(*dc_s(NDC))
        for n in range(2):
            w = lambda k: PC[:, SCW + 2 * k + n:SCW + 2 * k + n + 1]
            acc = CAC[:, n, :]
            dve.wait_ge(*cb_in(16 * (n + 1)))
            chain(V.tensor_tensor(CTP[:, 2:2 + L], CB[:, 1, :], CB[:, 2, :], MUL))
            chain(V.tensor_scalar(acc, CTP[:, 0:L], w(0), None, MUL))
            for k in (1, 2):
                chain(V.scalar_tensor_tensor(acc, CTP[:, k:k + L], w(k), acc, MUL, ADD))
            V.tensor_tensor(acc, acc, CB[:, 0, :], MUL).then_inc(*sc_acc.by(1))
            yield -0.14 + 0.05 * n
            dve.wait_ge(*sc_hi(n + 1))
            V.tensor_tensor(OP_LO[:, OPC_CONV + n, :], acc, OP_HI[:, OPC_CONV + n, :].bitcast(F32), ALU.subtract)\
                .then_inc(*sc_lo.by(1))

    def act_conv(act):
        def store(n):
            act.wait_ge(*dc_t(n + 1))
            if n >= 2:
                act.wait_ge(*dc_out[n % 2](16 * (n // 2)))
            act.activation(OV[:, n % 2], PS_T(2 * (n % 2)), ACT.Copy).then_inc(*dc_ov.by(1))
            act.wait_ge(*dc_ov(n + 1))
            act.dma_start(dqkv_d[:, n * P:(n + 1) * P].rearrange("(t p) c -> p t c", p=P), OV[:, n % 2])\
               .then_inc(*dc_out[n % 2].by(16))

        for n in range(NDC):
            yield conv_time(n) + 0.02
            act.wait_ge(*dc_acc(n + 1))
            if n >= 2:
                act.wait_ge(*dc_t(n - 1))
            act.activation(CSL[:, n % 2, :], CAC[:, n % 2, :], ACT.Silu).then_inc(*dc_s.by(1))
            if n:
                store(n - 1)
        yield -0.2
        store(NDC - 1)
        for n in range(2):
            yield -0.145 + 0.05 * n
            act.wait_ge(*sc_acc(n + 1))
            act.activation(OP_HI[:, OPC_CONV + n, :], CAC[:, n, :], ACT.Copy).then_inc(*sc_hi.by(1))

    def pe_conv(pe):
        for n in range(NDC):
            yield conv_time(n) + 0.03
            pe.wait_ge(*dc_s(n + 1))
            if n >= 2:
                pe.wait_ge(*dc_ov(n - 1))
            for t in range(TT):
                ins = nc.tensor.transpose(PS_T(2 * (n % 2))[:, t, :], CSL[:, n % 2, t * P:(t + 1) * P], ident)
            ins.then_inc(*dc_t.by(1))

    SUV = at("SUV", "x", 8192, [P, 2, 2, GW])
    SGL = at("SGL", "x", 12288, [P, 2, GW])
    SVN = at("SVN", "x", 14336, [P, GH, GD])
    SYA = at("SYA", "x", 15360, [P, GH, GD])
    WSL = at("WSL", "x", 16384, [P, GH, P])
    WST = at("WST", "x", 18432, [P, GH, P])
    LNW = at("LNW", "x", 20480, [P, GH, GD])
    LNB = at("LNB", "x", 21504, [P, GH, GD])
    BSC = at("BSC", "x", 22528, [P, GH])
    SBN = at("SBN", "x", 22560, [P, 16])
    SOUT = at("SOUT", "x", 0, [P, 2, L])
    su_in = (sem("su_in0"), sem("su_in1"))
    sg_in, sg_w, sg_wt, sg_gl, sg_var, sg_root, sg_vn, sg_mm, sg_y, sg_t, sg_hi, sg_lo = (
        sem(n) for n in ("sg_in", "sg_w", "sg_wt", "sg_gl", "sg_var", "sg_root", "sg_vn", "sg_mm", "sg_y", "sg_t",
                         "sg_hi", "sg_lo"))

    def sp_sgu(sp):
        yield 0
        wait_stores(sp, "ptok")
        sp.wait_ge(*x_out(32))
        sp.wait_ge(*xn_full(turned_base(4) + TT))
        sp.dma_start(WSL[:, :, :], I["sgu_w_spatial_2"][0].rearrange("h t s -> t h s")).then_inc(*sg_in.by(16))
        sp.dma_start(LNW[:, :, :].rearrange("p h d -> p (h d)"), I["sgu_ln_w_2"].to_broadcast([P, GW])).then_inc(*sg_in.by(16))
        sp.dma_start(LNB[:, :, :].rearrange("p h d -> p (h d)"), I["sgu_ln_b_2"].to_broadcast([P, GW])).then_inc(*sg_in.by(16))
        sp.dma_start(BSC[:, :], I["sgu_b_spatial_2"][0].rearrange("h t -> t h")).then_inc(*sg_in.by(16))
        for t in range(TT):
            yield max(0, 3 * t - 4)
            if t >= 2:
                sp.wait_ge(*sg_gl(t - 1))
            sp.dma_start(SUV[:, t % 2].rearrange("p a n -> p (a n)"), ptok_d[t * P:(t + 1) * P, C_AU:C_AU + 2 * GW])\
              .then_inc(*su_in[t % 2].by(16))

    def pe_sgu(pe):
        T = nc.tensor
        yield 1.5
        pe.wait_ge(*sg_in(64))
        for h in range(GH):
            ins = T.transpose(PS[:, 4, h * P:(h + 1) * P], WSL[:, h, :], ident)
        ins.then_inc(*sg_w.by(1))
        for t in range(TT):
            yield 3 * t + 2.5
            if t == 0:
                pe.wait_ge(*sg_wt(1))
            pe.wait_ge(*sg_vn(t + 1))
            if t:
                pe.wait_ge(*sg_y(2 * t - 1))
            for h in range(GH):
                ins = T.matmul(PS[:, 5, h * GD:(h + 1) * GD], WST[:, h, :], SVN[:, h, :], start=True, stop=True)
            ins.then_inc(*sg_mm.by(1))
            yield 3 * t + 3.5
            pe.wait_ge(*sg_y(2 * t + 2))
            if t:
                pe.wait_ge(*sg_hi(t))
            flat = SYA[:, :, :].rearrange("p h d -> p (h d)")
            for c in range(2):
                ins = T.transpose(PS[:, 6, c * P:(c + 1) * P], flat[:, c * P:(c + 1) * P], ident)
            ins.then_inc(*sg_t.by(1))

    def act_sgu(act):
        for t in range(TT):
            yield 3 * t + 1.92 if t else 1.6
            act.wait_ge(*su_in[t % 2](16 * (t // 2 + 1)))
            if t:
                act.wait_ge(*sg_y(2 * t))
            act.activation(SGL[:, :, :], SUV[:, t % 2], ACT.Gelu_apprx_tanh).then_inc(*sg_gl.by(1))
            yield 3 * t + 2.1
            act.wait_ge(*sg_var(t + 1))
            act.activation(SBN[:, 9:10], SBN[:, 8:9], ACT.Sqrt).then_inc(*sg_root.by(1))
            yield 3 * t + 3.6
            act.wait_ge(*sg_t(t + 1))
            act.activation(SOUT[:, :, t * P:(t + 1) * P], PS[:, 6, 0:2 * P].rearrange("p (c t) -> p c t", c=2),
                           ACT.Copy).then_inc(*sg_hi.by(1))
        yield 30
        act.wait_ge(*mm_done(gemms["pch"].end))
        act.wait_ge(*sg_hi(TT))
        act.activation(OP_HI[:, 0:2, :], SOUT[:, :, :], ACT.Copy).then_inc(*sg_hi.by(1))

    def dve_sgu(dve, chain):
        V = nc.vector
        MUL, ADD, SUB = ALU.mult, ALU.add, ALU.subtract
        yield 1.55
        dve.wait_ge(*sg_w(1))
        V.tensor_tensor(WST[:, :, :], PS[:, 4, :].rearrange("p (h t) -> p h t", h=GH),
                        K["causal"].unsqueeze(1).to_broadcast([P, GH, P]), MUL).then_inc(*sg_wt.by(1))
        for t in range(TT):
            yield 3 * t + 2
            dve.wait_ge(*sg_gl(t + 1))
            chain(V.bn_stats(SBN[:, 0:6], SGL[:, 1, :]))
            chain(V.bn_aggr(SBN[:, 6:8], SBN[:, 0:6]))
            V.tensor_scalar(SBN[:, 8:9], SBN[:, 7:8], EPS, None, ADD).then_inc(*sg_var.by(1))
            yield 3 * t + 2.2
            dve.wait_ge(*sg_root(t + 1))
            chain(V.reciprocal(SBN[:, 10:11], SBN[:, 9:10]))
            if t:
                dve.wait_ge(*sg_mm(t))
            flat = SVN[:, :, :].rearrange("p h d -> p (h d)")
            chain(V.tensor_scalar(flat, SGL[:, 1, :], SBN[:, 6:7], SBN[:, 10:11], SUB, MUL))
            chain(V.tensor_tensor(SVN[:, :, :], SVN[:, :, :], LNW[:, :, :], MUL))
            V.tensor_tensor(SVN[:, :, :], SVN[:, :, :], LNB[:, :, :], ADD).then_inc(*sg_vn.by(1))
            yield 3 * t + 2.6
            dve.wait_ge(*sg_mm(t + 1))
            if t:
                dve.wait_ge(*sg_t(t))
            V.tensor_tensor(SYA[:, :, :], PS[:, 5, 0:GW].rearrange("p (h d) -> p h d", h=GH),
                            BSC[:, :].unsqueeze(2).to_broadcast([P, GH, GD]), ADD).then_inc(*sg_y.by(1))
            dve.wait_ge(*sg_y(2 * t + 1))
            V.tensor_tensor(SYA[:, :, :], SYA[:, :, :], SGL[:, 0, :].rearrange("p (h d) -> p h d", h=GH), MUL)\
                .then_inc(*sg_y.by(1))
        yield 30.1
        dve.wait_ge(*sg_hi(TT + 1))
        V.tensor_tensor(OP_LO[:, 0:2, :], SOUT[:, :, :], OP_HI[:, 0:2, :].bitcast(F32), SUB).then_inc(*sg_lo.by(1))

    class Finish:
        def __init__(self, tag, region, off, op_tile, weight):
            self.OQ = at(f"{tag}OQ", region, off, [P, GH, GD])
            self.O = at(f"{tag}O", region, off + 1024, [P, GH, GD])
            self.SQ = at(f"{tag}SQ", region, off + 2048, [P, GH, GD])
            self.ZS = at(f"{tag}ZS", region, off + 3072, [P, GH, GD])
            self.OG = at(f"{tag}OG", region, off + 4096, [P, 2, P])
            self.ST = at(f"{tag}ST", region, off + 5120, [P, 4, GH])
            self.op_tile, self.weight = op_tile, weight
            self.q_t, self.q = sem(f"{tag}_q_t"), sem(f"{tag}_q")
            self.av, self.zs = sem(f"{tag}_av"), sem(f"{tag}_zs")
            self.ms, self.root = sem(f"{tag}_ms"), sem(f"{tag}_root")
            self.on, self.turn = sem(f"{tag}_on"), sem(f"{tag}_turn")
            self.og, self.hi, self.lo = sem(f"{tag}_og"), sem(f"{tag}_hi"), sem(f"{tag}_lo")

        def act_q(self, act, t, bank):
            act.wait_ge(*self.q_t(t + 1))
            if t:
                act.wait_ge(*self.on(t))
            act.activation(self.OQ[:, :, :].rearrange("p (q a) d -> p a q d", a=2),
                           PS[:, bank:bank + 2, 0:P].rearrange("p a (q d) -> p a q d", q=2), ACT.Copy)\
               .then_inc(*self.q.by(1))

        def dve_norm(self, dve, chain, t, bank, later):
            V = nc.vector
            dve.wait_ge(*self.q(t + 1))
            dve.wait_ge(*self.av(t + 1))
            if t:
                dve.wait_ge(*self.turn(t))
            chain(V.tensor_tensor(self.O[:, :, :], self.OQ[:, :, :],
                                  PS[:, bank, 0:GW].rearrange("p (h d) -> p h d", h=GH), ALU.add))
            chain(V.tensor_tensor(self.SQ[:, :, :], self.O[:, :, :], self.O[:, :, :], ALU.mult))
            chain(V.tensor_reduce(self.ST[:, 0, :], self.SQ[:, :, :], AX.X, ALU.add))
            V.tensor_scalar(self.ST[:, 1, :], self.ST[:, 0, :], 1.0 / GD, EPS, ALU.mult, ALU.add).then_inc(*self.ms.by(1))
            yield later
            dve.wait_ge(*self.root(t + 1))
            chain(V.reciprocal(self.ST[:, 3, :], self.ST[:, 2, :]))
            chain(V.tensor_tensor(self.O[:, :, :], self.O[:, :, :],
                                  self.ST[:, 3, :].unsqueeze(2).to_broadcast([P, GH, GD]), ALU.mult))
            dve.wait_ge(*self.zs(t + 1))
            V.tensor_tensor(self.O[:, :, :], self.O[:, :, :], self.ZS[:, :, :], ALU.mult).then_inc(*self.on.by(1))

        def act_root(self, act, t):
            act.wait_ge(*self.ms(t + 1))
            act.activation(self.ST[:, 2, :], self.ST[:, 1, :], ACT.Sqrt).then_inc(*self.root.by(1))

        def act_z(self, act, t, z):
            if t:
                act.wait_ge(*self.on(t))
            act.activation(self.ZS[:, :, :].rearrange("p h d -> p (h d)"), z, ACT.Silu).then_inc(*self.zs.by(1))

        def pe_turn(self, pe, t, bank):
            pe.wait_ge(*self.on(t + 1))
            flat = self.O[:, :, :].rearrange("p h d -> p (h d)")
            for c in range(2):
                ins = nc.tensor.transpose(PS[:, bank, c * P:(c + 1) * P], flat[:, c * P:(c + 1) * P], ident)
            ins.then_inc(*self.turn.by(1))

        def dve_gain(self, dve, t, bank):
            dve.wait_ge(*self.turn(t + 1))
            if t:
                dve.wait_ge(*self.lo(t))
            nc.vector.tensor_scalar(self.OG[:, :, :].rearrange("p c t -> p (c t)"), PS[:, bank, 0:2 * P],
                                    PC[:, self.weight:self.weight + 1], None, ALU.mult).then_inc(*self.og.by(1))

        def act_hi(self, act, t):
            act.wait_ge(*self.og(t + 1))
            k = self.op_tile
            act.activation(OP_HI[:, k:k + 2, t * P:(t + 1) * P], self.OG[:, :, :], ACT.Copy).then_inc(*self.hi.by(1))

        def dve_lo(self, dve, t):
            dve.wait_ge(*self.hi(t + 1))
            k = self.op_tile
            nc.vector.tensor_tensor(OP_LO[:, k:k + 2, t * P:(t + 1) * P], self.OG[:, :, :],
                                    OP_HI[:, k:k + 2, t * P:(t + 1) * P].bitcast(F32), ALU.subtract)\
                .then_inc(*self.lo.by(1))

    LEVELS = (1, 2, 4, 8, 16, 32)
    DQ = at("DQ", "x", 0, [P, 2, 3, GH, GD])
    DZ = at("DZ", "x", 6144, [P, 2, GW])
    CAB = at("CAB", "x", 8192, [P, TT, 8])
    GTB = at("GTB", "x", 8448, [P, 6, TT, GH])
    ADT = at("ADT", "x", 9216, [P, 3, GH])
    AG = at("AG", "x", 9344, [P, 4, P])
    EX = at("EX", "x", 11392, [P, 4, GH])
    DRS = at("DRS", "x", 11456, [P, 3, 8])
    KK = at("KK", "x", 11776, [P, 7, GH, GD])
    TR = at("TR", "x", 18944, [P, 8, P])
    DTB = at("DTB", "x", 23040, [P, 4, P])
    DTU = at("DTU", "x", 25088, [P, 4, P])
    LT = at("LT", "x", 27136, [P, 4, P])
    AT = at("AT", "x", 29184, [P, 4, P])
    DU = at("DU", "x", 31232, [P, GH, GD])
    CTM = at("CTM", "stage", 0, [P, 2, 4, P])
    P1 = at("P1", "stage", 4096, [P, 4, P])
    VV = at("VV", "stage", 6144, [P, 4, P])
    VT = at("VT", "stage", 8192, [P, 4, P])
    WT = at("WT", "stage", 10240, [P, 2, P])
    VN = at("VN", "stage", 11264, [P, GH, GD])
    SD = at("SD", "stage", 12288, [P, 2, GD])
    DECP = at("DECP", "stage", 12800, [P, 2, 2])
    K_HAT, K_B, Q_HAT, Q_G, K_BG, K_D, V_B = range(7)
    G_, BETA = 4, 5
    fin_d = Finish("dn", "stage", 13312, 4, DNW)
    dn = {n: sem(f"dn_{n}") for n in (
        "in0", "in1", "par", "sp", "e1", "g", "ag", "gm", "ex", "dec", "dt", "ss", "rt", "kk", "tr", "trc", "la",
        "lt", "ct", "c1", "p1", "p1c", "w", "v", "uw", "u", "ws", "vn", "ks", "s", "zero")}

    def sp_delta(sp):
        yield 0
        sp.wait_ge(*sc_lo(2))
        for s in dc_out:
            sp.wait_ge(*s(16 * NDC // 2))
        sp.dma_start(CAB[:, :, :], ptok_d[:, C_CA:C_CA + 8].rearrange("(t p) c -> p t c", p=P)).then_inc(*dn["par"].by(16))
        sp.dma_start(ADT[:, 0, :], I["dn_a_log_2"].to_broadcast([P, GH])).then_inc(*dn["par"].by(16))
        sp.dma_start(ADT[:, 1, :], I["dn_dt_bias_2"].to_broadcast([P, GH])).then_inc(*dn["par"].by(16))
        for t in range(TT):
            yield max(0, t - 0.8)
            rows, s = slice(t * P, (t + 1) * P), dn[f"in{t % 2}"]
            if t >= 2:
                sp.wait_ge(*dn["kk"](t - 1))
                sp.wait_ge(*fin_d.zs(t - 1))
            sp.dma_start(DQ[:, t % 2].rearrange("p a h d -> p (a h d)"), dqkv_d[rows, :]).then_inc(*s.by(16))
            sp.dma_start(DZ[:, t % 2, :], ptok_d[rows, C_CZ:C_CZ + GW]).then_inc(*s.by(16))

    def order(h):
        return 2 * (h % 2) + h // 2

    def level_time(t, k):
        return t + 0.24 + 0.085 * (k - 1)

    def pe_delta(pe):
        T = nc.tensor
        yield 0
        pe.wait_ge(*dn["g"](2))
        pe.wait_ge(*dn["zero"](1))
        for t in range(TT):
            yield t
            g = GTB[:, G_, t, :]
            if t:
                pe.wait_ge(*fin_d.og(t))
                pe.wait_ge(*fin_d.q(t))
            for m, name in enumerate(("upto", "later", "first", "second")):
                ins = T.matmul(PS[:, 0, 4 * m:4 * m + 4], K[name], g, start=True, stop=True)
            ins.then_inc(*dn["gm"].by(1))
            yield t + 0.02
            pe.wait_ge(*dn["ag"](t + 1))
            for h in range(GH):
                ins = T.matmul(PS[:, 1, order(h) * P:(order(h) + 1) * P], AG[:, h, :], K["upto"],
                               start=True, stop=True)
            ins.then_inc(*dn["dec"].by(1))
            yield t + 0.12
            pe.wait_ge(*dn["kk"](t + 1))
            for n, (slot, p) in enumerate(((K_HAT, 0), (K_HAT, 1), (K_B, 0), (Q_HAT, 0), (K_B, 1), (Q_HAT, 1),
                                           (Q_G, 0), (Q_G, 1))):
                ins = T.transpose(PS_T(2)[:, n, :], KK[:, slot, 2 * p:2 * p + 2, :].rearrange("p h d -> p (h d)"), ident)
            ins.then_inc(*dn["tr"].by(1))
            yield t + 0.16
            pe.wait_ge(*dn["trc"](t + 1))
            for h in range(GH):
                lo, p = 64 * (h % 2), h // 2
                ins = T.matmul(PS[:, 2 + h % 2, p * 256:(p + 1) * 256], TR[lo:lo + 64, p, :],
                               TR[lo:lo + 64, 2 + 2 * p:4 + 2 * p, :], start=True, stop=True)
            ins.then_inc(*dn["la"].by(1))
            n = 5 * t
            yield t + 0.22
            pe.wait_ge(*dn["ct"](6 * t + 1))
            for h in range(GH):
                ins = T.transpose(PS[:, 4, h * P:(h + 1) * P], CTM[:, 0, h, :], ident)
            ins.then_inc(*dn["c1"].by(1))
            for k in range(1, 6):
                yield level_time(t, k)
                pe.wait_ge(*dn["ct"](6 * t + k + 1))
                pe.wait_ge(*dn["v"](11 * t + 2 * k))
                for h in range(GH):
                    ins = T.matmul(PS[:, 4, h * P:(h + 1) * P], CTM[:, k % 2, h, :], VV[:, h, :], start=True, stop=True)
                ins.then_inc(*dn["p1"].by(1))
                yield level_time(t, k) + 0.04
                pe.wait_ge(*dn["p1c"](n + k))
                if k < 5:
                    for h in range(GH):
                        T.matmul(PS[:, 1, h * P:(h + 1) * P], VT[:, h, :], P1[:, h, :], start=True, stop=True)
                for h in range(GH):
                    ins = T.matmul(PS[:, 0, h * P:(h + 1) * P], P1[:, h, :], VT[:, h, :], start=True, stop=True)
                ins.then_inc(*dn["w"].by(1))
            yield t + 0.66
            pe.wait_ge(*dn["v"](11 * t + 11))
            for h in range(GH):
                T.matmul(PS[:, 1, h * GD:(h + 1) * GD], VT[:, order(h), :], KK[:, V_B, h, :], start=True, stop=True)
            for h in range(GH):
                lo, p = 64 * (h % 2), h // 2
                ins = T.matmul(PS[lo:lo + 64, 4, p * P:(p + 1) * P], KK[:, K_BG, h, :], VT[:, order(h), :],
                               start=True, stop=True)
            ins.then_inc(*dn["uw"].by(1))
            for c in range(2):
                yield t + 0.72 + 0.08 * c
                if c == 0:
                    pe.wait_ge(*dn["u"](2 * t + 2))
                r = slice(64 * c, 64 * c + 64)
                pe.wait_ge(*dn["s"](3 * (2 * t + c)))
                for h in range(GH):
                    lo, p = 64 * (h % 2), h // 2
                    ins = T.matmul(PS[r, 2 + h % 2, p * GD:(p + 1) * GD], WT[lo:lo + 64, p, r], SD[lo:lo + 64, p, :],
                                   start=True, stop=True)
                ins.then_inc(*dn["ws"].by(1))
                for h in range(GH):
                    lo, p = 64 * (h % 2), h // 2
                    ins = T.matmul(PS[r, h % 2, p * GD:(p + 1) * GD], TR[lo:lo + 64, 6 + p, r], SD[lo:lo + 64, p, :],
                                   start=True, stop=True)
                if c:
                    ins.then_inc(*fin_d.q_t.by(1))
                yield t + 0.76 + 0.08 * c
                pe.wait_ge(*dn["vn"](2 * t + c + 1))
                for p in range(2):
                    ins = T.matmul(PS[:, 2 + c, (2 + p) * P:(3 + p) * P],
                                   KK[r, K_D, 2 * p:2 * p + 2, :].rearrange("p h d -> p (h d)"),
                                   VN[r, 2 * p:2 * p + 2, :].rearrange("p h d -> p (h d)"), start=True, stop=True)
                ins.then_inc(*dn["ks"].by(1))
            yield t + 0.87
            for h in range(GH):
                ins = T.matmul(PS[:, 4, h * GD:(h + 1) * GD], AT[:, order(h), :], VN[:, h, :], start=True, stop=True)
            ins.then_inc(*fin_d.av.by(1))
            yield t + 0.95
            fin_d.pe_turn(pe, t, 1)

    def act_delta(act):
        yield 0
        act.wait_ge(*dn["par"](48))
        act.activation(ADT[:, 2, :], ADT[:, 0, :], ACT.Exp).then_inc(*dn["e1"].by(1))
        act.wait_ge(*dn["sp"](1))
        act.activation(GTB[:, 2], GTB[:, 1], ACT.Exp, scale=-1.0).then_inc(*dn["e1"].by(1))
        act.wait_ge(*dn["e1"](2))
        act.activation(GTB[:, 3], GTB[:, 2], ACT.Ln, bias=1.0).then_inc(*dn["e1"].by(1))
        act.activation(GTB[:, BETA], CAB[:, :, 4:8], ACT.Sigmoid).then_inc(*dn["g"].by(1))
        for t in range(TT):
            yield t + 0.005
            act.wait_ge(*dn[f"in{t % 2}"](32 * (t // 2 + 1)))
            fin_d.act_z(act, t, DZ[:, t % 2, :])
            yield t + 0.01
            act.wait_ge(*dn["gm"](t + 1))
            if t:
                act.wait_ge(*dn["s"](6 * t))
            act.activation(EX[:, :, :].rearrange("p m h -> p (m h)"), PS[:, 0, 0:16], ACT.Exp).then_inc(*dn["ex"].by(1))
            yield t + 0.04
            act.wait_ge(*dn["ss"](t + 1))
            act.activation(DRS[:, 1, :], DRS[:, 0, :], ACT.Sqrt).then_inc(*dn["rt"].by(1))
            yield t + 0.06
            act.wait_ge(*dn["dec"](t + 1))
            if t:
                act.wait_ge(*dn["lt"](2 * t))
            act.activation(DTU[:, :, :].rearrange("p h c -> p (h c)"), PS[:, 1, :], ACT.Exp).then_inc(*dn["dt"].by(1))
            yield t + 0.13
            act.wait_ge(*dn["tr"](t + 1))
            act.activation(TR[:, :, :], PS_T(2), ACT.Copy).then_inc(*dn["trc"].by(1))
            for k in range(1, 6):
                yield level_time(t, k) + 0.02
                act.wait_ge(*dn["p1"](5 * t + k))
                act.activation(P1[:, :, :].rearrange("p h c -> p (h c)"), PS[:, 4, :], ACT.Copy).then_inc(*dn["p1c"].by(1))
            yield t + 0.68
            act.wait_ge(*dn["uw"](t + 1))
            act.activation(WT[:, :, :].rearrange("p q c -> p (q c)"), PS[:, 4, 0:2 * P], ACT.Copy).then_inc(*dn["u"].by(1))
            act.activation(DU[:, :, :].rearrange("p h d -> p (h d)"), PS[:, 1, 0:GW], ACT.Copy).then_inc(*dn["u"].by(1))
            yield t + 0.86
            fin_d.act_q(act, t, 0)
            yield t + 0.92
            fin_d.act_root(act, t)
            yield t + 0.97
            fin_d.act_hi(act, t)

    def dve_delta(dve, chain):
        V = nc.vector
        MUL, ADD, SUB = ALU.mult, ALU.add, ALU.subtract
        yield 0
        dve.wait_ge(*dn["par"](48))
        V.memset(SD[:, :, :], 0.0).then_inc(*dn["zero"].by(1))
        chain(V.tensor_tensor(GTB[:, 0], CAB[:, :, 0:4], ADT[:, 1, :].unsqueeze(1).to_broadcast([P, TT, GH]), ADD))
        V.scalar_tensor_tensor(GTB[:, 1], GTB[:, 0], -1.0, GTB[:, 0], MUL, ALU.max).then_inc(*dn["sp"].by(1))
        dve.wait_ge(*dn["e1"](3))
        chain(V.scalar_tensor_tensor(GTB[:, 1], GTB[:, 0], 0.0, GTB[:, 3], ALU.max, ADD))
        chain(V.tensor_tensor(GTB[:, 0], GTB[:, 1], ADT[:, 2, :].unsqueeze(1).to_broadcast([P, TT, GH]), MUL))
        V.tensor_scalar(GTB[:, G_], GTB[:, 0], -1.0, None, MUL).then_inc(*dn["g"].by(1))
        dve.wait_ge(*dn["g"](2))
        dve.wait_ge(*dn["zero"](1))
        heads = lambda v: v.unsqueeze(2).to_broadcast([P, GH, GD])
        for t in range(TT):
            b = t % 2
            yield t
            if t:
                dve.wait_ge(*dn["dec"](t))
            V.tensor_tensor(AG[:, :, :], K["later"].unsqueeze(1).to_broadcast([P, 4, P]),
                            GTB[:, G_, t, :].unsqueeze(2).to_broadcast([P, 4, P]), MUL).then_inc(*dn["ag"].by(1))
            yield t + 0.03
            dve.wait_ge(*dn[f"in{b}"](32 * (t // 2 + 1)))
            qk = DQ[:, b, 0:2].rearrange("p a h d -> p (a h) d")
            sq = DTB[:, :, :].rearrange("p h c -> p (h c)").rearrange("p (h d) -> p h d", d=GD)
            chain(V.tensor_tensor(sq, qk, qk, MUL))
            chain(V.tensor_reduce(DRS[:, 2, :], sq, AX.X, ADD))
            V.tensor_scalar(DRS[:, 0, :], DRS[:, 2, :], EPS, None, ADD).then_inc(*dn["ss"].by(1))
            yield t + 0.05
            dve.wait_ge(*dn["rt"](t + 1))
            chain(V.reciprocal(DRS[:, 2, :], DRS[:, 1, :]))
            chain(V.tensor_scalar(DRS[:, 2, 0:4], DRS[:, 2, 0:4], GD ** -0.5, None, MUL))
            chain(V.tensor_tensor(KK[:, Q_HAT], DQ[:, b, 0], heads(DRS[:, 2, 0:4]), MUL))
            chain(V.tensor_tensor(KK[:, K_HAT], DQ[:, b, 1], heads(DRS[:, 2, 4:8]), MUL))
            chain(V.tensor_tensor(KK[:, K_B], KK[:, K_HAT], heads(GTB[:, BETA, t, :]), MUL))
            V.tensor_tensor(KK[:, V_B], DQ[:, b, 2], heads(GTB[:, BETA, t, :]), MUL).then_inc(*chain.s.by(1))
            chain.n += 1
            dve.wait_ge(*dn["ex"](t + 1))
            V.tensor_tensor(KK[:, Q_G], KK[:, Q_HAT], heads(EX[:, 0, :]), MUL).then_inc(*chain.s.by(1))
            V.tensor_tensor(KK[:, K_D], KK[:, K_HAT], heads(EX[:, 1, :]), MUL).then_inc(*chain.s.by(1))
            chain.n += 2
            dve.wait_ge(*chain.s(chain.n))
            V.tensor_tensor(KK[:, K_BG], KK[:, K_B], heads(EX[:, 0, :]), MUL).then_inc(*dn["kk"].by(1))
            for a in range(2):
                chain(V.tensor_copy(DECP[64 * a:64 * a + 64, :, :],
                                    EX[64 * a:64 * a + 64, 2:4, :].rearrange("p c (q a) -> p c q a", a=2)[:, :, :, a]))
            yield t + 0.15
            dve.wait_ge(*dn["dt"](t + 1))
            chain(V.tensor_tensor(DTB[:, :, :], DTU[:, :, :], K["before"].unsqueeze(1).to_broadcast([P, 4, P]), MUL))
            chain(V.tensor_tensor(DTU[:, :, :], DTU[:, :, :], K["upto"].unsqueeze(1).to_broadcast([P, 4, P]), MUL))
            yield t + 0.18
            dve.wait_ge(*dn["la"](t + 1))
            la = PS[:, 2:4, :].rearrange("p a (q m c) -> p a q m c", q=2, m=2)
            V.tensor_tensor(LT[:, :, :].rearrange("p (a q) c -> p a q c", a=2), la[:, :, :, 0, :],
                            DTB[:, :, :].rearrange("p (a q) c -> p a q c", a=2), MUL).then_inc(*dn["lt"].by(1))
            V.tensor_tensor(AT[:, :, :].rearrange("p (a q) c -> p a q c", a=2), la[:, :, :, 1, :],
                            DTU[:, :, :].rearrange("p (a q) c -> p a q c", a=2), MUL).then_inc(*dn["lt"].by(1))
            dve.wait_ge(*dn["lt"](2 * t + 2))

            def level(k):
                V.tensor_tensor(CTM[:, k % 2], LT[:, :, :],
                                K[f"join{LEVELS[k]}"].unsqueeze(1).to_broadcast([P, 4, P]), MUL).then_inc(*dn["ct"].by(1))

            level(0)
            level(1)
            eye = ident.unsqueeze(1).to_broadcast([P, 4, P])
            dve.wait_ge(*dn["ct"](6 * t + 1))
            V.tensor_tensor(VT[:, :, :], eye, CTM[:, 0], SUB).then_inc(*dn["v"].by(1))
            yield t + 0.23
            dve.wait_ge(*dn["c1"](t + 1))
            V.tensor_tensor(VV[:, :, :], eye, PS[:, 4, :].rearrange("p (h c) -> p h c", h=4), SUB).then_inc(*dn["v"].by(1))
            flat = lambda x: x[:, :, :].rearrange("p h c -> p (h c)")
            for k in range(1, 6):
                yield level_time(t, k) + 0.01
                if k < 5:
                    dve.wait_ge(*dn["v"](11 * t + 2 * k))
                    level(k + 1)
                yield level_time(t, k) + 0.05
                dve.wait_ge(*dn["w"](5 * t + k))
                if k < 5:
                    V.tensor_tensor(flat(VV), flat(VV), PS[:, 1, :], SUB).then_inc(*dn["v"].by(1))
                V.tensor_tensor(flat(VT), flat(VT), PS[:, 0, :], SUB).then_inc(*dn["v"].by(1))
            for c in range(2):
                r = slice(64 * c, 64 * c + 64)
                n = 2 * t + c
                yield t + 0.74 + 0.08 * c
                dve.wait_ge(*dn["u"](2 * t + 2))
                dve.wait_ge(*dn["ws"](n + 1))
                V.tensor_tensor(VN[r].rearrange("p (q a) d -> p a q d", a=2),
                                DU[r].rearrange("p (q a) d -> p a q d", a=2),
                                PS[r, 2:4, 0:P].rearrange("p a (q d) -> p a q d", q=2), SUB).then_inc(*dn["vn"].by(1))
                yield t + 0.77 + 0.08 * c
                dve.wait_ge(*dn["ks"](n + 1))
                V.tensor_tensor(SD[:, :, :], SD[:, :, :], DECP[:, c, :].unsqueeze(2).to_broadcast([P, 2, GD]), MUL)\
                    .then_inc(*dn["s"].by(1))
                dve.wait_ge(*dn["s"](3 * n + 1))
                for a in range(2):
                    h = slice(64 * a, 64 * a + 64)
                    V.tensor_tensor(SD[h], SD[h], PS[h, 2 + c, 2 * P:4 * P]
                                    .rearrange("p (q b d) -> p q b d", q=2, b=2)[:, :, a, :], ADD).then_inc(*dn["s"].by(1))
            yield t + 0.9
            yield from fin_d.dve_norm(dve, chain, t, 4, t + 0.93)
            yield t + 0.96
            fin_d.dve_gain(dve, t, 1)
            yield t + 0.98
            fin_d.dve_lo(dve, t)

    NGP = C_TOK - C_DG
    GP = at("GP", "whi", 0, [P, 2, NGP])
    GTT = at("GTT", "whi", 15488, [32, P])
    W2A = at("W2A", "wlo", 9728, [32, GW])
    LGA = at("LGA", "whi", 12416, [P, 3, GW])
    EE = at("EE", "whi", 8320, [P, 4, GW])
    ED = at("ED", "whi", 16000, [P, 2, 2])
    KG = at("KG", "wlo", 0, [P, 4, GW])
    TG = at("TG", "wlo", 4096, [P, 6, P])
    ATG = at("ATG", "wlo", 7168, [P, 4, P])
    SGS = at("SGS", "wlo", 9216, [P, 2, GD])
    fin_g = Finish("gl", "wlo", 10752, 6, GLW)
    gl = {n: sem(f"gl_{n}") for n in (
        "in0", "in1", "par", "zero", "gt", "gtc", "pre", "ab", "ex", "ln", "la", "cum", "ee", "kg", "tr", "trc",
        "a", "at", "s", "kv")}
    O_DQ, O_DK, O_DV, O_DZ = C_DQ - C_DG, C_DK - C_DG, C_DV - C_DG, C_DZ - C_DG
    RANK = 16

    GLA_LEAD = 0.6

    def sp_gla(sp):
        yield -1
        sp.wait_ge(*mm_done(gemms["pch"].end))
        sp.dma_start(W2A[0:RANK, :], I["gla_w_gate2_2"][0]).then_inc(*gl["par"].by(16))
        sp.dma_start(W2A[RANK:RANK + 1, :], I["gla_gate_bias_2"]).then_inc(*gl["par"].by(16))
        for t in range(TT):
            yield max(-1, t - GLA_LEAD - 0.4)
            if t >= 2:
                sp.wait_ge(*fin_g.av(t - 1))
                sp.wait_ge(*fin_g.zs(t - 1))
            sp.dma_start(GP[:, t % 2, :], ptok_d[t * P:(t + 1) * P, C_DG:C_TOK]).then_inc(*gl[f"in{t % 2}"].by(16))

    def pe_gla(pe):
        T = nc.tensor
        yield -0.9
        pe.wait_ge(*sg_hi(TT))
        pe.wait_ge(*gl["par"](32))
        pe.wait_ge(*gl["zero"](3))
        for t in range(TT):
            b = t % 2
            s = t - GLA_LEAD
            yield s + 0.05
            pe.wait_ge(*gl[f"in{b}"](16 * (t // 2 + 1)))
            if t:
                pe.wait_ge(*fin_g.og(t))
                pe.wait_ge(*fin_g.q(t))
                pe.wait_ge(*gl["s"](6 * t))
            T.transpose(PS[0:RANK, 5, 0:P], GP[:, b, 0:RANK], ident).then_inc(*gl["gt"].by(1))
            yield s + 0.08
            pe.wait_ge(*gl["gtc"](t + 1))
            T.matmul(PS[:, 5, P:P + GW], GTT[0:RANK + 1, :], W2A[0:RANK + 1, :], start=True, stop=True).then_inc(*gl["pre"].by(1))
            yield s + 0.17
            pe.wait_ge(*gl["la"](t + 1))
            la = LGA[:, 2, :]
            T.matmul(PS[:, 6, 0:GW], K["frommid"], la, start=True, stop=True)
            T.matmul(PS[:, 6, GW:2 * GW], K["upto"], la, start=True, stop=True)
            T.matmul(PS[:, 7, 0:GW], K["later"], la, start=True, stop=True)
            for c, name in enumerate(("first", "second")):
                for p in range(2):
                    ins = T.matmul(PS[:, 7, GW + 2 * c + p:GW + 2 * c + p + 1], la[:, p * P:(p + 1) * P],
                                   K[name][:, 0:1], start=True, stop=True)
            ins.then_inc(*gl["cum"].by(1))
            yield s + 0.3
            pe.wait_ge(*gl["kg"](t + 1))
            for n, (slot, p) in enumerate(((0, 0), (0, 1), (1, 0), (1, 1), (2, 0), (2, 1))):
                ins = T.transpose(PS_T(6)[:, n, :], KG[:, slot, p * P:(p + 1) * P], ident)
            ins.then_inc(*gl["tr"].by(1))
            yield s + 0.36
            pe.wait_ge(*gl["trc"](t + 1))
            for h in range(GH):
                lo, p = 64 * (h % 2), h // 2
                ins = T.matmul(PS[:, 6 + h % 2, p * P:(p + 1) * P], TG[lo:lo + 64, 2 + p, :], TG[lo:lo + 64, p, :],
                               start=True, stop=True)
            ins.then_inc(*gl["a"].by(1))
            for c in range(2):
                r = slice(64 * c, 64 * c + 64)
                for p in range(2):
                    ins = T.matmul(PS[:, 6 + c, (2 + p) * P:(3 + p) * P], KG[r, 3, p * P:(p + 1) * P],
                                   GP[r, b, O_DV + p * P:O_DV + (p + 1) * P], start=True, stop=True)
                ins.then_inc(*gl["kv"].by(1))
            for c in range(2):
                yield s + 0.45 + 0.05 * c
                r = slice(64 * c, 64 * c + 64)
                pe.wait_ge(*gl["at"](t + 1))
                pe.wait_ge(*gl["s"](3 * (2 * t + c)))
                for h in range(GH):
                    lo, p = 64 * (h % 2), h // 2
                    ins = T.matmul(PS[r, 6 + h % 2, p * GD:(p + 1) * GD], TG[lo:lo + 64, 4 + p, r], SGS[lo:lo + 64, p, :],
                                   start=True, stop=True)
                ins.then_inc(*(fin_g.q_t if c else gl["kv"]).by(1))
            yield s + 0.54
            for h in range(GH):
                ins = T.matmul(PS[:, 5, h * GD:(h + 1) * GD], ATG[:, order(h), :],
                               GP[:, b, O_DV + h * GD:O_DV + (h + 1) * GD], start=True, stop=True)
            ins.then_inc(*fin_g.av.by(1))
            yield s + 0.65
            fin_g.pe_turn(pe, t, 5)

    def act_gla(act):
        inv = 1.0 / 16.0
        for t in range(TT):
            b = t % 2
            s = t - GLA_LEAD
            yield s + 0.06
            act.wait_ge(*gl["gt"](t + 1))
            act.wait_ge(*gl["zero"](3))
            act.activation(GTT[0:RANK, :], PS[0:RANK, 5, 0:P], ACT.Copy).then_inc(*gl["gtc"].by(1))
            fin_g.act_z(act, t, GP[:, b, O_DZ:O_DZ + GW])
            yield s + 0.12
            act.wait_ge(*gl["ab"](t + 1))
            act.activation(LGA[:, 1, :], LGA[:, 0, :], ACT.Exp, scale=-1.0).then_inc(*gl["ex"].by(1))
            act.wait_ge(*gl["ex"](t + 1))
            act.activation(LGA[:, 0, :], LGA[:, 1, :], ACT.Ln, bias=1.0).then_inc(*gl["ln"].by(1))
            yield s + 0.2
            act.wait_ge(*gl["cum"](t + 1))
            act.activation(EE[:, 0:2, :].rearrange("p a n -> p (a n)"), PS[:, 6, :], ACT.Exp, scale=inv)\
               .then_inc(*gl["ee"].by(1))
            act.activation(EE[:, 2, :], PS[:, 6, 0:GW], ACT.Exp, scale=-inv).then_inc(*gl["ee"].by(1))
            act.activation(EE[:, 3, :], PS[:, 7, 0:GW], ACT.Exp, scale=inv).then_inc(*gl["ee"].by(1))
            act.activation(ED[:, :, :].rearrange("p a n -> p (a n)"), PS[:, 7, GW:GW + 4], ACT.Exp, scale=inv)\
               .then_inc(*gl["ee"].by(1))
            yield s + 0.33
            act.wait_ge(*gl["tr"](t + 1))
            act.activation(TG[:, :, :], PS_T(6)[:, 0:6, :], ACT.Copy).then_inc(*gl["trc"].by(1))
            yield s + 0.55
            act.wait_ge(*gl["s"](6 * t + 6))
            fin_g.act_q(act, t, 6)
            yield s + 0.6
            fin_g.act_root(act, t)
            yield s + 0.67
            fin_g.act_hi(act, t)

    def dve_gla(dve, chain):
        V = nc.vector
        MUL, ADD, SUB = ALU.mult, ALU.add, ALU.subtract
        yield -1
        dve.wait_ge(*mm_done(gemms["pch"].end))
        V.memset(GTT[:, :], 1.0).then_inc(*gl["zero"].by(1))
        V.memset(ATG[:, :, :], 0.0).then_inc(*gl["zero"].by(1))
        V.memset(SGS[:, :, :], 0.0).then_inc(*gl["zero"].by(1))
        dve.wait_ge(*gl["zero"](3))
        for t in range(TT):
            b = t % 2
            s = t - GLA_LEAD
            yield s + 0.1
            dve.wait_ge(*gl["pre"](t + 1))
            pre = PS[:, 5, P:P + GW]
            chain(V.tensor_copy(LGA[:, 1, :], pre))
            V.scalar_tensor_tensor(LGA[:, 0, :], LGA[:, 1, :], -1.0, LGA[:, 1, :], MUL, ALU.max).then_inc(*gl["ab"].by(1))
            yield s + 0.14
            dve.wait_ge(*gl["ln"](t + 1))
            V.scalar_tensor_tensor(LGA[:, 2, :], pre, 0.0, LGA[:, 0, :], ALU.min, SUB).then_inc(*gl["la"].by(1))
            yield s + 0.25
            dve.wait_ge(*gl["ee"](4 * t + 4))
            q, k = GP[:, b, O_DQ:O_DQ + GW], GP[:, b, O_DK:O_DK + GW]
            V.scalar_tensor_tensor(KG[:, 0, :], q, GD ** -0.5, EE[:, 0, :], MUL, MUL)
            V.scalar_tensor_tensor(KG[:, 2, :], q, GD ** -0.5, EE[:, 1, :], MUL, MUL)
            V.tensor_tensor(KG[:, 1, :], k, EE[:, 2, :], MUL)
            V.tensor_tensor(KG[:, 3, :], k, EE[:, 3, :], MUL).then_inc(*gl["kg"].by(1))
            yield s + 0.4
            dve.wait_ge(*gl["kv"](3 * t + 2))
            if t:
                dve.wait_ge(*fin_g.av(t))
            V.copy_predicated(ATG[:, :, :].rearrange("p (a q) c -> p a q c", a=2),
                              K["upto"].bitcast(I32).unsqueeze(1).unsqueeze(1).to_broadcast([P, 2, 2, P]),
                              PS[:, 6:8, 0:2 * P].rearrange("p a (q c) -> p a q c", q=2)).then_inc(*gl["at"].by(1))
            for c in range(2):
                n = 2 * t + c
                yield s + 0.48 + 0.05 * c
                if c == 0:
                    dve.wait_ge(*gl["kv"](3 * t + 3))
                else:
                    dve.wait_ge(*fin_g.q_t(t + 1))
                V.tensor_tensor(SGS[:, :, :], SGS[:, :, :], ED[:, c, :].unsqueeze(2).to_broadcast([P, 2, GD]), MUL)\
                    .then_inc(*gl["s"].by(1))
                dve.wait_ge(*gl["s"](3 * n + 1))
                for a in range(2):
                    h = slice(64 * a, 64 * a + 64)
                    V.tensor_tensor(SGS[h], SGS[h], PS[h, 6 + c, 2 * P:4 * P]
                                    .rearrange("p (q b d) -> p q b d", q=2, b=2)[:, :, a, :], ADD).then_inc(*gl["s"].by(1))
            yield s + 0.58
            yield from fin_g.dve_norm(dve, chain, t, 5, s + 0.61)
            yield s + 0.66
            fin_g.dve_gain(dve, t, 5)
            yield s + 0.68
            fin_g.dve_lo(dve, t)

    RAWD = at("RAWD", "stage", 0, [P, 2, D])
    GSB = at("GSB", "stage", 8192, [P, 2, HALF])
    AB = at("AB", "stage", 12288, [P, 2, HALF])
    flat2 = lambda ap: ap.rearrange("p k n -> p (k n)").rearrange("p (f n) -> p f n", f=2)
    WD_HI, WD_LO = flat2(W_HI[:, 1, 0:4, :]), flat2(W_LO[:, 1, 0:4, :])
    A_HI, A_LO = flat2(W_HI[:, 1, 4:8, :]), flat2(W_LO[:, 1, 4:8, :])
    ff_raw = [sem("ff_raw0"), sem("ff_raw1"), sem("ff_raw_down")]
    ff_whi, ff_split = sem("ff_whi"), sem("ff_split")
    ff_gu, ff_silu, ff_ab, ff_ahi, ff_alo, ff_dn, ff_x = (
        sem(n) for n in ("ff_gu", "ff_silu", "ff_ab", "ff_ahi", "ff_alo", "ff_dn", "ff_x"))
    wgu, wdn = I["w_gate_up_2"][0], I["w_down_2"][0]

    def sp_ffn(sp):
        sp.wait_ge(*w_split(len(halves)))

        def load(i, first):
            for half in range(2):
                if not first:
                    sp.wait_ge(*ff_split(3 * i + half - 2))
                for m in range(2):
                    src = wgu[half * HALF:(half + 1) * HALF, bass.ds(i * 256 + m * FF, 256)]
                    sp.dma_start(RAW[:, half, :, m * 256:(m + 1) * 256], src.rearrange("(k p) n -> p k n", p=P))\
                      .then_inc(*ff_raw[half].by(16))
            if not first:
                sp.wait_ge(*ff_split(3 * i))
            sp.dma_start(RAWD[:, :, :], wdn[bass.ds(i * 256, 256), :].rearrange("(k p) n -> p k n", p=P))\
              .then_inc(*ff_raw[2].by(16))

        load(0, True)
        with sp.Fori(1, FFB) as i:
            load(i, False)

    def pool_ffn(pool):
        G = nc.gpsimd
        pool.wait_ge(*mm_done(gemms["out2"].end))
        for i in range(FFB):
            def split(part, raw, hi, lo):
                G.tensor_scalar(hi, raw, 1.0, 1.0, ALU.mult, ALU.mult).then_inc(*ff_whi.by(1))
                pool.wait_ge(*ff_whi(3 * i + part + 1))
                G.tensor_tensor(lo, raw, hi.bitcast(F32), ALU.subtract).then_inc(*ff_split.by(1))

            if i:
                pool.wait_ge(*ff_gu(4 * i))
            for half in range(2):
                pool.wait_ge(*ff_raw[half](32 * i + 32))
                ks = slice(4 * half, 4 * half + 4)
                split(half, RAW[:, half], W_HI[:, 0, ks, :], W_LO[:, 0, ks, :])
            if i:
                pool.wait_ge(*ff_dn(16 * i))
            pool.wait_ge(*ff_raw[2](16 * i + 16))
            split(2, RAWD[:, :, :], WD_HI, WD_LO)

    def pe_ffn(pe):
        T = nc.tensor
        pe.wait_ge(*op_lo_done(turned_base(5) + TT))
        pe.wait_ge(*bank_dve(gemms["out2"].free1_dve))

        def turn(i, first=False):
            pe.wait_ge(*ff_split(3 * i + 2))
            for u in range(4):
                th, f = u // 2, u % 2
                if not (first and u < 2):
                    pe.wait_ge(*ff_ab(4 * i + u - 1))
                for m in range(2):
                    bank = 2 * (u % 2) + m
                    for n, (w, x) in enumerate(((W_HI, OP_HI), (W_LO, OP_HI), (W_HI, OP_LO))):
                        for k in range(KT):
                            ins = T.matmul(PS[:, bank, :], w[:, 0, k, m * 256 + f * P:m * 256 + (f + 1) * P],
                                           x[:, k, th * HALF:(th + 1) * HALF],
                                           start=n == 0 and k == 0, stop=n == 2 and k == KT - 1)
                ins.then_inc(*ff_gu.by(1))
            pe.wait_ge(*ff_split(3 * i + 3))
            for v in range(16):
                t, c = v // 2, v % 2
                if v == 0:
                    pe.wait_ge(*ff_alo(4 * i + 2))
                if v == 8:
                    pe.wait_ge(*ff_alo(4 * i + 4))
                if not (first and v < 4):
                    pe.wait_ge(*ff_x(16 * i + v - 3))
                for n, (a, w) in enumerate(((A_HI, WD_HI), (A_HI, WD_LO), (A_LO, WD_HI))):
                    for f in range(2):
                        ins = T.matmul(PS[:, 4 + v % 4, :], a[:, f, t * P:(t + 1) * P],
                                       w[:, f, c * HALF:(c + 1) * HALF], start=n == 0 and f == 0,
                                       stop=n == 2 and f == 1)
                ins.then_inc(*ff_dn.by(1))

        turn(0, first=True)
        with pe.Fori(1, FFB) as i:
            turn(i)

    def act_ffn(act):
        def turn(i, first=False):
            for u in range(4):
                th, f = u // 2, u % 2
                act.wait_ge(*ff_gu(4 * i + u + 1))
                act.activation(GSB[:, u % 2, :], PS[:, 2 * (u % 2), :], ACT.Silu).then_inc(*ff_silu.by(1))
                act.wait_ge(*ff_ab(4 * i + u + 1))
                if u == 0 and not first:
                    act.wait_ge(*ff_dn(16 * i))
                act.activation(A_HI[:, f, th * HALF:(th + 1) * HALF], AB[:, u % 2, :], ACT.Copy).then_inc(*ff_ahi.by(1))

        turn(0, first=True)
        with act.Fori(1, FFB) as i:
            turn(i)

    def dve_ffn(dve):
        V = nc.vector
        with dve.Fori(0, FFB) as i:
            for u in range(4):
                th, f = u // 2, u % 2
                dve.wait_ge(*ff_silu(4 * i + u + 1))
                V.tensor_tensor(AB[:, u % 2, :], PS[:, 2 * (u % 2) + 1, :], GSB[:, u % 2, :], ALU.mult)\
                    .then_inc(*ff_ab.by(1))
                dve.wait_ge(*ff_ahi(4 * i + u + 1))
                V.tensor_tensor(A_LO[:, f, th * HALF:(th + 1) * HALF], AB[:, u % 2, :],
                                A_HI[:, f, th * HALF:(th + 1) * HALF].bitcast(F32), ALU.subtract).then_inc(*ff_alo.by(1))
            for v in range(16):
                t, c = v // 2, v % 2
                dve.wait_ge(*ff_dn(16 * i + v + 1))
                V.tensor_tensor(X[:, t, c * HALF:(c + 1) * HALF], X[:, t, c * HALF:(c + 1) * HALF],
                                PS[:, 4 + v % 4, :], ALU.add).then_inc(*ff_x.by(1))

    done = lambda name: (mm_done, gemms[name].end)
    tok_to = lambda dram_: (lambda b, a, h, w: dram_[a * P:(a + 1) * P, b * HALF:b * HALF + w])
    ch_to = lambda dram_: (lambda b, a, h, w: dram_[(4 * b + a) * P:(4 * b + a + 1) * P, h * HALF:h * HALF + w])
    x_view, mem_view = rows_of(I["x"][0]), rows_of(I["mem"][0])

    with nc.Block() as block:
        @block.sync
        def _(sp):
            sp_s5_tables(sp)
            sp_columns(sp)
            sp.wait_ge(*s5_out(S5_STORES))
            sp.wait_ge(*s5_dd(1))
            sp_gain(sp, 0)
            sp.dma_start(X[:, 0:2, :], mem_view).then_inc(*x_in.by(16))
            sp_weights(sp, weights_before("xk"))
            sp_gain(sp, 1, ready=[(xn_full, 2)])
            sp.dma_start(X[:, :, :], x_view).then_inc(*x_in.by(16))
            sp_weights(sp, weights_before("qk"))
            sp_s5_in(sp)
            sp_weights(sp, weights_before("glu"))
            sp_s5_y(sp)
            wait_stores(sp, "gs5")
            for s in s5y_outs:
                sp.wait_ge(*s(64))
            sp_load_operand(sp, 0, yt_d)
            sp_weights(sp, weights_before("out_ret"))
            sp_retention(sp)
            sp.wait_ge(*r_lo(TT))
            sp.dma_start(X[:, :, :], x_view).then_inc(*x_in.by(16))
            sp_weights(sp, weights_before("out_s5"))
            sp_load_operand(sp, 1, st_d, gate=gs5_d)
            sp_gain(sp, 2)
            sp_weights(sp, weights_before("xq"))
            sp.wait_ge(*bank_dve(gemms["out_s5"].free1_dve))
            sp.wait_ge(*xn_full(turned_base(2) + TT))
            sp.dma_start(rows_of(x1_d), X[:, :, :]).then_inc(*x_out.by(16))
            sp_gain(sp, 3)
            sp_weights(sp, weights_before("xo"))
            sp.wait_ge(*x_out(16))
            wait_stores(sp, "xq")
            sp_attention(sp)
            sp.wait_ge(*xa_lo(TT))
            sp.dma_start(X[:, :, :], rows_of(x1_d)).then_inc(*x_in.by(16))
            sp_weights(sp, weights_before("ptok"))
            sp.wait_ge(*inplace(TT))
            sp_gain(sp, 4)
            sp.dma_start(rows_of(x2_d), X[:, :, :]).then_inc(*x_out.by(16))
            sp_weights(sp, 2 * gemms["pch"].first_block + 4)
            together(sp_weights_steps(sp, len(halves), gemms["pch"].first_block), sp_sgu(sp))
            together(sp_conv(sp), sp_delta(sp), sp_gla(sp))
            sp.wait_ge(*fin_d.lo(TT))
            sp.dma_start(X[:, :, :], rows_of(x2_d)).then_inc(*x_in.by(16))
            sp_gain(sp, 5)
            sp_ffn(sp)
            sp.wait_ge(*xn_full(turned_base(5) + TT))
            sp_gain(sp, 6)
            sp.wait_ge(*inplace(2 * TT))
            sp.dma_start(out[0].rearrange("(t p) d -> p t d", p=P), X[:, :, :]).then_inc(*x_out.by(16))
            sp.wait_ge(*x_out(48))

        @block.gpsimd
        def _(pool):
            pool_s5_tables(pool, None)
            pool.wait_ge(*s5_out(S5_STORES))
            pool_split_all(pool)
            pool_ffn(pool)

        @block.scalar
        def _(act):
            act_s5_tables(act)
            act_norm_stats(act, 0, ready=[(x_in, 16)], tiles=2)
            act_norm_hi(act, 0, free=[(s5_out, S5_STORES)], tiles=2)
            act_norm_stats(act, 1, ready=[(x_in, 32)])
            act_gemm_store(act, "xk", lambda b, a, h, w: ka_d[(4 * b + a) * P:(4 * b + a + 1) * P, :])
            act_gemm_store(act, "xv", tok_to(va_d))
            act_norm_hi(act, 1, free=[done("xv")])
            act_gemm_store(act, "u", tok_to(u_d))
            wait_stores(act, "u")
            act_s5_in(act)
            act_gemm_store(act, "qk", tok_to(qk_d))
            act_gemm_store(act, "v", tok_to(v_d))
            act_gemm_store(act, "gret", ch_to(gret_d), func=ACT.Silu)
            act_gemm_store(act, "gs5", ch_to(gs5_d), func=ACT.Silu)
            act_s5_y(act)
            act_load_operand(act, 0, False)
            act_glu(act)
            act.wait_ge(*glu_z(16))
            act_retention(act)
            act.wait_ge(*mm_done(gemms["out_ret"].end))
            act_load_operand(act, 1, True)
            act_norm_stats(act, 2, ready=[(bank_dve, gemms["out_s5"].free1_dve)])
            act_norm_hi(act, 2, free=[done("out_s5")])
            act_gemm_store(act, "xq", ch_to(qa_d))
            act_attention(act)
            act_norm_stats(act, 3, ready=[(bank_dve, gemms["xo"].free1_dve)])
            act_norm_stats(act, 4, ready=[(inplace, TT)])
            act_norm_hi(act, 4, free=[done("xo")])
            act_gemm_store(act, "ptok", lambda b, a, h, w: ptok_d[a * P:(a + 1) * P, PTOK0[b]:PTOK0[b] + w])
            together(act_gemm_store_steps(act, "pch", ch_to(pch_d)), act_sgu(act))
            together(act_conv(act), act_delta(act), act_gla(act))
            act_norm_stats(act, 5, ready=[(bank_dve, gemms["out2"].free1_dve)])
            act_norm_hi(act, 5, free=[done("out2")])
            act_ffn(act)
            act_norm_stats(act, 6, ready=[(ff_x, 16 * FFB)])

        @block.vector
        def _(dve):
            chain = Chain(dve, sem("dve_chain"))
            dve_s5_tables(dve, chain)
            dve_norm_split(dve, 0, chain, tiles=2)
            dve_norm_split(dve, 1, chain)
            dve_s5_in(dve)
            dve_s5_scan(dve)
            dve_s5_y(dve)
            dve_load_operand(dve, 0, False)
            dve_glu(dve)
            dve.wait_ge(*pc_in(PC_LOADED))
            dve_retention(dve, chain)
            dve.wait_ge(*x_in(48))
            dve_gemm_add(dve, "out_ret")
            dve_load_operand(dve, 1, True)
            dve_gemm_add(dve, "out_s5")
            dve_norm_split(dve, 2, chain)
            dve_attention(dve, chain)
            dve.wait_ge(*x_in(64))
            dve_gemm_add(dve, "xo")
            dve_norm_inplace(dve, 3, chain)
            dve_norm_split(dve, 4, chain)
            dve.wait_ge(*x_out(32))
            dve.wait_ge(*pc_in(PC_LOADED))
            alone(dve_sgu(dve, chain))
            together(dve_conv(dve, chain), dve_delta(dve, chain), dve_gla(dve, chain))
            dve.wait_ge(*x_in(80))
            dve_gemm_add(dve, "out2")
            dve_norm_split(dve, 5, chain)
            dve_ffn(dve)
            dve_norm_inplace(dve, 6, chain)

        @block.tensor
        def _(pe):
            pe_s5_tables(pe)
            pe_norm(pe, 0, tiles=2)
            pe_gemm(pe, "xk", ready=[(op_lo_done, 2)])
            pe_gemm(pe, "xv")
            pe_norm(pe, 1)
            pe_gemm(pe, "u", ready=[(op_lo_done, turned_base(1) + TT)])
            pe_s5_in(pe)
            pe_gemm(pe, "qk")
            pe_gemm(pe, "v")
            pe_gemm(pe, "gret")
            pe_gemm(pe, "gs5")
            pe_s5_y(pe)
            pe_gemm(pe, "glu", ready=[(la_lo, KT)])
            pe_retention(pe)
            pe_gemm(pe, "out_ret", ready=[(r_lo, TT)])
            pe_gemm(pe, "out_s5", ready=[(la_lo, 2 * KT)])
            pe_norm(pe, 2)
            pe_gemm(pe, "xq", ready=[(op_lo_done, turned_base(2) + TT)])
            pe_attention(pe)
            pe_gemm(pe, "xo", ready=[(xa_lo, TT)])
            pe_norm(pe, 4)
            pe_gemm(pe, "ptok", ready=[(op_lo_done, turned_base(4) + TT)])
            together(pe_gemm_steps(pe, "pch"), pe_sgu(pe))
            pe.wait_ge(*bank_act(gemms["pch"].free1_act))
            together(pe_conv(pe), pe_delta(pe), pe_gla(pe))
            pe_gemm(pe, "out2", ready=[(fin_d.lo, TT), (fin_g.lo, TT)])
            pe_norm(pe, 5)
            pe_ffn(pe)

    for before, total in SHARED.values():
        assert sems[before].count == total, (before, sems[before].count, total)


INPUTS = [
    "x", "mem", "positions", "norm1_g", "w_in", "ret_gn_g", "s5_a_re", "s5_a_im", "s5_log_dt", "s5_b_re",
    "s5_b_im", "s5_c_re", "s5_c_im", "s5_d", "s5_glu_w", "s5_glu_b", "w_out", "norm2_g", "norm_mem_g", "xa_wq",
    "xa_wk", "xa_wv", "xa_wo", "norm_f_g", "norm1_w_2", "w_in_2", "sgu_ln_w_2", "sgu_ln_b_2",
    "sgu_w_spatial_2", "sgu_b_spatial_2", "sc_conv_w_2", "dn_conv_w_2", "dn_a_log_2", "dn_dt_bias_2",
    "dn_norm_w_2", "gla_w_gate2_2", "gla_gate_bias_2", "gla_norm_w_2", "w_out_2", "norm2_w_2",
    "w_gate_up_2", "w_down_2", "final_norm_w_2",
]


def kernel(**inputs):
    import concourse.bacc as bacc
    from concourse.bass_utils import run_bass_kernel_spmd

    nc = bacc.Bacc("TRN2", target_bir_lowering=False, num_devices=1)
    arrays = {name: np.ascontiguousarray(inputs[name]) for name in INPUTS}
    base, _, ret, place = shape_constants()
    arrays["c_base"], arrays["c_ret"], arrays["c_place"] = base, ret, place
    I = {n: nc.dram_tensor(f"in_{n}", a.shape, mybir.dt.from_np(a.dtype), kind="ExternalInput").ap()
         for n, a in arrays.items()}
    out = nc.dram_tensor("out", (1, L, D), F32, kind="ExternalOutput").ap()
    build(nc, I, out)
    r = run_bass_kernel_spmd(nc, [{f"in_{n}": a for n, a in arrays.items()}], core_ids=[0])
    return r.results[0]["out"]
```

```python
import math
from contextlib import ExitStack

import numpy as np

import concourse.bass as bass
from concourse import mybir

F32 = mybir.dt.float32
F32R = mybir.dt.float32r
I32 = mybir.dt.int32
ALU = mybir.AluOpType
ACT = mybir.ActivationFunctionType
AX = mybir.AxisListType

P = 128
D = 1024
L = 1024
TT = L // P
KT = D // P
MEM = 256
EPS = 1e-6
HALF = 512

RH, RDK, RDV = 8, 64, 128
SG, SP_, SN = 64, 16, 64
SC = 8
NCH = L // SC
PAIRS = SG // 2
XH, XD = 4, 256
GW, GH, GD = 256, 4, 64
FF = 2816
FFB = FF // 256

TWO_PI = 2 * math.pi
PI_A = 6.28125
PI_B = 0.0019350051879882812
PI_C = TWO_PI - PI_A - PI_B
ROUND = 12582912.0
PI_SAFE = 3.1415925

C_AU, C_AV, C_CA, C_CB, C_CZ, C_DG, C_DQ, C_DK, C_DV, C_DZ, C_TOK = (
    0, 256, 512, 516, 520, 776, 792, 1048, 1304, 1560, 1816)


PTOK0 = (C_AU, C_CA, C_DQ, C_DV)


SHARED = {}
for later, earlier, total in (e.split() for e in (
        "gt s5b_t 16, pre s5b_mm 16, cum s5y_t 8, tr s5y_mm 8, a s5y_tt 8, kv s5_bt_t 16, q_t sg_mm 8, av sg_t 8,"
        "turn s5_r 1, gtc s5b_ut 16, ex s5y_ut 8, ln s5y_yo 8, ee s5_bt 16, trc s5_cp 8, q sg_gl 8, zs sg_root 8,"
        "root sg_hi 9, hi s5_act 4, zero s5_prm 1, ab s5b_s 16, la s5b_ur 16, kg s5y_ur 8, at s5y_ys 16, s s5_xpw 16,"
        "ms sg_var 8, on sg_vn 8, og sg_y 16, lo s5_small 4, in0 s5y_in0 192, in1 s5y_in1 192,"
        "par s5b_in 128").split(",")):
    SHARED["gl_" + later] = (earlier, int(total))
for later, earlier, total in (e.split() for e in (
        "gm r_turn 8, dec r_sc 8, tr r_o 8, la r_kv 8, c1 r_back 8, ex r_qkt 8, rt r_root 8, trc r_hi 8, e1 r_trig 2,"
        "ag r_scr 8, ss r_var 8, kk r_on 8, s r_rst 25, lt r_g 16, ct r_ang 1, in0 rq_in 128, in1 rv_in 128,"
        "par rc_in 32").split(",")):
    SHARED["dn_" + later] = (earlier, int(total))
for later, earlier, total in (e.split() for e in (
        "sg_w xa_s 8, sg_mm xa_t 8, sg_t xa_o 8, sg_gl xa_pt 8, sg_root xa_hi 8, sg_hi xa_e 32, sg_wt xa_nm 8,"
        "sg_var xa_p 8, sg_vn xa_lo 8, sg_y r_ab 16, sg_lo r_rot 8, su_in0 xa_q0 64, su_in1 xa_q1 64,"
        "sg_in xa_kv 32").split(",")):
    SHARED[later] = (earlier, int(total))


def shape_constants():
    i = np.arange(P)
    row, col = i[:, None], i[None, :]
    same = (row // 64) == (col // 64)
    f = np.float32
    tabs = {"ident": np.eye(P, dtype=f)}
    tabs["upto"] = (same & (row <= col)).astype(f)
    tabs["later"] = (same & (row > col)).astype(f)
    tabs["before"] = (same & (row < col)).astype(f)
    tabs["frommid"] = tabs["upto"] - (same & (row % 64 <= 32)).astype(f)
    tabs["first"] = np.broadcast_to(row < 64, (P, P)).astype(f)
    tabs["second"] = np.broadcast_to(row >= 64, (P, P)).astype(f)
    tabs["causal"] = (row <= col).astype(f)
    for b in (1, 2, 4, 8, 16, 32):
        m = ((row // (2 * b)) == (col // (2 * b))) & (col % (2 * b) >= b) & (row % (2 * b) < b)
        tabs[f"join{b}"] = m.astype(f)
    base = np.concatenate([tabs[k] for k in tabs], axis=1)
    names = list(tabs)
    gam = 1.0 - 2.0 ** (-5.0 - np.arange(RH))
    mask = np.where(row <= col, 1.0, 0.0)
    by_parity = np.r_[0:RH:2, 1:RH:2]
    rmask = mask[:, None, :] * (gam ** -128.0)[by_parity][None, :, None]
    qw = gam[None, :] ** (i[:, None] + 1.0)
    kw = gam[None, :] ** (127.0 - i[:, None]) * RDK ** -0.5
    dec = np.empty((P, RH // 2))
    dec[:64] = gam[0::2] ** 128.0
    dec[64:] = gam[1::2] ** 128.0
    inv = (np.float32(10000.0) ** (-np.arange(32, dtype=f) / f(32))).astype(f)
    inv = np.broadcast_to(inv[None, :], (P, 32))
    ret = np.concatenate([rmask.reshape(P, -1), qw, kw, dec, inv], axis=1).astype(f)
    place = np.zeros((SP_, P + SP_), f)
    place[np.arange(SP_), P - SP_ + np.arange(SP_)] = 1.0
    place[np.arange(SP_), P + np.arange(SP_)] = 1.0
    return base.astype(f), names, ret, place


def build(nc, I, out):
    dram = {}

    def scratch(name, shape):
        dram[name] = nc.dram_tensor(name, shape, F32, kind="Internal").ap()
        return dram[name]

    qk_d = scratch("qk_d", (L, D))
    v_d = scratch("v_d", (L, D))
    u_d = scratch("u_d", (L, D))
    gret_d = scratch("gret_d", (D, L))
    gs5_d = scratch("gs5_d", (D, L))
    bct_d = scratch("bct_d", (P, PAIRS, 2, P))
    toep_d = scratch("toep_d", (P, SC, SG * SP_))
    cc_d = scratch("cc_d", (P, PAIRS, 2, P))
    st_d = scratch("st_d", (D, L))
    qa_d = scratch("qa_d", (D, L))
    x1_d = scratch("x1_d", (L, D))
    x2_d = scratch("x2_d", (L, D))
    ptok_d = scratch("ptok_d", (L, C_TOK))
    pch_d = scratch("pch_d", (1536, L))
    ka_d = scratch("ka_d", (D, MEM))
    va_d = scratch("va_d", (MEM, D))

    ctx = ExitStack()
    ctx.enter_context(nc.allow_non_contiguous_dma(reason="small parameters, once"))
    where = {}
    top = [16640]

    def region(name, size):
        where[name] = top[0]
        top[0] += size

    for name, size in (("const", 7168), ("small", 3072), ("x", 33024), ("ophi", 32768), ("oplo", 32768),
                       ("whi", 32768), ("wlo", 32768), ("raw", 16384), ("stage", 20480)):
        region(name, size)
    assert top[0] <= 229344, top[0]
    used = {}

    def at(name, reg, off, shape, dt=F32):
        size = int(np.prod(shape[1:])) * 4
        limit = {"const": 7168, "small": 3072, "x": 33024, "ophi": 32768, "oplo": 32768, "whi": 32768,
                 "wlo": 32768, "raw": 16384, "stage": 20480}[reg]
        assert off + size <= limit, (name, off, size, limit)
        return nc.alloc_sbuf_tensor_at(name, list(shape), dt, offset=where[reg] + off)

    class Signal:
        def __init__(self, hw, base):
            self.hw, self.base, self.count = hw, base, 0

        def __call__(self, value):
            return self.hw, self.base + value

        def by(self, n):
            self.count += n
            return self.hw, n

    sems = {}

    def sem(name):
        if name not in sems:
            if name in SHARED:
                before, total = SHARED[name]
                earlier = sem(before)
                sems[name] = Signal(earlier.hw, earlier.base + total)
            else:
                sems[name] = Signal(ctx.enter_context(nc.semaphore(name)), 0)
        return sems[name]

    PS = ctx.enter_context(nc.psum_tensor("PS", [P, 8, HALF], F32))
    _, names, _, _ = shape_constants()
    CONST = at("CONST", "const", 0, [P, len(names) * P])
    K = {n: CONST[:, j * P:(j + 1) * P] for j, n in enumerate(names)}
    ident = K["ident"]
    X = at("X", "x", 0, [P, TT, D])
    OP_HI = at("OP_HI", "ophi", 0, [P, KT, L], F32R)
    OP_LO = at("OP_LO", "oplo", 0, [P, KT, L], F32R)
    W_HI = at("W_HI", "whi", 0, [P, 2, KT, HALF], F32R)
    W_LO = at("W_LO", "wlo", 0, [P, 2, KT, HALF], F32R)
    RAW = at("RAW", "raw", 0, [P, 2, 4, HALF])
    OST = at("OST", "stage", 0, [P, 4, HALF])
    XN = at("XN", "stage", 8192, [P, 2, D])
    GROW = at("GROW", "stage", 16384, [P, D])
    st = at("st", "small", 0, [P, 64])
    bcol = at("bcol", "small", 256, [P, 16])
    halfpi = at("halfpi", "small", 512, [P, 1])

    def together(*stages):
        nexts = [[next(s), n, s] for n, s in enumerate(stages)]
        while nexts:
            first = min(nexts, key=lambda x: (x[0], x[1]))
            first[0] = next(first[2], None)
            if first[0] is None:
                nexts.remove(first)

    def one_after_other(first, units, second):
        yield from first
        for time in second:
            yield units + time

    def first_part(stage):
        next(stage)
        next(stage)

    def alone(stage):
        for _ in stage:
            pass

    class Chain:
        def __init__(self, eng, s):
            self.eng, self.s, self.n = eng, s, 0

        def __call__(self, ins):
            ins.then_inc(*self.s.by(1))
            self.n += 1
            self.eng.wait_ge(*self.s(self.n))
    class Gemm:
        pass

    gemms, blocks, halves = {}, [], []
    raw_total = [0, 0]
    count = [0]

    def add_gemm(name, weight, col_blocks, major, tiles, row0=0, engine="act"):
        g = Gemm()
        g.name, g.major, g.tiles, g.engine = name, major, tiles, engine
        g.first_block, g.first = len(blocks), count[0]
        g.units = []
        g.cols = col_blocks
        for segs in col_blocks:
            b = len(blocks)
            width = sum(n for _, n in segs)
            if major == "tok":
                units = [(b, t, 0, width) for t in range(tiles)]
            else:
                step = min(HALF, tiles)
                units = [(b, c, h, step) for c in range(width // P) for h in range(tiles // step)]
            g.units += units
            count[0] += len(units)
            blocks.append((width, count[0]))
            for half in range(2):
                r = len(halves)
                raw_total[r % 2] += 16 * len(segs)
                halves.append((weight, row0 + half * HALF, segs, b, half, raw_total[r % 2], width))
        g.end = count[0]
        gemms[name] = g

    def cols(a, b):
        return [[(c, min(HALF, b - c))] for c in range(a, b, HALF)]

    w_in, w_out = I["w_in"][0], I["w_out"][0]
    add_gemm("xk", I["xa_wk"][0], cols(0, D), "ch", MEM)
    add_gemm("xv", I["xa_wv"][0], cols(0, D), "tok", MEM // P)
    add_gemm("u", w_in, cols(3072, 4096), "tok", TT)
    add_gemm("qk", w_in, cols(0, 1024), "tok", TT)
    add_gemm("v", w_in, cols(1024, 2048), "tok", TT)
    add_gemm("gret", w_in, cols(2048, 3072), "ch", L)
    add_gemm("gs5", w_in, cols(4096, 5120), "ch", L)
    add_gemm("glu", I["s5_glu_w"][0], cols(0, D), "ch", L)
    add_gemm("out_ret", w_out, cols(0, D), "tok", TT, row0=0, engine="dve")
    add_gemm("out_s5", w_out, cols(0, D), "tok", TT, row0=D, engine="dve")
    add_gemm("xq", I["xa_wq"][0], cols(0, D), "ch", L)
    add_gemm("xo", I["xa_wo"][0], cols(0, D), "tok", TT, engine="dve")
    w_in2 = I["w_in_2"][0]
    add_gemm("ptok", w_in2, [[(0, 512)], [(2048, 264), (3080, 16)], [(2312, 512)], [(2824, 256), (3096, 256)]],
             "tok", TT)
    add_gemm("pch", w_in2, cols(512, 2048), "ch", L)
    add_gemm("out2", I["w_out_2"][0], cols(0, D), "tok", TT, engine="dve")

    raw_in = [sem("raw_in0"), sem("raw_in1")]
    w_split = sem("w_split")
    w_hi = sem("w_hi")
    mm_done = sem("mm_done")
    bank_act = sem("bank_act")
    bank_dve = sem("bank_dve")
    ost_out = [sem(f"ost_out{i}") for i in range(4)]

    act_total, dve_total = [0], [0]
    for g in gemms.values():
        g.free0_act, g.free0_dve = act_total[0], dve_total[0]
        (act_total if g.engine == "act" else dve_total)[0] += len(g.units)
        g.free1_act, g.free1_dve = act_total[0], dve_total[0]

    issued = [0]

    def sp_weights(sp, upto):
        alone(sp_weights_steps(sp, upto, 0))

    def sp_weights_steps(sp, upto, block0):
        while issued[0] < min(upto, len(halves)):
            r = issued[0]
            yield 8 * (halves[r][3] - block0 - 2) + 0.05
            weight, row, segs, _, _, _, _ = halves[r]
            if r >= 2:
                sp.wait_ge(*w_split(r - 1))
            c = 0
            for c0, n in segs:
                sp.dma_start(RAW[:, r % 2, :, c:c + n],
                             weight[row:row + HALF, c0:c0 + n].rearrange("(k p) n -> p k n", p=P))\
                  .then_inc(*raw_in[r % 2].by(16))
                c += n
            issued[0] += 1

    def weights_before(name):
        return 2 * gemms[name].first_block + 6

    FIRST_HALVES = 8

    def dve_split_first(dve):
        for r in range(FIRST_HALVES):
            b, half, width = halves[r][3], halves[r][4], halves[r][6]
            ks = slice(4 * half, 4 * half + 4)
            dve.wait_ge(*w_hi(r + 1))
            nc.vector.tensor_tensor(W_LO[:, b % 2, ks, 0:width], RAW[:, r % 2, :, 0:width],
                                    W_HI[:, b % 2, ks, 0:width].bitcast(F32), ALU.subtract)\
                .then_inc(*w_split.by(1))

    def pool_split_all(pool):
        for r, (_, _, _, b, half, arrived, width) in enumerate(halves):
            pool.wait_ge(*raw_in[r % 2](arrived))
            if b >= 2 and half == 0:
                pool.wait_ge(*mm_done(blocks[b - 2][1]))
            if b == gemms["out2"].first_block + 1 and half == 0:
                pool.wait_ge(*fin_g.lo(TT))
            raw = RAW[:, r % 2, :, 0:width]
            hi = W_HI[:, b % 2, 4 * half:4 * half + 4, 0:width]
            nc.gpsimd.tensor_scalar(hi, raw, 1.0, 1.0, ALU.mult, ALU.mult).then_inc(*w_hi.by(1))
            if r < FIRST_HALVES:
                continue
            if r == FIRST_HALVES:
                pool.wait_ge(*w_split(FIRST_HALVES))
            pool.wait_ge(*w_hi(r + 1))
            nc.gpsimd.tensor_tensor(W_LO[:, b % 2, 4 * half:4 * half + 4, 0:width], raw, hi.bitcast(F32),
                                    ALU.subtract).then_inc(*w_split.by(1))

    def pe_gemm(pe, name, ready=()):
        alone(pe_gemm_steps(pe, name, ready))

    def pe_gemm_steps(pe, name, ready=()):
        g = gemms[name]
        for s, v in ready:
            pe.wait_ge(*s(v))
        if g.engine == "act" and g.free0_dve:
            pe.wait_ge(*bank_dve(g.free0_dve))
        if g.engine == "dve" and g.free0_act:
            pe.wait_ge(*bank_act(g.free0_act))
        mine, base = (bank_act, g.free0_act) if g.engine == "act" else (bank_dve, g.free0_dve)
        last = -1
        for n, (b, a, h, width) in enumerate(g.units):
            yield n
            if b != last:
                pe.wait_ge(*w_split(2 * b + 2))
                last = b
            if base + n - 3 > 0:
                pe.wait_ge(*mine(base + n - 3))
            bank = (g.first + n) % 4
            slot = b % 2
            for i, (act_part, w_part) in enumerate(((OP_HI, W_HI), (OP_HI, W_LO), (OP_LO, W_HI))):
                for k in range(KT):
                    start, stop = i == 0 and k == 0, i == 2 and k == KT - 1
                    if g.major == "tok":
                        ins = nc.tensor.matmul(PS[:, bank, 0:width], act_part[:, k, a * P:(a + 1) * P],
                                               w_part[:, slot, k, 0:width], start=start, stop=stop)
                    else:
                        ins = nc.tensor.matmul(PS[:, bank, 0:width], w_part[:, slot, k, a * P:(a + 1) * P],
                                               act_part[:, k, h * HALF:h * HALF + width], start=start, stop=stop)
            ins.then_inc(*mm_done.by(1))

    stores = [0]

    def act_gemm_store(act, name, dst, func=ACT.Copy):
        alone(act_gemm_store_steps(act, name, dst, func))

    def act_gemm_store_steps(act, name, dst, func=ACT.Copy):
        g = gemms[name]
        for n, (b, a, h, width) in enumerate(g.units):
            yield n + 0.9
            s = stores[0]
            act.wait_ge(*mm_done(g.first + n + 1))
            if s >= 4:
                act.wait_ge(*ost_out[s % 4](16 * (s // 4)))
            act.activation(OST[:, s % 4, 0:width], PS[:, (g.first + n) % 4, 0:width], func)\
               .then_inc(*bank_act.by(1))
            act.wait_ge(*bank_act(g.free0_act + n + 1))
            places = dst(b - g.first_block, a, h, width)
            act.dma_start(places, OST[:, s % 4, 0:width]).then_inc(*ost_out[s % 4].by(16))
            stores[0] += 1

    store_ends, total = {}, 0
    for name in ("xk", "xv", "u", "qk", "v", "gret", "gs5", "xq", "ptok", "pch"):
        total += len(gemms[name].units)
        store_ends[name] = total

    def wait_stores(eng, name, more=0):
        n = store_ends[name] + more
        for i in range(4):
            if (n - i + 3) // 4 > 0:
                eng.wait_ge(*ost_out[i](16 * ((n - i + 3) // 4)))

    def dve_gemm_add(dve, name):
        g = gemms[name]
        for n, (b, a, h, width) in enumerate(g.units):
            c = (b - g.first_block) * HALF
            dve.wait_ge(*mm_done(g.first + n + 1))
            nc.vector.tensor_tensor(X[:, a, c:c + width], X[:, a, c:c + width],
                                    PS[:, (g.first + n) % 4, 0:width], ALU.add).then_inc(*bank_dve.by(1))

    sq_done, st_a, st_b = sem("sq_done"), sem("st_a"), sem("st_b")
    xn_full, xn_turned = sem("xn_full"), sem("xn_turned")
    op_hi_done, op_lo_done = sem("op_hi_done"), sem("op_lo_done")
    x_in, grow_in = sem("x_in"), sem("grow_in")
    norms = []
    JUNK = XN[:, :, :]

    def norm_base(q):
        return sum(norms[:q])

    def act_norm_root(act, q, tiles=TT):
        act.wait_ge(*st_a(q + 1))
        act.activation(st[:, 16:16 + tiles], st[:, 8:8 + tiles], ACT.Sqrt).then_inc(*st_b.by(1))

    def act_norm_stats(act, q, ready, step=0, tiles=TT, root=True):
        base = norm_base(q)
        if base:
            act.wait_ge(*xn_turned(turned_base(q)))
        for t in range(tiles):
            if t == 0 or step:
                act.wait_ge(*ready[0](ready[1] + t * step))
            ins = act.activation(XN[:, t % 2, :], X[:, t, :], ACT.Square, accum_out=st[:, t:t + 1])
            ins.then_inc(*sq_done.by(1))
            act.wait_ge(*sq_done(base + t + 1))
        if root:
            act_norm_root(act, q, tiles)

    def dve_norm_rstd(dve, q, tiles=TT):
        dve.wait_ge(*sq_done(norm_base(q) + tiles))
        nc.vector.tensor_scalar(st[:, 8:8 + tiles], st[:, 0:tiles], 1.0 / D, EPS, ALU.mult, ALU.add)\
            .then_inc(*st_a.by(1))
        dve.wait_ge(*st_b(q + 1))
        return nc.vector.reciprocal(st[:, 24:24 + tiles], st[:, 16:16 + tiles])

    def dve_norm_split(dve, q, chain, tiles=TT):
        base = turned_base(q)
        chain(dve_norm_rstd(dve, q, tiles))
        dve.wait_ge(*grow_in(16 * (q + 1)))

        def lo(t):
            dve.wait_ge(*op_hi_done(base + t + 1))
            p = turn_bank(base + t)
            nc.vector.tensor_tensor(OP_LO[:, :, t * P:(t + 1) * P], PS_T(p),
                                    OP_HI[:, :, t * P:(t + 1) * P].bitcast(F32), ALU.subtract)\
                .then_inc(*op_lo_done.by(1))

        for t in range(tiles):
            if t >= 2:
                dve.wait_ge(*xn_turned(base + t - 1))
            nc.vector.scalar_tensor_tensor(XN[:, t % 2, :], X[:, t, :], st[:, 24 + t:25 + t], GROW[:, :],
                                           ALU.mult, ALU.mult).then_inc(*xn_full.by(1))
            if t:
                lo(t - 1)
        lo(tiles - 1)

    def turn_bank(n):
        return 4 + 2 * (n % 2)

    def PS_T(p):
        return PS[:, p:p + 2, :].rearrange("p b (c t) -> p (b c) t", t=P)

    def pe_norm(pe, q, tiles=TT):
        base = turned_base(q)
        if q == 0:
            pe.wait_ge(*consts_in(16))
        for t in range(tiles):
            pe.wait_ge(*xn_full(base + t + 1))
            if base + t >= 2:
                pe.wait_ge(*op_lo_done(base + t - 1))
            for c in range(KT):
                ins = nc.tensor.transpose(PS_T(turn_bank(base + t))[:, c, :], XN[:, t % 2, c * P:(c + 1) * P],
                                          ident)
            ins.then_inc(*xn_turned.by(1))

    def act_norm_hi(act, q, free=(), tiles=TT):
        base = turned_base(q)
        for s, v in free:
            act.wait_ge(*s(v))
        for t in range(tiles):
            act.wait_ge(*xn_turned(base + t + 1))
            act.activation(OP_HI[:, :, t * P:(t + 1) * P], PS_T(turn_bank(base + t)), ACT.Copy)\
               .then_inc(*op_hi_done.by(1))

    norms += [MEM // P, TT, TT, TT, TT, TT, TT]
    turned = [0, 1, 2, 4, 5]
    turned_by = {}

    def turned_base(q):
        return sum(norms[j] for j in turned if j < q)

    for q_ in range(7):
        turned_by[q_] = turned_base(q_)
    gains = ["norm_mem_g", "norm1_g", "norm2_g", "norm_f_g", "norm1_w_2", "norm2_w_2", "final_norm_w_2"]
    consts_in = sem("consts_in")

    def sp_gain(sp, q, ready=()):
        for s, v in ready:
            sp.wait_ge(*s(v))
        row = I[gains[q]]
        row = row[0:1, :] if len(row.shape) == 2 else row.rearrange("(a n) -> a n", a=1)
        sp.dma_start(GROW[:, :], row.to_broadcast([P, D])).then_inc(*grow_in.by(16))

    PW = at("PW", "stage", 0, [32, 24, P])
    PRM = at("PRM", "stage", 12288, [P, 8, PAIRS])
    DD = at("DD", "stage", 13312, [SP_, SG, SP_])
    PLACE = at("PLACE", "stage", 17408, [SP_, P + SP_])
    DCOL = at("DCOL", "stage", 18432, [SP_, SG])
    A8T = at("A8T", "small", 1024, [P, 2, 2, PAIRS])
    BNAT = at("BNAT", "x", 0, [P, 2, PAIRS, SP_])
    T12 = at("T12", "x", 4096, [P, 2, 2, PAIRS, SP_])
    T34 = at("T34", "x", 12288, [P, 2, 2, PAIRS, SP_])
    CNAT = at("CNAT", "x", 20480, [P, 8, 2, SN])
    CP = at("CP", "x", 24576, [P, 2, PAIRS, SP_])
    RSB = at("RSB", "x", 28672, [P, SG * SP_])
    XPW = at("XPW", "ophi", 0, [P, 2, PAIRS, SC, SP_])
    CPW = at("CPW", "oplo", 0, [P, 2, PAIRS, SC, SP_])
    BT = at("BT", "whi", 0, [P, PAIRS, 2, P])
    ZER = at("ZER", "wlo", 0, [P, SG * SP_])
    CPB = at("CPB", "wlo", 4096, [P, 2, PAIRS, 2, SP_])

    s5_in = sem("s5_in")
    s5_small = sem("s5_small")
    s5_act = sem("s5_act")
    s5_prm_t = sem("s5_prm_t")
    s5_prm = sem("s5_prm")
    s5_cp_t = sem("s5_cp_t")
    s5_cp = sem("s5_cp")
    s5_xpw = sem("s5_xpw")
    s5_cpw = sem("s5_cpw")
    s5_dd = sem("s5_dd")
    s5_r = sem("s5_r")
    s5_rsb = sem("s5_rsb")
    s5_bt_t = sem("s5_bt_t")
    s5_bt = sem("s5_bt")
    s5_zero_out, s5_bt_out = sem("s5_zero_out"), sem("s5_bt_out")
    s5_out = sem("s5_out")
    PRE_LOADS = 12

    def sp_s5_tables(sp):
        loads = [
            (PW[:, 0, :], I["s5_a_re"][0].rearrange("(q b) s -> q (b s)", b=2)),
            (PW[:, 1, :], I["s5_a_im"][0].rearrange("(q b) s -> q (b s)", b=2)),
            (PW[:, 2, 0:2], I["s5_log_dt"].rearrange("a (q b) -> (a q) b", b=2)),
            (BNAT[0:P, 0, :, :], I["s5_b_re"][0].rearrange("(q b) s c -> (b s) q c", b=2)),
            (BNAT[0:P, 1, :, :], I["s5_b_im"][0].rearrange("(q b) s c -> (b s) q c", b=2)),
            (CNAT[:, :, 0, :], I["s5_c_re"][0].rearrange("(t g) c s -> (g c) t s", g=8)),
            (CNAT[:, :, 1, :], I["s5_c_im"][0].rearrange("(t g) c s -> (g c) t s", g=8)),
            (DCOL[:, :], I["s5_d"].rearrange("a (g c) -> (a c) g", c=SP_)),
            (PLACE[:, :], I["c_place"]),
        ]
        for dst, src in loads:
            sp.dma_start(dst, src).then_inc(*s5_in.by(16))
        sp_weights(sp, 2)
        sp.wait_ge(*s5_rsb(1))
        for i in range(SC - 1):
            sp.dma_start(toep_d[SP_ * (i + 1):P, i, :], ZER[SP_ * (i + 1):P, :]).then_inc(*s5_zero_out.by(16))
        sp.wait_ge(*s5_bt(16))
        sp.dma_start(bct_d, BT[:, :, :, :]).then_inc(*s5_bt_out.by(16))
        sp.wait_ge(*s5_xpw(2 * SC))
        sp.dma_start(X[:, 0:2, :], rows_of(I["mem"][0])).then_inc(*x_in.by(16))
        sp.wait_ge(*s5_cpw(4 * SC))
        for c in range(2):
            sp.dma_start(cc_d[:, :, c, :], CPW[:, c, :, :, :].rearrange("p q i c -> p q (i c)"))\
              .then_inc(*s5_out.by(16))
        sp.wait_ge(*s5_rsb(4))
        sp_gain(sp, 0)
        for i in range(SC):
            rows = SP_ * (i + 1)
            sp.dma_start(toep_d[0:rows, i, :], RSB[P - rows:P, :]).then_inc(*s5_out.by(16))
    S5_STORES = 16 * (SC + 2)
    S5_LOADED = 16 * 9

    def reduce_angle(chain, angle, r, n):
        V = nc.vector
        chain(V.tensor_scalar(n, angle, 1.0 / TWO_PI, ROUND, ALU.mult, ALU.add))
        chain(V.tensor_scalar(n, n, ROUND, None, ALU.subtract))
        chain(V.scalar_tensor_tensor(r, n, -PI_A, angle, ALU.mult, ALU.add))
        chain(V.scalar_tensor_tensor(r, n, -PI_B, r, ALU.mult, ALU.add))
        chain(V.scalar_tensor_tensor(r, n, -PI_C, r, ALU.mult, ALU.add))
        chain(V.tensor_scalar(r, r, PI_SAFE, -PI_SAFE, ALU.min, ALU.max))

    def dve_s5_tables(dve, chain):
        V = nc.vector
        w = lambda k: PW[:, k, :]
        MUL, ADD, SUB = ALU.mult, ALU.add, ALU.subtract

        def tt(o, a, b, op):
            chain(V.tensor_tensor(o, a, b, op))

        V.memset(halfpi[:, :], math.pi / 2).then_inc(*s5_small.by(1))
        V.memset(ZER[:, :], 0.0).then_inc(*s5_rsb.by(1))
        V.memset(CPB[:, :, :, :, :], 0.0).then_inc(*s5_rsb.by(1))
        dve.wait_ge(*s5_in(S5_LOADED))
        dve.wait_ge(*s5_act(1))
        chain(V.tensor_copy(w(4).rearrange("q (b s) -> q b s", b=2), PW[:, 3, 0:2].unsqueeze(2).to_broadcast([32, 2, SN])))
        tt(w(5), w(0), w(4), MUL)
        tt(w(6), w(1), w(4), MUL)
        reduce_angle(chain, w(6), w(7), w(8))
        chain(V.scalar_tensor_tensor(w(9), w(7), -1.0, w(7), MUL, ALU.max))
        V.tensor_copy(w(10), w(9)).then_inc(*s5_small.by(1))
        dve.wait_ge(*s5_act(4))
        tt(w(14), w(11), w(13), MUL)
        tt(w(15), w(11), w(12), MUL)
        tt(w(3), w(0), w(0), MUL)
        tt(w(4), w(1), w(1), MUL)
        tt(w(3), w(3), w(4), ADD)
        chain(V.reciprocal(w(5), w(3)))
        chain(V.tensor_scalar(w(6), w(14), -1.0, None, ADD))
        tt(w(7), w(6), w(0), MUL)
        tt(w(8), w(15), w(1), MUL)
        tt(w(7), w(7), w(8), ADD)
        tt(w(16), w(7), w(5), MUL)
        tt(w(7), w(15), w(0), MUL)
        tt(w(8), w(6), w(1), MUL)
        tt(w(7), w(7), w(8), SUB)
        tt(w(17), w(7), w(5), MUL)
        re, im = 14, 15
        for k in range(3):
            tt(w(7), w(re), w(re), MUL)
            tt(w(8), w(im), w(im), MUL)
            tt(w(9), w(re), w(im), MUL)
            re, im = (18, 19) if k % 2 == 0 else (20, 21)
            tt(w(re), w(7), w(8), SUB)
            chain(V.tensor_scalar(w(im), w(9), 2.0, None, MUL))
        V.tensor_copy(w(22), w(re)).then_inc(*s5_small.by(1))
        V.tensor_copy(w(23), w(im)).then_inc(*s5_small.by(1))
        dve.wait_ge(*s5_prm_t(1))
        chain(V.tensor_copy(PRM[:, 0:6, :], PS[:, 4, 0:192].rearrange("p (k q) -> p k q", k=6)))
        chain(V.tensor_scalar(PRM[:, 6, :], PRM[:, 1, :], -1.0, None, MUL))
        for o, t, k in ((0, 0, 4), (1, 1, 4), (1, 0, 5)):
            chain(V.tensor_copy(A8T[:, o, t, :], PRM[:, k, :]))
        V.tensor_scalar(A8T[:, 0, 1, :], PRM[:, 5, :], -1.0, None, MUL).then_inc(*s5_prm.by(1))
        chain(V.tensor_copy(DD[:, :, :], PLACE[:, P:P + SP_].unsqueeze(1).to_broadcast([SP_, SG, SP_])))
        V.tensor_tensor(DD[:, :, :], DD[:, :, :], DCOL[:, :].unsqueeze(2).to_broadcast([SP_, SG, SP_]), MUL)\
            .then_inc(*s5_dd.by(1))
        dve.wait_ge(*s5_dd(1))
        shape = [P, 2, PAIRS, SP_]

        def spread(k):
            return PRM[:, k, :].unsqueeze(1).unsqueeze(3).to_broadcast(shape)

        src = BNAT[:, :, :, :]
        fac = (2, 3)
        for e in range(SC):
            j = SC - 1 - e
            chain(V.tensor_tensor(T12[:, 0], src, spread(fac[0]), MUL))
            chain(V.tensor_tensor(T12[:, 1], src, spread(fac[1]), MUL))
            V.tensor_tensor(XPW[:, 0, :, j, :], T12[:, 0, 0], T12[:, 1, 1], SUB).then_inc(*s5_xpw.by(1))
            V.tensor_tensor(XPW[:, 1, :, j, :], T12[:, 0, 1], T12[:, 1, 0], ADD).then_inc(*s5_xpw.by(1))
            dve.wait_ge(*s5_xpw(2 * e + 2))
            src, fac = XPW[:, :, :, j, :], (0, 1)
        dve.wait_ge(*s5_r(1))
        for half in range(2):
            V.tensor_copy(RSB[:, half * HALF:(half + 1) * HALF], PS[:, 4 + half, :]).then_inc(*s5_rsb.by(1))

    def pool_s5_tables(pool, chain):
        G = nc.gpsimd
        pool.wait_ge(*s5_prm(1))
        pool.wait_ge(*s5_cp(8))
        shape = [P, 2, PAIRS, SP_]

        def spread(k):
            return PRM[:, k, :].unsqueeze(1).unsqueeze(3).to_broadcast(shape)

        src = CP[:, :, :, :]
        for i in range(SC):
            G.tensor_tensor(T34[:, 0], src, spread(0), ALU.mult).then_inc(*s5_cpw.by(1))
            G.tensor_tensor(T34[:, 1], src, spread(6), ALU.mult).then_inc(*s5_cpw.by(1))
            pool.wait_ge(*s5_cpw(4 * i + 2))
            G.tensor_tensor(CPW[:, 0, :, i, :], T34[:, 0, 0], T34[:, 1, 1], ALU.subtract).then_inc(*s5_cpw.by(1))
            G.tensor_tensor(CPW[:, 1, :, i, :], T34[:, 0, 1], T34[:, 1, 0], ALU.add).then_inc(*s5_cpw.by(1))
            pool.wait_ge(*s5_cpw(4 * i + 4))
            src = CPW[:, :, :, i, :]

    def act_s5_tables(act):
        act.wait_ge(*s5_in(S5_LOADED))
        act.activation(PW[:, 3, 0:2], PW[:, 2, 0:2], ACT.Exp).then_inc(*s5_act.by(1))
        act.wait_ge(*s5_small(2))
        act.activation(PW[:, 11, :], PW[:, 5, :], ACT.Exp).then_inc(*s5_act.by(1))
        act.activation(PW[:, 12, :], PW[:, 7, :], ACT.Sin).then_inc(*s5_act.by(1))
        act.activation(PW[:, 13, :], PW[:, 10, :], ACT.Sin, scale=-1.0, bias=halfpi[0:32, :]).then_inc(*s5_act.by(1))
        act.wait_ge(*s5_cp_t(1))
        act.wait_ge(*s5_rsb(2))
        for c in range(2):
            for par in range(2):
                src = PS[64 * c:64 * c + 64, 6:8, :].rearrange("p b (t g e q) -> p (b t) g e q", t=4, g=4, e=2)
                for dst in (CP[64 * par:64 * par + 64, c], CPB[64 * par:64 * par + 64, c, :, par, :]):
                    act.activation(dst.rearrange("p (t g) q -> p t g q", g=4), src[:, :, :, par, :], ACT.Copy,
                                   scale=1.0 if c == 0 else -1.0).then_inc(*s5_cp.by(1))
        for n in range(16):
            act.wait_ge(*s5_bt_t(n + 1))
            act.activation(BT[:, 2 * n:2 * n + 2, :, :].rearrange("p q c s -> p (q c s)"), PS[:, 6 + n % 2, :],
                           ACT.Copy).then_inc(*s5_bt.by(1))

    def pe_s5_tables(pe):
        T = nc.tensor
        pe.wait_ge(*consts_in(16))
        pe.wait_ge(*s5_in(S5_LOADED))
        for t in range(8):
            ins = T.transpose(PS[:, 6 + t // 4, (t % 4) * P:(t % 4 + 1) * P],
                              CNAT[:, t, :, :].rearrange("p c s -> p (c s)"), ident)
        ins.then_inc(*s5_cp_t.by(1))
        pe.wait_ge(*s5_small(4))
        for n, k in enumerate((14, 15, 16, 17, 22, 23)):
            ins = T.transpose(PS[:, 4, 32 * n:32 * n + 32], PW[:, k, :], ident[0:32, 0:32])
        ins.then_inc(*s5_prm_t.by(1))
        pe.wait_ge(*s5_prm(1))
        pe.wait_ge(*s5_xpw(2 * SC))
        pe.wait_ge(*s5_cp(8))
        for n in range(16):
            if n >= 2:
                pe.wait_ge(*s5_bt(n - 1))
            for m in range(4):
                q, c = 2 * n + m // 2, m % 2
                ins = T.transpose(PS[:, 6 + n % 2, m * P:(m + 1) * P],
                                  XPW[:, c, q, :, :].rearrange("p j c -> p (j c)"), ident)
            ins.then_inc(*s5_bt_t.by(1))
        pe.wait_ge(*s5_dd(1))
        for half in range(2):
            T.matmul(PS[:, 4 + half, :], PLACE[:, 0:P],
                     DD[:, 32 * half:32 * half + 32, :].rearrange("p g c -> p (g c)"), start=True, stop=False)
        for q in range(PAIRS):
            for c in range(2):
                ins = T.matmul(PS[:, 4 + q // 16, 32 * (q % 16):32 * (q % 16) + 32],
                               XPW[:, c, q, :, :].rearrange("p j c -> p (j c)"),
                               CPB[:, c, q, :, :].rearrange("p b c -> p (b c)"), start=False,
                               stop=c == 1 and q % 16 == 15)
        ins.then_inc(*s5_r.by(1))

    SCAN = at("SCAN", "x", 0, [P, 2, PAIRS, NCH + 1])
    U8 = at("U8", "stage", 8192, [P, SC, P])
    BCTq = at("BCTq", "stage", 12288, [P, 2, 2, 2, P])
    UTq = at("UTq", "stage", 16384, [P, 4, P])
    URq = at("URq", "stage", 18432, [P, 4, P])
    SM = at("SM", "small", 1536, [P, 2, 2, PAIRS])
    SS = at("SS", "small", 2048, [P, 2, PAIRS])

    s5b_bs = (sem("s5b_b0"), sem("s5b_b1"))
    s5b_in, s5b_t, s5b_ut, s5b_mm, s5b_s = (sem(n) for n in ("s5b_in", "s5b_t", "s5b_ut", "s5b_mm", "s5b_s"))
    s5b_ur = sem("s5b_ur")
    scan_step = sem("scan_step")

    PARTS = SG // 4

    def s5_in_time(m):
        return 3 + 1.6 * m

    def sp_s5_in(sp):
        yield -1
        wait_stores(sp, "u")
        sp.wait_ge(*s5_bt_out(16))
        for m in range(PARTS):
            if m % 2 == 0:
                q = m // 2
                yield s5_in_time(m) - 1.5
                if m:
                    sp.wait_ge(*s5b_ur(m))
                sp.dma_start(U8[:, :, :], u_d.rearrange("(n j) c -> n j c", j=SC)[:, :, q * P:(q + 1) * P])\
                  .then_inc(*s5b_in.by(16))
            yield s5_in_time(m) - 0.7
            if m >= 2:
                sp.wait_ge(*s5b_mm(m - 1))
            sp.dma_start(BCTq[:, m % 2], bct_d[:, 2 * m:2 * m + 2, :, :]).then_inc(*s5b_bs[m % 2].by(16))

    def pe_s5_in(pe):
        T = nc.tensor

        def turn(m):
            pe.wait_ge(*s5b_ur(m + 1))
            if m >= 2:
                pe.wait_ge(*s5b_ut(m - 1))
            for g in range(4):
                ins = T.transpose(PS[:, 4 + m % 2, g * P:(g + 1) * P], URq[:, g, :], ident)
            ins.then_inc(*s5b_t.by(1))

        yield s5_in_time(0) + 0.1
        turn(0)
        for m in range(PARTS):
            if m + 1 < PARTS:
                yield s5_in_time(m) + 1.0
                turn(m + 1)
            yield s5_in_time(m) + 1.02
            pe.wait_ge(*s5b_bs[m % 2](16 * (m // 2 + 1)))
            pe.wait_ge(*s5b_ut(m + 1))
            if m >= 2:
                pe.wait_ge(*s5b_s(m - 1))
            for c in range(2):
                for g in range(4):
                    lo, col = 64 * (g % 2), (2 * c + g // 2) * P
                    ins = T.matmul(PS[lo:lo + 64, 6 + m % 2, col:col + P], BCTq[:, m % 2, g // 2, c, lo:lo + 64],
                                   UTq[:, g, :], start=True, stop=True)
            ins.then_inc(*s5b_mm.by(1))

    def act_s5_in(act):
        for m in range(PARTS):
            yield s5_in_time(m) + 0.15
            act.wait_ge(*s5b_t(m + 1))
            if m:
                act.wait_ge(*s5b_mm(m))
            act.activation(UTq[:, :, :].rearrange("p g n -> p (g n)"), PS[:, 4 + m % 2, :], ACT.Copy)\
               .then_inc(*s5b_ut.by(1))

    def dve_s5_in(dve):
        nc.vector.memset(SCAN[:, :, :, 0:1], 0.0).then_inc(*scan_step.by(1))

        def regroup(m):
            dve.wait_ge(*s5b_in(16 * (m // 2 + 1)))
            if m:
                dve.wait_ge(*s5b_t(m))
            half = U8[:, :, 64 * (m % 2):64 * (m % 2) + 64]
            nc.vector.tensor_copy(URq[:, :, :].rearrange("n g (j c) -> n g j c", j=SC),
                                  half.rearrange("n j (g c) -> n g j c", g=4)).then_inc(*s5b_ur.by(1))

        regroup(0)
        for m in range(PARTS):
            if m + 1 < PARTS:
                regroup(m + 1)
            dve.wait_ge(*s5b_mm(m + 1))
            nc.vector.tensor_copy(SCAN[:, :, 2 * m:2 * m + 2, 1:NCH + 1],
                                  PS[:, 6 + m % 2, :].rearrange("p (c q n) -> p c q n", c=2, q=2))\
                .then_inc(*s5b_s.by(1))

    def dve_s5_scan(dve):
        V = nc.vector
        dve.wait_ge(*s5b_s(PARTS))
        UN = 4
        with dve.Fori(0, NCH // UN) as m:
            for k in range(UN):
                col = m * UN + k
                base = m * (3 * UN) + 3 * k + 1
                dve.wait_ge(*scan_step(base))
                cur = SCAN[:, :, :, bass.ds(col, 1)].rearrange("p c q o -> p (c o) q")
                V.tensor_tensor(SM[:, :, :, :], A8T[:, :, :, :],
                                cur.unsqueeze(1).to_broadcast([P, 2, 2, PAIRS]), ALU.mult).then_inc(*scan_step.by(1))
                dve.wait_ge(*scan_step(base + 1))
                V.tensor_tensor(SS[:, :, :], SM[:, :, 0, :], SM[:, :, 1, :], ALU.add).then_inc(*scan_step.by(1))
                dve.wait_ge(*scan_step(base + 2))
                nxt = SCAN[:, :, :, bass.ds(col + 1, 1)].rearrange("p c q o -> p (c o) q")
                V.tensor_tensor(nxt, nxt, SS[:, :, :], ALU.add).then_inc(*scan_step.by(1))
    SCAN_END = 3 * NCH + 1

    UY = at("UY", "ophi", 0, [P, 2, SC, P])
    TY = at("TY", "ophi", 8192, [P, 2, SC, P])
    CY = at("CY", "ophi", 16384, [P, 2, 4, 2, P])
    UTy = at("UTy", "ophi", 24576, [P, 8, P])
    YS = at("YS", "ophi", 28672, [P, SC, 8, SP_])
    YO = at("YO", "oplo", 0, [P, KT, NCH, SC])

    URy = at("URy", "stage", 16384, [P, 8, P])
    s5y_ur = sem("s5y_ur")
    s5y_in0, s5y_in1 = sem("s5y_in0"), sem("s5y_in1")
    s5y_t, s5y_ut, s5y_mm, s5y_ys, s5y_tt, s5y_yo = (
        sem(n) for n in ("s5y_t", "s5y_ut", "s5y_mm", "s5y_ys", "s5y_tt", "s5y_yo"))

    def sp_s5_y(sp):
        sp.wait_ge(*s5_zero_out(16 * (SC - 1)))
        sp.wait_ge(*mm_done(gemms["gs5"].end))
        for q in range(8):
            b = q % 2
            if q >= 2:
                sp.wait_ge(*s5y_mm(q - 1))
            s = s5y_in1 if b else s5y_in0
            sp.dma_start(UY[:, b], u_d.rearrange("(n j) c -> n j c", j=SC)[:, :, q * P:(q + 1) * P]).then_inc(*s.by(16))
            sp.dma_start(TY[:, b], toep_d[:, :, q * P:(q + 1) * P]).then_inc(*s.by(16))
            sp.dma_start(CY[:, b], cc_d[:, 4 * q:4 * q + 4, :, :]).then_inc(*s.by(16))

    def pe_s5_y(pe):
        T = nc.tensor
        pe.wait_ge(*scan_step(SCAN_END))
        pe.wait_ge(*bank_act(gemms["gs5"].free1_act))

        def turn_back(q):
            pe.wait_ge(*s5y_ys(2 * q + 2))
            if q:
                pe.wait_ge(*s5y_yo(q))
            for i in range(SC):
                ins = T.transpose(PS_T(6)[:, i, :], YS[:, i, :, :].rearrange("n g c -> n (g c)"), ident)
            ins.then_inc(*s5y_tt.by(1))

        for q in range(8):
            b = q % 2
            pe.wait_ge(*(s5y_in1 if b else s5y_in0)(48 * (q // 2 + 1)))
            pe.wait_ge(*s5y_ur(q + 1))
            if q:
                pe.wait_ge(*s5y_ut(q))
            for g in range(8):
                ins = T.transpose(PS_T(2)[:, g, :], URy[:, g, :], ident)
            ins.then_inc(*s5y_t.by(1))
            if q:
                turn_back(q - 1)
            pe.wait_ge(*s5y_ut(q + 1))
            if q:
                pe.wait_ge(*s5y_ys(2 * q))
            for g in range(8):
                lo = 64 * (g % 2)
                o = PS[:, 4 + g % 2, (g // 2) * P:(g // 2 + 1) * P]
                T.matmul(o, UTy[:, g, :], TY[:, b, :, 16 * g:16 * g + 16], start=True, stop=False)
                for c in range(2):
                    ins = T.matmul(o, SCAN[lo:lo + 64, c, 4 * q + g // 2, 0:NCH], CY[lo:lo + 64, b, g // 2, c, :],
                                   start=False, stop=c == 1)
            ins.then_inc(*s5y_mm.by(1))
        turn_back(7)

    def act_s5_y(act):
        for q in range(8):
            act.wait_ge(*s5y_t(q + 1))
            if q:
                act.wait_ge(*s5y_mm(q))
            act.activation(UTy[:, :, :], PS_T(2), ACT.Copy).then_inc(*s5y_ut.by(1))
            if q:
                y_gelu(act, q - 1)
        y_gelu(act, 7)

    def y_gelu(act, q):
        act.wait_ge(*s5y_tt(q + 1))
        act.activation(YO[:, q].rearrange("c n i -> c i n"), PS_T(6), ACT.Gelu_apprx_tanh).then_inc(*s5y_yo.by(1))

    def act_split_y(act):
        act.wait_ge(*s5y_mm(8))
        act.wait_ge(*s5y_yo(8))
        for k in range(KT):
            act.activation(OP_HI[:, k, :], YO[:, k].rearrange("c n i -> c (n i)"), ACT.Copy).then_inc(*la_hi.by(1))

    def dve_split_y(dve):
        for k in range(KT):
            dve.wait_ge(*la_hi(k + 1))
            nc.vector.tensor_tensor(OP_LO[:, k, :], YO[:, k].rearrange("c n i -> c (n i)"),
                                    OP_HI[:, k, :].bitcast(F32), ALU.subtract).then_inc(*la_lo.by(1))

    def dve_s5_y(dve):
        def regroup(q):
            dve.wait_ge(*(s5y_in1 if q % 2 else s5y_in0)(48 * (q // 2 + 1)))
            if q:
                dve.wait_ge(*s5y_t(q))
            nc.vector.tensor_copy(URy[:, :, :].rearrange("n g (j c) -> n g j c", j=SC),
                                  UY[:, q % 2].rearrange("n j (g c) -> n g j c", g=8)).then_inc(*s5y_ur.by(1))

        regroup(0)
        for q in range(8):
            if q + 1 < 8:
                regroup(q + 1)
            dve.wait_ge(*s5y_mm(q + 1))
            if q:
                dve.wait_ge(*s5y_tt(q))
            for par in range(2):
                nc.vector.tensor_copy(YS[:, :, par::2, :].rearrange("n i g c -> n g i c"),
                                      PS[:, 4 + par, :].rearrange("n (g i c) -> n g i c", g=4, i=SC))\
                    .then_inc(*s5y_ys.by(1))

    PC = at("PC", "small", 2304, [P, 64])
    GLUB, GN, DNW, GLW, SCW, DNC = 0, 8, 16, 17, 18, 24
    pc_in = sem("pc_in")
    PC_LOADED = 16 * 8

    def sp_columns(sp):
        for dst, src in (
                (PC[:, GLUB:GLUB + 8], I["s5_glu_b"].rearrange("a (k p) -> p (a k)", p=P)),
                (PC[:, GN:GN + 8], I["ret_gn_g"].rearrange("a (k p) -> p (a k)", p=P)),
                (PC[0:64, DNW:DNW + 1], I["dn_norm_w_2"].rearrange("a p -> p a")),
                (PC[64:P, DNW:DNW + 1], I["dn_norm_w_2"].rearrange("a p -> p a")),
                (PC[0:64, GLW:GLW + 1], I["gla_norm_w_2"].rearrange("a p -> p a")),
                (PC[64:P, GLW:GLW + 1], I["gla_norm_w_2"].rearrange("a p -> p a")),
                (PC[:, SCW:SCW + 6], I["sc_conv_w_2"][0].rearrange("k (c p) -> p (k c)", p=P)),
                (PC[:, DNC:DNC + 24], I["dn_conv_w_2"][0].rearrange("k (c p) -> p (k c)", p=P))):
            sp.dma_start(dst, src).then_inc(*pc_in.by(16))

    LA = at("LA", "stage", 0, [P, 4, L])
    la_in = [sem(f"la_in{i}") for i in range(4)]
    la_hi, la_lo = sem("la_hi"), sem("la_lo")

    def sp_load_operand(sp, src):
        for k in range(KT):
            yield 0 if k < 4 else 16.5
            if k >= 4:
                sp.wait_ge(*la_lo(KT + k - 3))
            sp.dma_start(LA[:, k % 4, :], src[k * P:(k + 1) * P, :]).then_inc(*la_in[k % 4].by(16))

    def act_load_operand(act):
        for k in range(KT):
            act.wait_ge(*la_in[k % 4](16 * (k // 4 + 1)))
            act.activation(OP_HI[:, k, :], LA[:, k % 4, :], ACT.Copy).then_inc(*la_hi.by(1))

    def dve_load_operand(dve):
        for k in range(KT):
            dve.wait_ge(*la_hi(KT + k + 1))
            nc.vector.tensor_tensor(OP_LO[:, k, :], LA[:, k % 4, :], OP_HI[:, k, :].bitcast(F32), ALU.subtract)\
                .then_inc(*la_lo.by(1))

    GA = at("GA", "stage", 12288, [P, 2, HALF])
    ZB = at("ZB", "stage", 16384, [P, 2, HALF])
    YB = at("YB", "x", 28160, [P, HALF])
    GG = at("GG", "x", 24064, [P, 2, HALF])
    glu_y, glu_z = sem("glu_y"), sem("glu_z")
    glu_in = [sem("glu_in0"), sem("glu_in1")]
    glu_out = [sem("glu_out0"), sem("glu_out1")]

    def sp_glu(sp):
        g = gemms["glu"]
        for n, (b, a, h, _) in enumerate(g.units):
            c = 4 * (b - g.first_block) + a
            yield n - 0.5
            if n >= 2:
                sp.wait_ge(*glu_z(n - 1))
            sp.dma_start(GG[:, n % 2, :], gs5_d[c * P:(c + 1) * P, h * HALF:(h + 1) * HALF])\
              .then_inc(*glu_in[n % 2].by(16))

    def act_glu(act):
        g = gemms["glu"]
        act.wait_ge(*pc_in(PC_LOADED))

        def store(n):
            b, a, h, _ = g.units[n]
            c = 4 * (b - g.first_block) + a
            act.wait_ge(*glu_z(n + 1))
            act.dma_start(st_d[c * P:(c + 1) * P, h * HALF:(h + 1) * HALF], ZB[:, n % 2, :])\
               .then_inc(*glu_out[n % 2].by(16))

        for n, (b, a, h, _) in enumerate(g.units):
            c = 4 * (b - g.first_block) + a
            act.wait_ge(*mm_done(g.first + n + 1))
            if n >= 2:
                act.wait_ge(*glu_z(n - 1))
            act.activation(GA[:, n % 2, :], PS[:, (g.first + n) % 4, :], ACT.Sigmoid,
                           bias=PC[:, GLUB + c:GLUB + c + 1]).then_inc(*bank_act.by(1))
            if n:
                store(n - 1)
        store(len(g.units) - 1)

    def dve_glu(dve):
        g = gemms["glu"]
        for n, (b, a, h, _) in enumerate(g.units):
            c = 4 * (b - g.first_block) + a
            s = slice(h * HALF, (h + 1) * HALF)
            if n:
                dve.wait_ge(*glu_z(n))
            nc.vector.tensor_tensor(YB[:, :], OP_HI[:, c, s].bitcast(F32), OP_LO[:, c, s].bitcast(F32), ALU.add)\
                .then_inc(*glu_y.by(1))
            dve.wait_ge(*glu_y(2 * n + 1))
            dve.wait_ge(*glu_in[n % 2](16 * (n // 2 + 1)))
            nc.vector.tensor_tensor(YB[:, :], YB[:, :], GG[:, n % 2, :], ALU.mult).then_inc(*glu_y.by(1))
            dve.wait_ge(*glu_y(2 * n + 2))
            dve.wait_ge(*bank_act(g.free0_act + n + 1))
            if n >= 2:
                dve.wait_ge(*glu_out[n % 2](16 * (n // 2)))
            nc.vector.tensor_tensor(ZB[:, n % 2, :], YB[:, :], GA[:, n % 2, :], ALU.mult).then_inc(*glu_z.by(1))

    NRC = RH * P + 2 * RH + RH // 2 + 32
    RC = at("RC", "x", 0, [P, NRC])
    RW = RC[:, RH * P:RH * P + 2 * RH]
    RDEC = RC[:, RH * P + 2 * RH:RH * P + 2 * RH + 4]
    RINV = RC[:, NRC - 32:NRC]
    COS = at("COS", "x", 4352, [P, TT, 32])
    SIN = at("SIN", "x", 5376, [P, TT, 32])
    POSI = at("POSI", "x", 6400, [P, TT], I32)
    POSF = at("POSF", "x", 6432, [P, TT])
    ANG = at("ANG", "x", 6656, [P, 3, TT, 32])
    RST = at("RST", "x", 9728, [P, 4, P])
    RTA = at("RTA", "x", 11776, [P, 2 * RH, 2, 32])
    RTB = at("RTB", "x", 15872, [P, 2 * RH, 2, 32])
    QKR = at("QKR", "x", 19968, [P, 2 * RH, 2, 32])
    QKT = at("QKT", "x", 24064, [P, 8, P])
    SCR = at("SCR", "x", 28160, [P, 2, 4, P])
    QKL = at("QKL", "stage", 0, [P, 2 * RH, 2, 32])
    VL = at("VL", "stage", 4096, [P, D])
    GRL = at("GRL", "stage", 8192, [P, 8, P])
    ONR = at("ONR", "stage", 12288, [P, RH, P])
    GOR = at("GOR", "stage", 16384, [P, RH, P])
    BNS = at("BNS", "small", 2560, [P, RH, 6])
    BNM = at("BNM", "small", 2752, [P, RH, 2])
    RRS = at("RRS", "small", 2816, [P, 3, RH])

    rc_in, rq_in, rv_in, rg_in = (sem(n) for n in ("rc_in", "rq_in", "rv_in", "rg_in"))
    r_ang, r_trig, r_ab, r_rot, r_turn, r_qkt, r_sc, r_scr, r_o, r_kv = (
        sem(n) for n in ("r_ang", "r_trig", "r_ab", "r_rot", "r_turn", "r_qkt", "r_sc", "r_scr", "r_o", "r_kv"))
    r_rst, r_var, r_root, r_on, r_back, r_g, r_hi, r_lo = (
        sem(n) for n in ("r_rst", "r_var", "r_root", "r_on", "r_back", "r_g", "r_hi", "r_lo"))

    def sp_retention(sp):
        yield
        sp.wait_ge(*s5y_mm(8))
        sp.dma_start(RC[:, :], I["c_ret"]).then_inc(*rc_in.by(16))
        sp.dma_start(POSI[:, :], I["positions"].rearrange("a (t p) -> p (a t)", p=P)).then_inc(*rc_in.by(16))
        rows = lambda t: slice(t * P, (t + 1) * P)

        def load_qk(t):
            sp.dma_start(QKL[:, :, :, :].rearrange("p h a b -> p (h a b)"), qk_d[rows(t), :]).then_inc(*rq_in.by(16))

        def load_v(t):
            sp.dma_start(VL[:, :], v_d[rows(t), :]).then_inc(*rv_in.by(16))

        load_qk(0)
        load_v(0)
        yield
        for t in range(TT):
            if t + 1 < TT:
                sp.wait_ge(*r_ab(2 * t + 2))
                load_qk(t + 1)
            if t:
                sp.wait_ge(*r_g(2 * t - 1))
            sp.dma_start(GRL[:, :, :], gret_d.rearrange("(k p) t -> p k t", p=P)[:, :, rows(t)]).then_inc(*rg_in.by(16))
            if t + 1 < TT:
                sp.wait_ge(*r_kv(t + 1))
                load_v(t + 1)

    def pe_retention(pe):
        T = nc.tensor
        pe.wait_ge(*bank_act(gemms["glu"].free1_act))

        def turn(t):
            pe.wait_ge(*r_rot(t + 1))
            if t >= 2:
                pe.wait_ge(*r_g(2 * t - 3))
            flat = QKR[:, :, :, :].rearrange("p h a b -> p (h a b)")
            for c in range(8):
                ins = T.transpose(PS_T(0)[:, c, :], flat[:, c * P:(c + 1) * P], ident)
            ins.then_inc(*r_turn.by(1))

        def scores(t):
            pe.wait_ge(*r_qkt(t + 1))
            if t:
                pe.wait_ge(*r_scr(t))
            for h in range(RH):
                lo, p = 64 * (h % 2), h // 2
                ins = T.matmul(PS[:, 2 + h % 2, p * P:(p + 1) * P], QKT[lo:lo + 64, 4 + p, :],
                               QKT[lo:lo + 64, p, :], start=True, stop=True)
            ins.then_inc(*r_sc.by(1))

        def outputs(t):
            pe.wait_ge(*r_scr(t + 1))
            pe.wait_ge(*rv_in(16 * (t + 1)))
            if t:
                pe.wait_ge(*r_rst(3 * t + 1))
                pe.wait_ge(*r_on(t))
            else:
                pe.wait_ge(*r_rst(1))
            for h in range(RH):
                lo, p = 64 * (h % 2), h // 2
                o = PS[:, 4 + h % 2, p * P:(p + 1) * P]
                T.matmul(o, SCR[:, h % 2, p, :], VL[:, h * P:(h + 1) * P], start=True, stop=False)
                ins = T.matmul(o, QKT[lo:lo + 64, p, :], RST[lo:lo + 64, p, :], start=False, stop=True)
            ins.then_inc(*r_o.by(1))

        def update(t):
            flat = QKR[:, :, :, :].rearrange("p h a b -> p (h a b)")
            for p in range(4):
                ins = T.matmul(PS[:, 6 + p // 2, (p % 2) * 256:(p % 2) * 256 + 256],
                               flat[:, HALF + p * P:HALF + (p + 1) * P], VL[:, p * 256:(p + 1) * 256],
                               start=True, stop=True)
            ins.then_inc(*r_kv.by(1))

        def turn_out(t):
            pe.wait_ge(*r_on(t + 1))
            if t + 1 < TT:
                pe.wait_ge(*r_qkt(t + 2))
            for h in range(RH):
                ins = T.transpose(PS_T(0)[:, h, :], ONR[:, h, :], ident)
            ins.then_inc(*r_back.by(1))

        turn(0)
        scores(0)
        for t in range(TT):
            outputs(t)
            update(t)
            if t + 1 < TT:
                turn(t + 1)
                scores(t + 1)
            turn_out(t)

    def act_retention(act):
        yield
        act.wait_ge(*r_ang(1))
        act.activation(SIN[:, :, :], ANG[:, 1, :, :], ACT.Sin).then_inc(*r_trig.by(1))
        act.activation(COS[:, :, :], ANG[:, 2, :, :], ACT.Sin, scale=-1.0, bias=halfpi[:, :]).then_inc(*r_trig.by(1))

        def turned(t):
            act.wait_ge(*r_turn(t + 1))
            act.activation(QKT[:, :, :], PS_T(0), ACT.Copy).then_inc(*r_qkt.by(1))

        yield
        act.wait_ge(*glu_z(16))
        turned(0)
        for t in range(TT):
            if t + 1 < TT:
                act.wait_ge(*r_o(t + 1))
                turned(t + 1)
            act.wait_ge(*r_var(t + 1))
            act.activation(RRS[:, 1, :], RRS[:, 0, :], ACT.Sqrt).then_inc(*r_root.by(1))
            act.wait_ge(*r_g(2 * t + 2))
            act.activation(OP_HI[:, :, t * P:(t + 1) * P], GOR[:, :, :], ACT.Copy).then_inc(*r_hi.by(1))

    def dve_retention(dve, chain):
        V = nc.vector
        MUL, ADD, SUB = ALU.mult, ALU.add, ALU.subtract
        yield
        dve.wait_ge(*pc_in(PC_LOADED))
        dve.wait_ge(*rc_in(32))
        V.memset(RST[:, :, :], 0.0).then_inc(*r_rst.by(1))
        chain(V.tensor_copy(POSF[:, :], POSI[:, :]))
        chain(V.tensor_tensor(ANG[:, 0, :, :], POSF[:, :].unsqueeze(2).to_broadcast([P, TT, 32]),
                              RINV.unsqueeze(1).to_broadcast([P, TT, 32]), MUL))
        reduce_angle(chain, ANG[:, 0, :, :], ANG[:, 1, :, :], ANG[:, 2, :, :])
        V.scalar_tensor_tensor(ANG[:, 2, :, :], ANG[:, 1, :, :], -1.0, ANG[:, 1, :, :], MUL, ALU.max)\
            .then_inc(*r_ang.by(1))
        dve.wait_ge(*r_trig(2))

        def products(t):
            dve.wait_ge(*rq_in(16 * (t + 1)))
            shape = [P, 2 * RH, 2, 32]
            cos = COS[:, t, :].unsqueeze(1).unsqueeze(1).to_broadcast(shape)
            sin = SIN[:, t, :].unsqueeze(1).unsqueeze(1).to_broadcast(shape)
            V.tensor_tensor(RTA[:, :, :, :], QKL[:, :, :, :], cos, MUL).then_inc(*r_ab.by(1))
            V.tensor_tensor(RTB[:, :, :, :], QKL[:, :, :, :], sin, MUL).then_inc(*r_ab.by(1))

        def rotate(t):
            dve.wait_ge(*r_ab(2 * t + 2))
            if t:
                dve.wait_ge(*r_kv(t))
            chain(V.tensor_tensor(QKR[:, :, 0, :], RTA[:, :, 0, :], RTB[:, :, 1, :], SUB))
            chain(V.tensor_tensor(QKR[:, :, 1, :], RTB[:, :, 0, :], RTA[:, :, 1, :], ADD))
            flat = QKR[:, :, :, :].rearrange("p h a b -> p h (a b)")
            V.tensor_tensor(flat, flat, RW.unsqueeze(2).to_broadcast([P, 2 * RH, 64]), MUL).then_inc(*r_rot.by(1))

        def mask(t):
            dve.wait_ge(*r_sc(t + 1))
            if t:
                dve.wait_ge(*r_o(t))
            V.tensor_tensor(SCR[:, :, :, :].rearrange("p a b i -> p (a b i)"),
                            PS[:, 2:4, :].rearrange("p b n -> p (b n)"), RC[:, 0:RH * P], MUL).then_inc(*r_scr.by(1))

        products(0)
        rotate(0)
        yield
        for s in glu_out:
            dve.wait_ge(*s(16 * 8))
        products(1)
        mask(0)
        for t in range(TT):
            if t + 1 < TT:
                rotate(t + 1)
            dve.wait_ge(*r_kv(t + 1))
            dve.wait_ge(*r_o(t + 1))
            kv = PS[:, 6:8, :].rearrange("p b (q e) -> p (b q) e", q=2)
            V.tensor_tensor(RST[:, :, :], RST[:, :, :], RDEC.unsqueeze(2).to_broadcast([P, 4, P]), MUL)\
                .then_inc(*r_rst.by(1))
            dve.wait_ge(*r_rst(3 * t + 2))
            V.tensor_tensor(RST[0:64, :, :], RST[0:64, :, :], kv[0:64, :, 0:P], ADD).then_inc(*r_rst.by(1))
            V.tensor_tensor(RST[64:P, :, :], RST[64:P, :, :], kv[64:P, :, P:2 * P], ADD).then_inc(*r_rst.by(1))
            for h in range(RH):
                V.bn_stats(BNS[:, h, :], PS[:, 4 + h % 2, (h // 2) * P:(h // 2 + 1) * P]).then_inc(*chain.s.by(1))
            chain.n += RH
            dve.wait_ge(*chain.s(chain.n))
            for h in range(RH):
                V.bn_aggr(BNM[:, h, :], BNS[:, h, :]).then_inc(*chain.s.by(1))
            chain.n += RH
            dve.wait_ge(*chain.s(chain.n))
            V.tensor_scalar(RRS[:, 0, :], BNM[:, :, 1], EPS, None, ADD).then_inc(*r_var.by(1))
            dve.wait_ge(*r_root(t + 1))
            chain(V.reciprocal(RRS[:, 2, :], RRS[:, 1, :]))
            if t:
                dve.wait_ge(*r_back(t))
            for h in range(RH):
                ins = V.tensor_scalar(ONR[:, h, :], PS[:, 4 + h % 2, (h // 2) * P:(h // 2 + 1) * P],
                                      BNM[:, h, 0:1], RRS[:, 2, h:h + 1], SUB, MUL)
            ins.then_inc(*r_on.by(1))
            if t + 1 < TT:
                mask(t + 1)
            if t + 2 < TT:
                products(t + 2)
            dve.wait_ge(*r_back(t + 1))
            dve.wait_ge(*rg_in(16 * (t + 1)))
            if t:
                dve.wait_ge(*r_lo(t))
            V.tensor_tensor(GOR[:, :, :], PS_T(0), GRL[:, :, :], MUL).then_inc(*r_g.by(1))
            dve.wait_ge(*r_g(2 * t + 1))
            V.tensor_tensor(GOR[:, :, :], GOR[:, :, :], PC[:, GN:GN + 8].unsqueeze(2).to_broadcast([P, 8, P]),
                            MUL).then_inc(*r_g.by(1))
            dve.wait_ge(*r_hi(t + 1))
            V.tensor_tensor(OP_LO[:, :, t * P:(t + 1) * P], GOR[:, :, :],
                            OP_HI[:, :, t * P:(t + 1) * P].bitcast(F32), SUB).then_inc(*r_lo.by(1))

    KA = at("KA", "stage", 0, [P, KT, MEM])
    VA = at("VA", "stage", 8192, [P, 2, D])
    QTL = at("QTL", "x", 0, [P, 2, KT, P])
    PM = at("PM", "x", 8192, [P, 2, XH, MEM])
    PT = at("PT", "x", 16384, [P, 8, P])
    XST = at("XST", "x", 20480, [P, 2, 4, XH])
    xa_kv, xa_q = sem("xa_kv"), (sem("xa_q0"), sem("xa_q1"))
    xa_s, xa_nm, xa_e, xa_p, xa_t, xa_pt, xa_o, xa_hi, xa_lo = (
        sem(n) for n in ("xa_s", "xa_nm", "xa_e", "xa_p", "xa_t", "xa_pt", "xa_o", "xa_hi", "xa_lo"))
    SCALE = XD ** -0.5

    def sp_attention(sp):
        sp.wait_ge(*xn_turned(turned_base(2) + TT))
        sp.dma_start(VA[:, :, :], va_d.rearrange("(k p) n -> p k n", p=P)).then_inc(*xa_kv.by(16))
        wait_stores(sp, "xq")
        for t in range(TT):
            if t >= 2:
                sp.wait_ge(*xa_s(t - 1))
            sp.dma_start(QTL[:, t % 2], qa_d.rearrange("(k p) t -> p k t", p=P)[:, :, t * P:(t + 1) * P])\
              .then_inc(*xa_q[t % 2].by(16))
            if t == 0:
                sp.dma_start(KA[:, :, :], ka_d.rearrange("(k p) m -> p k m", p=P)).then_inc(*xa_kv.by(16))

    def pe_attention_scores(pe):
        T = nc.tensor
        yield 0
        pe.wait_ge(*bank_act(gemms["xq"].free1_act))
        pe.wait_ge(*xa_kv(32))
        for t in range(TT):
            yield t
            pe.wait_ge(*xa_q[t % 2](16 * (t // 2 + 1)))
            if t >= 2:
                pe.wait_ge(*xa_e(4 * (t - 1)))
            for h in range(XH):
                for k in range(2):
                    ins = T.matmul(PS[:, 2 * (t % 2) + h // 2, (h % 2) * MEM:(h % 2 + 1) * MEM],
                                   QTL[:, t % 2, 2 * h + k, :], KA[:, 2 * h + k, :], start=k == 0, stop=k == 1)
            ins.then_inc(*xa_s.by(1))

    def pe_attention_outputs(pe):
        T = nc.tensor
        for t in range(TT):
            yield t + 1.1
            pe.wait_ge(*xa_p(t + 1))
            if t:
                pe.wait_ge(*xa_pt(t))
            for c in range(8):
                ins = T.transpose(PS_T(4)[:, c, :], PM[:, t % 2, c // 2, (c % 2) * P:(c % 2 + 1) * P], ident)
            ins.then_inc(*xa_t.by(1))
            yield t + 2.1
            pe.wait_ge(*xa_pt(t + 1))
            if t:
                pe.wait_ge(*xa_lo(t))
            for c in range(8):
                for m in range(2):
                    ins = T.matmul(PS_T(6)[:, c, :], VA[:, m, c * P:(c + 1) * P], PT[:, 2 * (c // 2) + m, :],
                                   start=m == 0, stop=m == 1)
            ins.then_inc(*xa_o.by(1))

    def act_attention_scores(act):
        for t in range(TT):
            yield t + 0.4
            act.wait_ge(*xa_nm(t + 1))
            if t >= 2:
                act.wait_ge(*xa_t(t - 1))
            for h in range(XH):
                act.activation(PM[:, t % 2, h, :], PS[:, 2 * (t % 2) + h // 2, (h % 2) * MEM:(h % 2 + 1) * MEM],
                               ACT.Exp, bias=XST[:, t % 2, 1, h:h + 1], scale=SCALE,
                               accum_out=XST[:, t % 2, 2, h:h + 1]).then_inc(*xa_e.by(1))

    def act_attention_outputs(act):
        for t in range(TT):
            yield t + 1.2
            act.wait_ge(*xa_t(t + 1))
            if t:
                act.wait_ge(*xa_o(t))
            act.activation(PT[:, :, :], PS_T(4), ACT.Copy).then_inc(*xa_pt.by(1))
            yield t + 2.2
            act.wait_ge(*xa_o(t + 1))
            act.activation(OP_HI[:, :, t * P:(t + 1) * P], PS_T(6), ACT.Copy).then_inc(*xa_hi.by(1))

    def dve_attention_scores(dve, chain):
        V = nc.vector
        for t in range(TT):
            st_ = XST[:, t % 2]
            yield t + 0.3
            dve.wait_ge(*xa_s(t + 1))
            chain(V.tensor_reduce(st_[:, 0, :], PS[:, 2 * (t % 2):2 * (t % 2) + 2, :]
                                  .rearrange("p b (h m) -> p (b h) m", h=2), AX.X, ALU.max))
            V.tensor_scalar(st_[:, 1, :], st_[:, 0, :], -SCALE, None, ALU.mult).then_inc(*xa_nm.by(1))
            yield t + 0.5
            dve.wait_ge(*xa_e(4 * (t + 1)))
            chain(V.reciprocal(st_[:, 3, :], st_[:, 2, :]))
            V.tensor_tensor(PM[:, t % 2], PM[:, t % 2], st_[:, 3, :].unsqueeze(2).to_broadcast([P, XH, MEM]),
                            ALU.mult).then_inc(*xa_p.by(1))

    def dve_attention_outputs(dve):
        for t in range(TT):
            yield t + 2.25
            dve.wait_ge(*xa_hi(t + 1))
            nc.vector.tensor_tensor(OP_LO[:, :, t * P:(t + 1) * P], PS_T(6),
                                    OP_HI[:, :, t * P:(t + 1) * P].bitcast(F32), ALU.subtract)\
                .then_inc(*xa_lo.by(1))

    inplace = sem("inplace")
    x_out = sem("x_out")

    def dve_norm_inplace(dve, q, chain):
        chain(dve_norm_rstd(dve, q))
        dve.wait_ge(*grow_in(16 * (q + 1)))
        for t in range(TT):
            nc.vector.scalar_tensor_tensor(X[:, t, :], X[:, t, :], st[:, 24 + t:25 + t], GROW[:, :],
                                           ALU.mult, ALU.mult).then_inc(*inplace.by(1))

    def rows_of(ap):
        return ap.rearrange("(t p) d -> p t d", p=P)

    dqkv_d = scratch("dqkv_d", (L, 3 * GW))
    CB = at("CB", "stage", 8192, [P, 3, L])
    SACC = at("SACC", "x", 24608, [P, 2, L])
    CAC = at("CAC", "x", 16416, [P, 2, L])
    CQ = at("CQ", "x", 24608, [P, 2, 1032])
    CSL = at("CSL", "stage", 0, [P, 2, L])
    OV = at("OV", "stage", 8192, [P, 2, TT, P])
    cq_in, cb_in, cv_zero, dc_acc, dc_s, dc_t, dc_ov = (
        sem(n) for n in ("cq_in0", "cb_in", "cv_zero", "dc_acc", "dc_s", "dc_t", "dc_ov"))
    cq_ins, dc_out = (cq_in, sem("cq_in1")), (sem("dc_out0"), sem("dc_out1"))
    sc_acc, sc_hi, sc_lo = sem("sc_acc"), sem("sc_hi"), sem("sc_lo")
    NDC = 3 * GW // P
    OPC_CONV = 2

    def sp_conv(sp):
        yield -2
        wait_stores(sp, "pch")
        sp.wait_ge(*sc_lo(1))
        for n in range(NDC):
            yield conv_time(n - 2) + 0.1
            if n >= 2:
                sp.wait_ge(*dc_acc(n - 1))
            sp.dma_start(CQ[:, n % 2, 3:3 + L], pch_d[3 * GW + n * P:3 * GW + (n + 1) * P, :]).then_inc(*cq_ins[n % 2].by(16))

    def conv_time(n):
        return -0.9 + 0.14 * n

    def dve_conv(dve, chain):
        V = nc.vector
        MUL, ADD = ALU.mult, ALU.add
        dve.wait_ge(*sc_lo(1))
        V.memset(CQ[:, :, 0:3], 0.0).then_inc(*cv_zero.by(1))
        dve.wait_ge(*cv_zero(1))
        for n in range(NDC):
            w = lambda k: PC[:, DNC + k * NDC + n:DNC + k * NDC + n + 1]
            acc = CAC[:, n % 2, :]
            yield conv_time(n)
            dve.wait_ge(*cq_ins[n % 2](16 * (n // 2 + 1)))
            if n >= 2:
                dve.wait_ge(*dc_s(n - 1))
            chain(V.tensor_scalar(acc, CQ[:, n % 2, 0:L], w(0), None, MUL))
            for k in (1, 2):
                chain(V.scalar_tensor_tensor(acc, CQ[:, n % 2, k:k + L], w(k), acc, MUL, ADD))
            V.scalar_tensor_tensor(acc, CQ[:, n % 2, 3:3 + L], w(3), acc, MUL, ADD).then_inc(*dc_acc.by(1))

    def sp_short_conv(sp):
        for n in range(2):
            yield 13.5 + 4 * n
            if n:
                sp.wait_ge(*sc_acc(n))
            else:
                wait_stores(sp, "ptok", more=2 * 3 * GW // P)
                sp.wait_ge(*xn_turned(turned_base(4) + TT))
                sp.wait_ge(*xn_full(turned_base(4) + TT))
            sp.dma_start(CB[:, :, :], pch_d[0:3 * GW, :].rearrange("(k c p) t -> c p k t", k=3, p=P)[n])\
              .then_inc(*cb_in.by(16))

    def dve_short_conv(dve, chain):
        V = nc.vector
        MUL, ADD = ALU.mult, ALU.add
        for n in range(2):
            w = lambda k: PC[:, SCW + 2 * k + n:SCW + 2 * k + n + 1]
            acc, c = SACC[:, n, :], CB[:, 1, :]
            yield 14.3 + 4 * n
            dve.wait_ge(*cb_in(16 * (n + 1)))
            chain(V.tensor_tensor(c, c, CB[:, 2, :], MUL))
            chain(V.tensor_scalar(acc, c, w(2), None, MUL))
            for k in (1, 0):
                late = 2 - k
                chain(V.scalar_tensor_tensor(acc[:, late:L], c[:, 0:L - late], w(k), acc[:, late:L], MUL, ADD))
            V.tensor_tensor(acc, acc, CB[:, 0, :], MUL).then_inc(*sc_acc.by(1))
        yield 30.3
        dve.wait_ge(*sc_hi(1))
        V.tensor_tensor(OP_LO[:, OPC_CONV:OPC_CONV + 2, :], SACC[:, :, :],
                        OP_HI[:, OPC_CONV:OPC_CONV + 2, :].bitcast(F32), ALU.subtract).then_inc(*sc_lo.by(1))

    def act_short_conv(act):
        yield 30.2
        act.wait_ge(*mm_done(gemms["pch"].end))
        act.wait_ge(*sc_acc(2))
        act.activation(OP_HI[:, OPC_CONV:OPC_CONV + 2, :], SACC[:, :, :], ACT.Copy).then_inc(*sc_hi.by(1))

    def act_conv(act):
        def store(n):
            act.wait_ge(*dc_t(n + 1))
            if n >= 2:
                act.wait_ge(*dc_out[n % 2](16 * (n // 2)))
            act.activation(OV[:, n % 2], PS_T(2 * (n % 2)), ACT.Copy).then_inc(*dc_ov.by(1))
            act.wait_ge(*dc_ov(n + 1))
            act.dma_start(dqkv_d[:, n * P:(n + 1) * P].rearrange("(t p) c -> p t c", p=P), OV[:, n % 2])\
               .then_inc(*dc_out[n % 2].by(16))

        for n in range(NDC):
            yield conv_time(n) + 0.02
            act.wait_ge(*dc_acc(n + 1))
            if n >= 2:
                act.wait_ge(*dc_t(n - 1))
            act.activation(CSL[:, n % 2, :], CAC[:, n % 2, :], ACT.Silu).then_inc(*dc_s.by(1))
            if n:
                store(n - 1)
        yield -0.2
        store(NDC - 1)

    def pe_conv(pe):
        for n in range(NDC):
            yield conv_time(n) + 0.03
            pe.wait_ge(*dc_s(n + 1))
            if n >= 2:
                pe.wait_ge(*dc_ov(n - 1))
            for t in range(TT):
                ins = nc.tensor.transpose(PS_T(2 * (n % 2))[:, t, :], CSL[:, n % 2, t * P:(t + 1) * P], ident)
            ins.then_inc(*dc_t.by(1))

    SUV = at("SUV", "x", 8192, [P, 2, 2, GW])
    SGL = at("SGL", "x", 12288, [P, 2, GW])
    SVN = at("SVN", "x", 14336, [P, GH, GD])
    SYA = at("SYA", "x", 15360, [P, GH, GD])
    WSL = at("WSL", "x", 16384, [P, GH, P])
    WST = at("WST", "x", 18432, [P, GH, P])
    LNW = at("LNW", "x", 20480, [P, GH, GD])
    LNB = at("LNB", "x", 21504, [P, GH, GD])
    BSC = at("BSC", "x", 22528, [P, GH])
    SBN = at("SBN", "x", 22560, [P, 16])
    SOUT = at("SOUT", "x", 0, [P, 2, L])
    su_in = (sem("su_in0"), sem("su_in1"))
    sg_in, sg_w, sg_wt, sg_gl, sg_var, sg_root, sg_vn, sg_mm, sg_y, sg_t, sg_hi, sg_lo = (
        sem(n) for n in ("sg_in", "sg_w", "sg_wt", "sg_gl", "sg_var", "sg_root", "sg_vn", "sg_mm", "sg_y", "sg_t",
                         "sg_hi", "sg_lo"))

    def sp_sgu(sp):
        yield 0
        wait_stores(sp, "ptok")
        sp.wait_ge(*x_out(32))
        sp.wait_ge(*xn_full(turned_base(4) + TT))
        sp.dma_start(WSL[:, :, :], I["sgu_w_spatial_2"][0].rearrange("h t s -> t h s")).then_inc(*sg_in.by(16))
        sp.dma_start(LNW[:, :, :].rearrange("p h d -> p (h d)"), I["sgu_ln_w_2"].to_broadcast([P, GW])).then_inc(*sg_in.by(16))
        sp.dma_start(LNB[:, :, :].rearrange("p h d -> p (h d)"), I["sgu_ln_b_2"].to_broadcast([P, GW])).then_inc(*sg_in.by(16))
        sp.dma_start(BSC[:, :], I["sgu_b_spatial_2"][0].rearrange("h t -> t h")).then_inc(*sg_in.by(16))
        for t in range(TT):
            yield max(0, 3 * t - 4)
            if t >= 2:
                sp.wait_ge(*sg_gl(t - 1))
            sp.dma_start(SUV[:, t % 2].rearrange("p a n -> p (a n)"), ptok_d[t * P:(t + 1) * P, C_AU:C_AU + 2 * GW])\
              .then_inc(*su_in[t % 2].by(16))

    def pe_sgu(pe):
        T = nc.tensor
        yield 1.5
        pe.wait_ge(*sg_in(64))
        for h in range(GH):
            ins = T.transpose(PS[:, 4, h * P:(h + 1) * P], WSL[:, h, :], ident)
        ins.then_inc(*sg_w.by(1))
        for t in range(TT):
            yield 3 * t + 2.5
            if t == 0:
                pe.wait_ge(*sg_wt(1))
            pe.wait_ge(*sg_vn(t + 1))
            if t:
                pe.wait_ge(*sg_y(2 * t - 1))
            for h in range(GH):
                ins = T.matmul(PS[:, 5, h * GD:(h + 1) * GD], WST[:, h, :], SVN[:, h, :], start=True, stop=True)
            ins.then_inc(*sg_mm.by(1))
            yield 3 * t + 3.5
            pe.wait_ge(*sg_y(2 * t + 2))
            if t:
                pe.wait_ge(*sg_hi(t))
            flat = SYA[:, :, :].rearrange("p h d -> p (h d)")
            for c in range(2):
                ins = T.transpose(PS[:, 6, c * P:(c + 1) * P], flat[:, c * P:(c + 1) * P], ident)
            ins.then_inc(*sg_t.by(1))

    def act_sgu(act):
        for t in range(TT):
            yield 3 * t + 1.92 if t else 1.6
            act.wait_ge(*su_in[t % 2](16 * (t // 2 + 1)))
            if t:
                act.wait_ge(*sg_y(2 * t))
            act.activation(SGL[:, :, :], SUV[:, t % 2], ACT.Gelu_apprx_tanh).then_inc(*sg_gl.by(1))
            yield 3 * t + 2.1
            act.wait_ge(*sg_var(t + 1))
            act.activation(SBN[:, 9:10], SBN[:, 8:9], ACT.Sqrt).then_inc(*sg_root.by(1))
            yield 3 * t + 3.6
            act.wait_ge(*sg_t(t + 1))
            act.activation(SOUT[:, :, t * P:(t + 1) * P], PS[:, 6, 0:2 * P].rearrange("p (c t) -> p c t", c=2),
                           ACT.Copy).then_inc(*sg_hi.by(1))
        yield 30
        act.wait_ge(*mm_done(gemms["pch"].end))
        act.wait_ge(*sg_hi(TT))
        act.activation(OP_HI[:, 0:2, :], SOUT[:, :, :], ACT.Copy).then_inc(*sg_hi.by(1))

    def dve_sgu(dve, chain):
        V = nc.vector
        MUL, ADD, SUB = ALU.mult, ALU.add, ALU.subtract
        yield 1.55
        dve.wait_ge(*sg_w(1))
        V.tensor_tensor(WST[:, :, :], PS[:, 4, :].rearrange("p (h t) -> p h t", h=GH),
                        K["causal"].unsqueeze(1).to_broadcast([P, GH, P]), MUL).then_inc(*sg_wt.by(1))
        for t in range(TT):
            yield 3 * t + 2
            dve.wait_ge(*sg_gl(t + 1))
            chain(V.bn_stats(SBN[:, 0:6], SGL[:, 1, :]))
            chain(V.bn_aggr(SBN[:, 6:8], SBN[:, 0:6]))
            V.tensor_scalar(SBN[:, 8:9], SBN[:, 7:8], EPS, None, ADD).then_inc(*sg_var.by(1))
            yield 3 * t + 2.2
            dve.wait_ge(*sg_root(t + 1))
            chain(V.reciprocal(SBN[:, 10:11], SBN[:, 9:10]))
            if t:
                dve.wait_ge(*sg_mm(t))
            flat = SVN[:, :, :].rearrange("p h d -> p (h d)")
            chain(V.tensor_scalar(flat, SGL[:, 1, :], SBN[:, 6:7], SBN[:, 10:11], SUB, MUL))
            chain(V.tensor_tensor(SVN[:, :, :], SVN[:, :, :], LNW[:, :, :], MUL))
            V.tensor_tensor(SVN[:, :, :], SVN[:, :, :], LNB[:, :, :], ADD).then_inc(*sg_vn.by(1))
            yield 3 * t + 2.6
            dve.wait_ge(*sg_mm(t + 1))
            if t:
                dve.wait_ge(*sg_t(t))
            V.tensor_tensor(SYA[:, :, :], PS[:, 5, 0:GW].rearrange("p (h d) -> p h d", h=GH),
                            BSC[:, :].unsqueeze(2).to_broadcast([P, GH, GD]), ADD).then_inc(*sg_y.by(1))
            dve.wait_ge(*sg_y(2 * t + 1))
            V.tensor_tensor(SYA[:, :, :], SYA[:, :, :], SGL[:, 0, :].rearrange("p (h d) -> p h d", h=GH), MUL)\
                .then_inc(*sg_y.by(1))
        yield 30.1
        dve.wait_ge(*sg_hi(TT + 1))
        V.tensor_tensor(OP_LO[:, 0:2, :], SOUT[:, :, :], OP_HI[:, 0:2, :].bitcast(F32), SUB).then_inc(*sg_lo.by(1))

    class Finish:
        def __init__(self, tag, region, off, op_tile, weight):
            self.OQ = at(f"{tag}OQ", region, off, [P, GH, GD])
            self.O = at(f"{tag}O", region, off + 1024, [P, GH, GD])
            self.SQ = at(f"{tag}SQ", region, off + 2048, [P, GH, GD])
            self.ZS = at(f"{tag}ZS", region, off + 3072, [P, GH, GD])
            self.OG = at(f"{tag}OG", region, off + 4096, [P, 2, P])
            self.ST = at(f"{tag}ST", region, off + 5120, [P, 4, GH])
            self.op_tile, self.weight = op_tile, weight
            self.q_t, self.q = sem(f"{tag}_q_t"), sem(f"{tag}_q")
            self.av, self.zs = sem(f"{tag}_av"), sem(f"{tag}_zs")
            self.ms, self.root = sem(f"{tag}_ms"), sem(f"{tag}_root")
            self.on, self.turn = sem(f"{tag}_on"), sem(f"{tag}_turn")
            self.og, self.hi, self.lo = sem(f"{tag}_og"), sem(f"{tag}_hi"), sem(f"{tag}_lo")

        def act_q(self, act, t, bank, col):
            act.wait_ge(*self.q_t(t + 1))
            if t:
                act.wait_ge(*self.on(t))
            act.activation(self.OQ[:, :, :].rearrange("p (q a) d -> p a q d", a=2),
                           PS[:, bank:bank + 2, col:col + P].rearrange("p a (q d) -> p a q d", q=2), ACT.Copy)\
               .then_inc(*self.q.by(1))

        def dve_norm(self, dve, chain, t, bank, later):
            V = nc.vector
            dve.wait_ge(*self.q(t + 1))
            dve.wait_ge(*self.av(t + 1))
            if t:
                dve.wait_ge(*self.turn(t))
            chain(V.tensor_tensor(self.O[:, :, :], self.OQ[:, :, :],
                                  PS[:, bank, 0:GW].rearrange("p (h d) -> p h d", h=GH), ALU.add))
            chain(V.tensor_tensor(self.SQ[:, :, :], self.O[:, :, :], self.O[:, :, :], ALU.mult))
            chain(V.tensor_reduce(self.ST[:, 0, :], self.SQ[:, :, :], AX.X, ALU.add))
            V.tensor_scalar(self.ST[:, 1, :], self.ST[:, 0, :], 1.0 / GD, EPS, ALU.mult, ALU.add).then_inc(*self.ms.by(1))
            yield later
            dve.wait_ge(*self.root(t + 1))
            chain(V.reciprocal(self.ST[:, 3, :], self.ST[:, 2, :]))
            chain(V.tensor_tensor(self.O[:, :, :], self.O[:, :, :],
                                  self.ST[:, 3, :].unsqueeze(2).to_broadcast([P, GH, GD]), ALU.mult))
            dve.wait_ge(*self.zs(t + 1))
            V.tensor_tensor(self.O[:, :, :], self.O[:, :, :], self.ZS[:, :, :], ALU.mult).then_inc(*self.on.by(1))

        def act_root(self, act, t):
            act.wait_ge(*self.ms(t + 1))
            act.activation(self.ST[:, 2, :], self.ST[:, 1, :], ACT.Sqrt).then_inc(*self.root.by(1))

        def act_z(self, act, t, z):
            if t:
                act.wait_ge(*self.on(t))
            act.activation(self.ZS[:, :, :].rearrange("p h d -> p (h d)"), z, ACT.Silu).then_inc(*self.zs.by(1))

        def pe_turn(self, pe, t, bank):
            pe.wait_ge(*self.on(t + 1))
            flat = self.O[:, :, :].rearrange("p h d -> p (h d)")
            for c in range(2):
                ins = nc.tensor.transpose(PS[:, bank, c * P:(c + 1) * P], flat[:, c * P:(c + 1) * P], ident)
            ins.then_inc(*self.turn.by(1))

        def dve_gain(self, dve, t, bank):
            dve.wait_ge(*self.turn(t + 1))
            if t:
                dve.wait_ge(*self.lo(t))
            nc.vector.tensor_scalar(self.OG[:, :, :].rearrange("p c t -> p (c t)"), PS[:, bank, 0:2 * P],
                                    PC[:, self.weight:self.weight + 1], None, ALU.mult).then_inc(*self.og.by(1))

        def act_hi(self, act, t):
            act.wait_ge(*self.og(t + 1))
            k = self.op_tile
            act.activation(OP_HI[:, k:k + 2, t * P:(t + 1) * P], self.OG[:, :, :], ACT.Copy).then_inc(*self.hi.by(1))

        def dve_lo(self, dve, t):
            dve.wait_ge(*self.hi(t + 1))
            k = self.op_tile
            nc.vector.tensor_tensor(OP_LO[:, k:k + 2, t * P:(t + 1) * P], self.OG[:, :, :],
                                    OP_HI[:, k:k + 2, t * P:(t + 1) * P].bitcast(F32), ALU.subtract)\
                .then_inc(*self.lo.by(1))

    LEVELS = (1, 2, 4, 8, 16, 32)
    DQ = at("DQ", "x", 0, [P, 2, 3, GH, GD])
    DZ = at("DZ", "x", 6144, [P, 2, GW])
    CAB = at("CAB", "x", 8192, [P, TT, 8])
    GTB = at("GTB", "x", 8448, [P, 6, TT, GH])
    ADT = at("ADT", "x", 9216, [P, 3, GH])
    AG = at("AG", "x", 9344, [P, 4, P])
    EX = at("EX", "small", 1536, [P, 4, TT, GH])
    DRS = at("DRS", "x", 11456, [P, 3, 8])
    KK2 = (at("KKa", "x", 11776, [P, 7, GH, GD]), at("KKb", "raw", 0, [P, 7, GH, GD]))
    TR2 = (at("TRa", "x", 18944, [P, 8, P]), at("TRb", "raw", 7168, [P, 8, P]))
    DTB = at("DTB", "x", 23040, [P, 4, P])
    DTU = at("DTU", "x", 25088, [P, 4, P])
    LT = at("LT", "x", 27136, [P, 4, P])
    AT2 = (at("ATa", "x", 29184, [P, 4, P]), at("ATb", "raw", 11264, [P, 4, P]))
    DU2 = (at("DUa", "x", 31232, [P, GH, GD]), at("DUb", "raw", 13312, [P, GH, GD]))
    CTM = at("CTM", "stage", 0, [P, 2, 4, P])
    P1 = at("P1", "stage", 4096, [P, 4, P])
    VV = at("VV", "stage", 6144, [P, 4, P])
    VT = at("VT", "stage", 8192, [P, 4, P])
    WT2 = (at("WTa", "stage", 10240, [P, 2, P]), at("WTb", "raw", 14336, [P, 2, P]))
    VN = at("VN", "stage", 11264, [P, GH, GD])
    SD = at("SD", "stage", 12288, [P, 2, GD])
    DECP = at("DECP", "small", 1024, [P, 2, TT, 2])
    K_HAT, K_B, Q_HAT, Q_G, K_BG, K_D, V_B = range(7)
    G_, BETA = 4, 5
    fin_d = Finish("dn", "stage", 13312, 4, DNW)
    dn = {n: sem(f"dn_{n}") for n in (
        "in0", "in1", "par", "sp", "e1", "g", "ag", "gm", "ex", "dec", "dt", "ss", "rt", "kk", "tr", "trc", "la",
        "lt", "ct", "c1", "p1", "p1c", "w", "v", "uw", "u", "ws", "vn", "ks", "s", "zero")}

    def sp_delta(sp):
        yield -0.8
        sp.wait_ge(*sg_lo(1))
        sp.dma_start(CAB[:, :, :], ptok_d[:, C_CA:C_CA + 8].rearrange("(t p) c -> p t c", p=P)).then_inc(*dn["par"].by(16))
        sp.dma_start(ADT[:, 0, :], I["dn_a_log_2"].to_broadcast([P, GH])).then_inc(*dn["par"].by(16))
        sp.dma_start(ADT[:, 1, :], I["dn_dt_bias_2"].to_broadcast([P, GH])).then_inc(*dn["par"].by(16))
        yield -0.1
        sp.wait_ge(*dc_s(NDC))
        for s in dc_out:
            sp.wait_ge(*s(16 * NDC // 2))
        for t in range(TT):
            yield max(0, t - 0.95)
            rows, s = slice(t * P, (t + 1) * P), dn[f"in{t % 2}"]
            if t >= 2:
                sp.wait_ge(*dn["kk"](t - 1))
                sp.wait_ge(*fin_d.zs(t - 1))
            sp.dma_start(DQ[:, t % 2].rearrange("p a h d -> p (a h d)"), dqkv_d[rows, :]).then_inc(*s.by(16))
            sp.dma_start(DZ[:, t % 2, :], ptok_d[rows, C_CZ:C_CZ + GW]).then_inc(*s.by(16))

    def order(h):
        return 2 * (h % 2) + h // 2

    def level_time(t, k):
        return t + 0.22 + 0.14 * (k - 1)

    def pe_delta_head(pe):
        T = nc.tensor
        yield -0.45
        pe.wait_ge(*dn["g"](2))
        for m, name in enumerate(("upto", "later", "first", "second")):
            ins = T.matmul(PS[:, 4, 32 * m:32 * m + 32], K[name], GTB[:, G_].rearrange("p t h -> p (t h)"),
                           start=True, stop=True)
        ins.then_inc(*dn["gm"].by(1))
        for t in range(TT):
            yield t
            KK, TR = KK2[t % 2], TR2[t % 2]
            pe.wait_ge(*dn["ag"](t + 1))
            if t:
                pe.wait_ge(*dn["v"](11 * t))
            else:
                pe.wait_ge(*dn["zero"](1))
            for h in range(GH):
                ins = T.matmul(PS[:, 2, order(h) * P:(order(h) + 1) * P], AG[:, h, :], K["upto"],
                               start=True, stop=True)
            ins.then_inc(*dn["dec"].by(1))
            yield t + 0.02
            pe.wait_ge(*dn["kk"](t + 1))
            if t:
                pe.wait_ge(*dn["u"](2 * t))
            for n, (slot, p) in enumerate(((K_HAT, 0), (K_HAT, 1), (K_B, 0), (Q_HAT, 0), (K_B, 1), (Q_HAT, 1),
                                           (Q_G, 0), (Q_G, 1))):
                ins = T.transpose(PS_T(0)[:, n, :], KK[:, slot, 2 * p:2 * p + 2, :].rearrange("p h d -> p (h d)"), ident)
            ins.then_inc(*dn["tr"].by(1))
            yield t + 0.08
            pe.wait_ge(*dn["trc"](t + 1))
            for h in range(GH):
                lo, p = 64 * (h % 2), h // 2
                ins = T.matmul(PS[:, h % 2, p * 256:(p + 1) * 256], TR[lo:lo + 64, p, :],
                               TR[lo:lo + 64, 2 + 2 * p:4 + 2 * p, :], start=True, stop=True)
            ins.then_inc(*dn["la"].by(1))
            n = 5 * t
            yield t + 0.16
            pe.wait_ge(*dn["ct"](6 * t + 1))
            for h in range(GH):
                ins = T.transpose(PS[:, 0, h * P:(h + 1) * P], CTM[:, 0, h, :], ident)
            ins.then_inc(*dn["c1"].by(1))
            for k in range(1, 6):
                yield level_time(t, k)
                pe.wait_ge(*dn["ct"](6 * t + k + 1))
                pe.wait_ge(*dn["v"](11 * t + 2 * k))
                for h in range(GH):
                    ins = T.matmul(PS[:, 0, h * P:(h + 1) * P], CTM[:, k % 2, h, :], VV[:, h, :], start=True, stop=True)
                ins.then_inc(*dn["p1"].by(1))
                yield level_time(t, k) + 0.05
                pe.wait_ge(*dn["p1c"](n + k))
                if k < 5:
                    for h in range(GH):
                        T.matmul(PS[:, 1, h * P:(h + 1) * P], VT[:, h, :], P1[:, h, :], start=True, stop=True)
                for h in range(GH):
                    ins = T.matmul(PS[:, 2, h * P:(h + 1) * P], P1[:, h, :], VT[:, h, :], start=True, stop=True)
                ins.then_inc(*dn["w"].by(1))
            yield t + 0.93
            pe.wait_ge(*dn["v"](11 * t + 11))
            for h in range(GH):
                T.matmul(PS[:, 1, h * GD:(h + 1) * GD], VT[:, order(h), :], KK[:, V_B, h, :], start=True, stop=True)
            for h in range(GH):
                lo, p = 64 * (h % 2), h // 2
                ins = T.matmul(PS[lo:lo + 64, 0, p * P:(p + 1) * P], KK[:, K_BG, h, :], VT[:, order(h), :],
                               start=True, stop=True)
            ins.then_inc(*dn["uw"].by(1))
    def pe_delta_tail(pe):
        T = nc.tensor
        for t in range(TT):
            KK, TR, AT, WT = KK2[t % 2], TR2[t % 2], AT2[t % 2], WT2[t % 2]
            for c in range(2):
                yield t + 1.03 + 0.14 * c
                if c == 0:
                    pe.wait_ge(*dn["u"](2 * t + 2))
                    if t:
                        pe.wait_ge(*fin_d.og(t))
                r = slice(64 * c, 64 * c + 64)
                pe.wait_ge(*dn["s"](3 * (2 * t + c)))
                for h in range(GH):
                    lo, p = 64 * (h % 2), h // 2
                    ins = T.matmul(PS[r, 3 + h % 2, p * GD:(p + 1) * GD], WT[lo:lo + 64, p, r], SD[lo:lo + 64, p, :],
                                   start=True, stop=True)
                for h in range(GH):
                    lo, p = 64 * (h % 2), h // 2
                    ins = T.matmul(PS[r, 3 + h % 2, P + p * GD:P + (p + 1) * GD], TR[lo:lo + 64, 6 + p, r], SD[lo:lo + 64, p, :],
                                   start=True, stop=True)
                ins.then_inc(*(fin_d.q_t if c else dn["ws"]).by(1))
                yield t + 1.10 + 0.14 * c
                pe.wait_ge(*dn["vn"](2 * t + c + 1))
                for p in range(2):
                    ins = T.matmul(PS[:, 3 + c, (2 + p) * P:(3 + p) * P],
                                   KK[r, K_D, 2 * p:2 * p + 2, :].rearrange("p h d -> p (h d)"),
                                   VN[r, 2 * p:2 * p + 2, :].rearrange("p h d -> p (h d)"), start=True, stop=True)
                ins.then_inc(*dn["ks"].by(1))
            yield t + 1.30
            pe.wait_ge(*fin_d.q(t + 1))
            for h in range(GH):
                ins = T.matmul(PS[:, 3, h * GD:(h + 1) * GD], AT[:, order(h), :], VN[:, h, :], start=True, stop=True)
            ins.then_inc(*fin_d.av.by(1))
            yield t + 1.42
            fin_d.pe_turn(pe, t, 4)

    def act_delta_prepare(act):
        yield -0.5
        act.wait_ge(*dn["par"](48))
        act.activation(ADT[:, 2, :], ADT[:, 0, :], ACT.Exp).then_inc(*dn["e1"].by(1))
        act.wait_ge(*dn["sp"](1))
        act.activation(GTB[:, 2], GTB[:, 1], ACT.Exp, scale=-1.0).then_inc(*dn["e1"].by(1))
        act.wait_ge(*dn["e1"](2))
        act.activation(GTB[:, 3], GTB[:, 2], ACT.Ln, bias=1.0).then_inc(*dn["e1"].by(1))
        act.activation(GTB[:, BETA], CAB[:, :, 4:8], ACT.Sigmoid).then_inc(*dn["g"].by(1))
        yield -0.42
        act.wait_ge(*dn["gm"](1))
        act.activation(EX[:, :, :, :].rearrange("p m t h -> p (m t h)"), PS[:, 4, 0:P], ACT.Exp).then_inc(*dn["ex"].by(1))
        for t in range(TT):
            yield max(0, t - 0.42)
            act.wait_ge(*dn["ss"](t + 1))
            act.activation(DRS[:, 1, :], DRS[:, 0, :], ACT.Sqrt).then_inc(*dn["rt"].by(1))

    def act_delta_head(act):
        for t in range(TT):
            yield t + 0.03
            act.wait_ge(*dn["dec"](t + 1))
            if t:
                act.wait_ge(*dn["lt"](2 * t))
            act.activation(DTU[:, :, :].rearrange("p h c -> p (h c)"), PS[:, 2, :], ACT.Exp).then_inc(*dn["dt"].by(1))
            yield t + 0.05
            act.wait_ge(*dn["tr"](t + 1))
            act.activation(TR2[t % 2][:, :, :], PS_T(0), ACT.Copy).then_inc(*dn["trc"].by(1))
            for k in range(1, 6):
                yield level_time(t, k) + 0.03
                act.wait_ge(*dn["p1"](5 * t + k))
                act.activation(P1[:, :, :].rearrange("p h c -> p (h c)"), PS[:, 0, :], ACT.Copy).then_inc(*dn["p1c"].by(1))
            yield t + 0.96
            act.wait_ge(*dn["uw"](t + 1))
            act.activation(WT2[t % 2][:, :, :].rearrange("p q c -> p (q c)"), PS[:, 0, 0:2 * P], ACT.Copy).then_inc(*dn["u"].by(1))
            act.activation(DU2[t % 2][:, :, :].rearrange("p h d -> p (h d)"), PS[:, 1, 0:GW], ACT.Copy).then_inc(*dn["u"].by(1))
    def act_delta_tail(act):
        for t in range(TT):
            yield t + 0.5
            act.wait_ge(*dn[f"in{t % 2}"](32 * (t // 2 + 1)))
            fin_d.act_z(act, t, DZ[:, t % 2, :])
            yield t + 1.28
            act.wait_ge(*dn["s"](6 * t + 6))
            fin_d.act_q(act, t, 3, P)
            yield t + 1.36
            fin_d.act_root(act, t)
            yield t + 1.46
            fin_d.act_hi(act, t)

    def dve_delta_prepare(dve, chain):
        V = nc.vector
        MUL, ADD, SUB = ALU.mult, ALU.add, ALU.subtract
        yield -0.5
        dve.wait_ge(*dn["par"](48))
        chain(V.tensor_tensor(GTB[:, 0], CAB[:, :, 0:4], ADT[:, 1, :].unsqueeze(1).to_broadcast([P, TT, GH]), ADD))
        V.scalar_tensor_tensor(GTB[:, 1], GTB[:, 0], -1.0, GTB[:, 0], MUL, ALU.max).then_inc(*dn["sp"].by(1))
        dve.wait_ge(*dn["e1"](3))
        chain(V.scalar_tensor_tensor(GTB[:, 1], GTB[:, 0], 0.0, GTB[:, 3], ALU.max, ADD))
        chain(V.tensor_tensor(GTB[:, 0], GTB[:, 1], ADT[:, 2, :].unsqueeze(1).to_broadcast([P, TT, GH]), MUL))
        V.tensor_scalar(GTB[:, G_], GTB[:, 0], -1.0, None, MUL).then_inc(*dn["g"].by(1))
        dve.wait_ge(*dn["g"](2))
        yield -0.4
        heads = lambda v: v.unsqueeze(2).to_broadcast([P, GH, GD])
        dve.wait_ge(*dn["ex"](1))
        for a in range(2):
            chain(V.tensor_copy(DECP[64 * a:64 * a + 64], EX[64 * a:64 * a + 64, 2:4]
                                .rearrange("p c t (q a) -> p c t q a", a=2)[:, :, :, :, a]))

        yield -0.05
        for s in dc_out:
            dve.wait_ge(*s(16 * NDC // 2))
        dve.wait_ge(*w_split(2 * gemms["out2"].first_block + 2))
        V.memset(SD[:, :, :], 0.0).then_inc(*dn["zero"].by(1))
        dve.wait_ge(*dn["zero"](1))
        for t in range(TT):
            b = t % 2
            KK = KK2[b]
            yield max(0, t - 0.5)
            if t:
                dve.wait_ge(*dn["dec"](t))
            V.tensor_tensor(AG[:, :, :], K["later"].unsqueeze(1).to_broadcast([P, 4, P]),
                            GTB[:, G_, t, :].unsqueeze(2).to_broadcast([P, 4, P]), MUL).then_inc(*dn["ag"].by(1))
            yield max(0, t - 0.45)
            dve.wait_ge(*dn[f"in{b}"](32 * (t // 2 + 1)))
            qk = DQ[:, b, 0:2].rearrange("p a h d -> p (a h) d")
            sq = DTB[:, :, :].rearrange("p h c -> p (h c)").rearrange("p (h d) -> p h d", d=GD)
            chain(V.tensor_tensor(sq, qk, qk, MUL))
            chain(V.tensor_reduce(DRS[:, 2, :], sq, AX.X, ADD))
            V.tensor_scalar(DRS[:, 0, :], DRS[:, 2, :], EPS, None, ADD).then_inc(*dn["ss"].by(1))
            yield max(0, t - 0.38)
            dve.wait_ge(*dn["rt"](t + 1))
            chain(V.reciprocal(DRS[:, 2, :], DRS[:, 1, :]))
            chain(V.tensor_scalar(DRS[:, 2, 0:4], DRS[:, 2, 0:4], GD ** -0.5, None, MUL))
            chain(V.tensor_tensor(KK[:, Q_HAT], DQ[:, b, 0], heads(DRS[:, 2, 0:4]), MUL))
            chain(V.tensor_tensor(KK[:, K_HAT], DQ[:, b, 1], heads(DRS[:, 2, 4:8]), MUL))
            chain(V.tensor_tensor(KK[:, K_B], KK[:, K_HAT], heads(GTB[:, BETA, t, :]), MUL))
            V.tensor_tensor(KK[:, V_B], DQ[:, b, 2], heads(GTB[:, BETA, t, :]), MUL).then_inc(*chain.s.by(1))
            chain.n += 1
            yield max(0, t - 0.32)
            V.tensor_tensor(KK[:, Q_G], KK[:, Q_HAT], heads(EX[:, 0, t, :]), MUL).then_inc(*chain.s.by(1))
            V.tensor_tensor(KK[:, K_D], KK[:, K_HAT], heads(EX[:, 1, t, :]), MUL).then_inc(*chain.s.by(1))
            chain.n += 2
            dve.wait_ge(*chain.s(chain.n))
            V.tensor_tensor(KK[:, K_BG], KK[:, K_B], heads(EX[:, 0, t, :]), MUL).then_inc(*dn["kk"].by(1))

    def dve_delta_head(dve, chain):
        V = nc.vector
        MUL, SUB = ALU.mult, ALU.subtract
        for t in range(TT):
            AT = AT2[t % 2]
            yield t + 0.05
            dve.wait_ge(*dn["dt"](t + 1))
            chain(V.tensor_tensor(DTB[:, :, :], DTU[:, :, :], K["before"].unsqueeze(1).to_broadcast([P, 4, P]), MUL))
            chain(V.tensor_tensor(DTU[:, :, :], DTU[:, :, :], K["upto"].unsqueeze(1).to_broadcast([P, 4, P]), MUL))
            yield t + 0.11
            dve.wait_ge(*dn["la"](t + 1))
            la = PS[:, 0:2, :].rearrange("p a (q m c) -> p a q m c", q=2, m=2)
            V.tensor_tensor(LT[:, :, :].rearrange("p (a q) c -> p a q c", a=2), la[:, :, :, 0, :],
                            DTB[:, :, :].rearrange("p (a q) c -> p a q c", a=2), MUL).then_inc(*dn["lt"].by(1))
            V.tensor_tensor(AT[:, :, :].rearrange("p (a q) c -> p a q c", a=2), la[:, :, :, 1, :],
                            DTU[:, :, :].rearrange("p (a q) c -> p a q c", a=2), MUL).then_inc(*dn["lt"].by(1))
            dve.wait_ge(*dn["lt"](2 * t + 2))

            def level(k):
                V.tensor_tensor(CTM[:, k % 2], LT[:, :, :],
                                K[f"join{LEVELS[k]}"].unsqueeze(1).to_broadcast([P, 4, P]), MUL).then_inc(*dn["ct"].by(1))

            level(0)
            level(1)
            eye = ident.unsqueeze(1).to_broadcast([P, 4, P])
            dve.wait_ge(*dn["ct"](6 * t + 1))
            if t:
                dve.wait_ge(*dn["uw"](t))
            V.tensor_tensor(VT[:, :, :], eye, CTM[:, 0], SUB).then_inc(*dn["v"].by(1))
            yield t + 0.18
            dve.wait_ge(*dn["c1"](t + 1))
            V.tensor_tensor(VV[:, :, :], eye, PS[:, 0, :].rearrange("p (h c) -> p h c", h=4), SUB).then_inc(*dn["v"].by(1))
            flat = lambda x: x[:, :, :].rearrange("p h c -> p (h c)")
            for k in range(1, 6):
                yield level_time(t, k) + 0.01
                if k < 5:
                    dve.wait_ge(*dn["v"](11 * t + 2 * k))
                    level(k + 1)
                yield level_time(t, k) + 0.1
                dve.wait_ge(*dn["w"](5 * t + k))
                if k < 5:
                    V.tensor_tensor(flat(VV), flat(VV), PS[:, 1, :], SUB).then_inc(*dn["v"].by(1))
                V.tensor_tensor(flat(VT), flat(VT), PS[:, 2, :], SUB).then_inc(*dn["v"].by(1))

    def dve_delta_tail(dve, chain):
        V = nc.vector
        MUL, ADD, SUB = ALU.mult, ALU.add, ALU.subtract
        for t in range(TT):
            DU = DU2[t % 2]
            for c in range(2):
                r = slice(64 * c, 64 * c + 64)
                n = 2 * t + c
                yield t + 1.07 + 0.14 * c
                dve.wait_ge(*dn["u"](2 * t + 2))
                dve.wait_ge(*(fin_d.q_t if c else dn["ws"])(t + 1))
                V.tensor_tensor(VN[r].rearrange("p (q a) d -> p a q d", a=2),
                                DU[r].rearrange("p (q a) d -> p a q d", a=2),
                                PS[r, 3:5, 0:P].rearrange("p a (q d) -> p a q d", q=2), SUB).then_inc(*dn["vn"].by(1))
                yield t + 1.13 + 0.14 * c
                dve.wait_ge(*dn["ks"](n + 1))
                V.tensor_tensor(SD[:, :, :], SD[:, :, :], DECP[:, c, t, :].unsqueeze(2).to_broadcast([P, 2, GD]), MUL)\
                    .then_inc(*dn["s"].by(1))
                dve.wait_ge(*dn["s"](3 * n + 1))
                for a in range(2):
                    h = slice(64 * a, 64 * a + 64)
                    V.tensor_tensor(SD[h], SD[h], PS[h, 3 + c, 2 * P:4 * P]
                                    .rearrange("p (q b d) -> p q b d", q=2, b=2)[:, :, a, :], ADD).then_inc(*dn["s"].by(1))
            yield t + 1.33
            yield from fin_d.dve_norm(dve, chain, t, 3, t + 1.37)
            yield t + 1.44
            fin_d.dve_gain(dve, t, 4)
            yield t + 1.48
            fin_d.dve_lo(dve, t)

    NGP = C_TOK - C_DG
    GP = at("GP", "whi", 0, [P, 2, NGP])
    GTT = at("GTT", "whi", 15488, [32, P])
    W2A = at("W2A", "wlo", 9728, [32, GW])
    LGA = at("LGA", "whi", 12416, [P, 3, GW])
    EE = at("EE", "whi", 8320, [P, 4, GW])
    ED = at("ED", "whi", 16000, [P, 2, 2])
    KG = at("KG", "wlo", 0, [P, 4, GW])
    TG = at("TG", "wlo", 4096, [P, 6, P])
    ATG = at("ATG", "wlo", 7168, [P, 4, P])
    SGS = at("SGS", "wlo", 9216, [P, 2, GD])
    fin_g = Finish("gl", "wlo", 10752, 6, GLW)
    gl = {n: sem(f"gl_{n}") for n in (
        "in0", "in1", "par", "zero", "gt", "gtc", "pre", "ab", "ex", "ln", "la", "cum", "ee", "kg", "tr", "trc",
        "a", "at", "s", "kv")}
    O_DQ, O_DK, O_DV, O_DZ = C_DQ - C_DG, C_DK - C_DG, C_DV - C_DG, C_DZ - C_DG
    RANK = 16

    GLA_LEAD = 0.68

    def sp_gla(sp):
        yield -1
        sp.wait_ge(*mm_done(gemms["pch"].end))
        sp.dma_start(W2A[0:RANK, :], I["gla_w_gate2_2"][0]).then_inc(*gl["par"].by(16))
        sp.dma_start(W2A[RANK:RANK + 1, :], I["gla_gate_bias_2"]).then_inc(*gl["par"].by(16))
        for t in range(TT):
            yield max(-1, t - GLA_LEAD - 0.4)
            if t >= 2:
                sp.wait_ge(*fin_g.av(t - 1))
                sp.wait_ge(*fin_g.zs(t - 1))
            sp.dma_start(GP[:, t % 2, :], ptok_d[t * P:(t + 1) * P, C_DG:C_TOK]).then_inc(*gl[f"in{t % 2}"].by(16))

    def pe_gla(pe):
        T = nc.tensor
        yield -0.9
        pe.wait_ge(*sg_hi(TT))
        pe.wait_ge(*gl["par"](32))
        pe.wait_ge(*gl["zero"](3))
        for t in range(TT):
            b = t % 2
            s = t - GLA_LEAD
            yield s + 0.05
            pe.wait_ge(*gl[f"in{b}"](16 * (t // 2 + 1)))
            if t:
                pe.wait_ge(*fin_g.og(t))
                pe.wait_ge(*fin_g.q(t))
                pe.wait_ge(*gl["s"](6 * t))
            T.transpose(PS[0:RANK, 5, 0:P], GP[:, b, 0:RANK], ident).then_inc(*gl["gt"].by(1))
            yield s + 0.08
            pe.wait_ge(*gl["gtc"](t + 1))
            T.matmul(PS[:, 5, P:P + GW], GTT[0:RANK + 1, :], W2A[0:RANK + 1, :], start=True, stop=True).then_inc(*gl["pre"].by(1))
            yield s + 0.17
            pe.wait_ge(*gl["la"](t + 1))
            la = LGA[:, 2, :]
            T.matmul(PS[:, 6, 0:GW], K["frommid"], la, start=True, stop=True)
            T.matmul(PS[:, 6, GW:2 * GW], K["upto"], la, start=True, stop=True)
            T.matmul(PS[:, 7, 0:GW], K["later"], la, start=True, stop=True)
            for c, name in enumerate(("first", "second")):
                for p in range(2):
                    ins = T.matmul(PS[:, 7, GW + 2 * c + p:GW + 2 * c + p + 1], la[:, p * P:(p + 1) * P],
                                   K[name][:, 0:1], start=True, stop=True)
            ins.then_inc(*gl["cum"].by(1))
            yield s + 0.3
            pe.wait_ge(*gl["kg"](t + 1))
            for n, (slot, p) in enumerate(((0, 0), (0, 1), (1, 0), (1, 1), (2, 0), (2, 1))):
                ins = T.transpose(PS_T(6)[:, n, :], KG[:, slot, p * P:(p + 1) * P], ident)
            ins.then_inc(*gl["tr"].by(1))
            yield s + 0.36
            pe.wait_ge(*gl["trc"](t + 1))
            for h in range(GH):
                lo, p = 64 * (h % 2), h // 2
                ins = T.matmul(PS[:, 6 + h % 2, p * P:(p + 1) * P], TG[lo:lo + 64, 2 + p, :], TG[lo:lo + 64, p, :],
                               start=True, stop=True)
            ins.then_inc(*gl["a"].by(1))
            for c in range(2):
                r = slice(64 * c, 64 * c + 64)
                for p in range(2):
                    ins = T.matmul(PS[:, 6 + c, (2 + p) * P:(3 + p) * P], KG[r, 3, p * P:(p + 1) * P],
                                   GP[r, b, O_DV + p * P:O_DV + (p + 1) * P], start=True, stop=True)
                ins.then_inc(*gl["kv"].by(1))
            for c in range(2):
                yield s + 0.45 + 0.05 * c
                r = slice(64 * c, 64 * c + 64)
                pe.wait_ge(*gl["at"](t + 1))
                pe.wait_ge(*gl["s"](3 * (2 * t + c)))
                for h in range(GH):
                    lo, p = 64 * (h % 2), h // 2
                    ins = T.matmul(PS[r, 6 + h % 2, p * GD:(p + 1) * GD], TG[lo:lo + 64, 4 + p, r], SGS[lo:lo + 64, p, :],
                                   start=True, stop=True)
                ins.then_inc(*(fin_g.q_t if c else gl["kv"]).by(1))
            yield s + 0.54
            for h in range(GH):
                ins = T.matmul(PS[:, 5, h * GD:(h + 1) * GD], ATG[:, order(h), :],
                               GP[:, b, O_DV + h * GD:O_DV + (h + 1) * GD], start=True, stop=True)
            ins.then_inc(*fin_g.av.by(1))
            yield s + 0.65
            fin_g.pe_turn(pe, t, 5)

    def act_gla(act):
        inv = 1.0 / 16.0
        for t in range(TT):
            b = t % 2
            s = t - GLA_LEAD
            yield s + 0.06
            act.wait_ge(*gl["gt"](t + 1))
            act.wait_ge(*gl["zero"](3))
            act.activation(GTT[0:RANK, :], PS[0:RANK, 5, 0:P], ACT.Copy).then_inc(*gl["gtc"].by(1))
            fin_g.act_z(act, t, GP[:, b, O_DZ:O_DZ + GW])
            yield s + 0.12
            act.wait_ge(*gl["ab"](t + 1))
            act.activation(LGA[:, 1, :], LGA[:, 0, :], ACT.Exp, scale=-1.0).then_inc(*gl["ex"].by(1))
            act.wait_ge(*gl["ex"](t + 1))
            act.activation(LGA[:, 0, :], LGA[:, 1, :], ACT.Ln, bias=1.0).then_inc(*gl["ln"].by(1))
            yield s + 0.2
            act.wait_ge(*gl["cum"](t + 1))
            act.activation(EE[:, 0:2, :].rearrange("p a n -> p (a n)"), PS[:, 6, :], ACT.Exp, scale=inv)\
               .then_inc(*gl["ee"].by(1))
            act.activation(EE[:, 2, :], PS[:, 6, 0:GW], ACT.Exp, scale=-inv).then_inc(*gl["ee"].by(1))
            act.activation(EE[:, 3, :], PS[:, 7, 0:GW], ACT.Exp, scale=inv).then_inc(*gl["ee"].by(1))
            act.activation(ED[:, :, :].rearrange("p a n -> p (a n)"), PS[:, 7, GW:GW + 4], ACT.Exp, scale=inv)\
               .then_inc(*gl["ee"].by(1))
            yield s + 0.33
            act.wait_ge(*gl["tr"](t + 1))
            act.activation(TG[:, :, :], PS_T(6)[:, 0:6, :], ACT.Copy).then_inc(*gl["trc"].by(1))
            yield s + 0.55
            act.wait_ge(*gl["s"](6 * t + 6))
            fin_g.act_q(act, t, 6, 0)
            yield s + 0.6
            fin_g.act_root(act, t)
            yield s + 0.67
            fin_g.act_hi(act, t)

    def dve_gla(dve, chain):
        V = nc.vector
        MUL, ADD, SUB = ALU.mult, ALU.add, ALU.subtract
        yield -1
        dve.wait_ge(*mm_done(gemms["pch"].end))
        V.memset(GTT[:, :], 1.0).then_inc(*gl["zero"].by(1))
        V.memset(ATG[:, :, :], 0.0).then_inc(*gl["zero"].by(1))
        V.memset(SGS[:, :, :], 0.0).then_inc(*gl["zero"].by(1))
        dve.wait_ge(*gl["zero"](3))
        for t in range(TT):
            b = t % 2
            s = t - GLA_LEAD
            yield s + 0.1
            dve.wait_ge(*gl["pre"](t + 1))
            pre = PS[:, 5, P:P + GW]
            chain(V.tensor_copy(LGA[:, 1, :], pre))
            V.scalar_tensor_tensor(LGA[:, 0, :], LGA[:, 1, :], -1.0, LGA[:, 1, :], MUL, ALU.max).then_inc(*gl["ab"].by(1))
            yield s + 0.14
            dve.wait_ge(*gl["ln"](t + 1))
            V.scalar_tensor_tensor(LGA[:, 2, :], pre, 0.0, LGA[:, 0, :], ALU.min, SUB).then_inc(*gl["la"].by(1))
            yield s + 0.25
            dve.wait_ge(*gl["ee"](4 * t + 4))
            q, k = GP[:, b, O_DQ:O_DQ + GW], GP[:, b, O_DK:O_DK + GW]
            V.scalar_tensor_tensor(KG[:, 0, :], q, GD ** -0.5, EE[:, 0, :], MUL, MUL)
            V.scalar_tensor_tensor(KG[:, 2, :], q, GD ** -0.5, EE[:, 1, :], MUL, MUL)
            V.tensor_tensor(KG[:, 1, :], k, EE[:, 2, :], MUL)
            V.tensor_tensor(KG[:, 3, :], k, EE[:, 3, :], MUL).then_inc(*gl["kg"].by(1))
            yield s + 0.4
            dve.wait_ge(*gl["kv"](3 * t + 2))
            if t:
                dve.wait_ge(*fin_g.av(t))
            V.copy_predicated(ATG[:, :, :].rearrange("p (a q) c -> p a q c", a=2),
                              K["upto"].bitcast(I32).unsqueeze(1).unsqueeze(1).to_broadcast([P, 2, 2, P]),
                              PS[:, 6:8, 0:2 * P].rearrange("p a (q c) -> p a q c", q=2)).then_inc(*gl["at"].by(1))
            for c in range(2):
                n = 2 * t + c
                yield s + 0.48 + 0.05 * c
                if c == 0:
                    dve.wait_ge(*gl["kv"](3 * t + 3))
                else:
                    dve.wait_ge(*fin_g.q_t(t + 1))
                V.tensor_tensor(SGS[:, :, :], SGS[:, :, :], ED[:, c, :].unsqueeze(2).to_broadcast([P, 2, GD]), MUL)\
                    .then_inc(*gl["s"].by(1))
                dve.wait_ge(*gl["s"](3 * n + 1))
                for a in range(2):
                    h = slice(64 * a, 64 * a + 64)
                    V.tensor_tensor(SGS[h], SGS[h], PS[h, 6 + c, 2 * P:4 * P]
                                    .rearrange("p (q b d) -> p q b d", q=2, b=2)[:, :, a, :], ADD).then_inc(*gl["s"].by(1))
            yield s + 0.58
            yield from fin_g.dve_norm(dve, chain, t, 5, s + 0.61)
            yield s + 0.66
            fin_g.dve_gain(dve, t, 5)
            yield s + 0.68
            fin_g.dve_lo(dve, t)

    RAWD = at("RAWD", "stage", 0, [P, 2, D])
    GSB = at("GSB", "stage", 8192, [P, 2, HALF])
    AB = at("AB", "stage", 12288, [P, 2, HALF])
    flat2 = lambda ap: ap.rearrange("p k n -> p (k n)").rearrange("p (f n) -> p f n", f=2)
    WD_HI, WD_LO = flat2(W_HI[:, 1, 0:4, :]), flat2(W_LO[:, 1, 0:4, :])
    A_HI, A_LO = flat2(W_HI[:, 1, 4:8, :]), flat2(W_LO[:, 1, 4:8, :])
    ff_raw = [sem("ff_raw0"), sem("ff_raw1"), sem("ff_raw_down")]
    ff_whi, ff_split = sem("ff_whi"), sem("ff_split")
    ff_gu, ff_silu, ff_ab, ff_ahi, ff_alo, ff_dn, ff_x = (
        sem(n) for n in ("ff_gu", "ff_silu", "ff_ab", "ff_ahi", "ff_alo", "ff_dn", "ff_x"))
    wgu, wdn = I["w_gate_up_2"][0], I["w_down_2"][0]

    def sp_ffn(sp):
        sp.wait_ge(*w_split(len(halves)))

        def load(i, first):
            for half in range(2):
                if not first:
                    sp.wait_ge(*ff_split(3 * i + half - 2))
                for m in range(2):
                    src = wgu[half * HALF:(half + 1) * HALF, bass.ds(i * 256 + m * FF, 256)]
                    sp.dma_start(RAW[:, half, :, m * 256:(m + 1) * 256], src.rearrange("(k p) n -> p k n", p=P))\
                      .then_inc(*ff_raw[half].by(16))
            if not first:
                sp.wait_ge(*ff_split(3 * i))
            sp.dma_start(RAWD[:, :, :], wdn[bass.ds(i * 256, 256), :].rearrange("(k p) n -> p k n", p=P))\
              .then_inc(*ff_raw[2].by(16))

        load(0, True)
        with sp.Fori(1, FFB) as i:
            load(i, False)

    def pool_ffn(pool):
        G = nc.gpsimd
        pool.wait_ge(*mm_done(gemms["out2"].end))
        for i in range(FFB):
            def split(part, raw, hi, lo):
                G.tensor_scalar(hi, raw, 1.0, 1.0, ALU.mult, ALU.mult).then_inc(*ff_whi.by(1))
                pool.wait_ge(*ff_whi(3 * i + part + 1))
                G.tensor_tensor(lo, raw, hi.bitcast(F32), ALU.subtract).then_inc(*ff_split.by(1))

            if i:
                pool.wait_ge(*ff_gu(4 * i))
            for half in range(2):
                pool.wait_ge(*ff_raw[half](32 * i + 32))
                ks = slice(4 * half, 4 * half + 4)
                split(half, RAW[:, half], W_HI[:, 0, ks, :], W_LO[:, 0, ks, :])
            if i:
                pool.wait_ge(*ff_dn(16 * i))
            pool.wait_ge(*ff_raw[2](16 * i + 16))
            split(2, RAWD[:, :, :], WD_HI, WD_LO)

    def pe_ffn(pe):
        T = nc.tensor
        pe.wait_ge(*op_lo_done(turned_base(5) + TT))
        pe.wait_ge(*bank_dve(gemms["out2"].free1_dve))

        def turn(i, first=False):
            pe.wait_ge(*ff_split(3 * i + 2))
            for u in range(4):
                th, f = u // 2, u % 2
                if not (first and u < 2):
                    pe.wait_ge(*ff_ab(4 * i + u - 1))
                for m in range(2):
                    bank = 2 * (u % 2) + m
                    for n, (w, x) in enumerate(((W_HI, OP_HI), (W_LO, OP_HI), (W_HI, OP_LO))):
                        for k in range(KT):
                            ins = T.matmul(PS[:, bank, :], w[:, 0, k, m * 256 + f * P:m * 256 + (f + 1) * P],
                                           x[:, k, th * HALF:(th + 1) * HALF],
                                           start=n == 0 and k == 0, stop=n == 2 and k == KT - 1)
                ins.then_inc(*ff_gu.by(1))
            pe.wait_ge(*ff_split(3 * i + 3))
            for v in range(16):
                t, c = v // 2, v % 2
                if v == 0:
                    pe.wait_ge(*ff_alo(4 * i + 2))
                if v == 8:
                    pe.wait_ge(*ff_alo(4 * i + 4))
                if not (first and v < 4):
                    pe.wait_ge(*ff_x(16 * i + v - 3))
                for n, (a, w) in enumerate(((A_HI, WD_HI), (A_HI, WD_LO), (A_LO, WD_HI))):
                    for f in range(2):
                        ins = T.matmul(PS[:, 4 + v % 4, :], a[:, f, t * P:(t + 1) * P],
                                       w[:, f, c * HALF:(c + 1) * HALF], start=n == 0 and f == 0,
                                       stop=n == 2 and f == 1)
                ins.then_inc(*ff_dn.by(1))

        turn(0, first=True)
        with pe.Fori(1, FFB) as i:
            turn(i)

    def act_ffn(act):
        def turn(i, first=False):
            for u in range(4):
                th, f = u // 2, u % 2
                act.wait_ge(*ff_gu(4 * i + u + 1))
                act.activation(GSB[:, u % 2, :], PS[:, 2 * (u % 2), :], ACT.Silu).then_inc(*ff_silu.by(1))
                act.wait_ge(*ff_ab(4 * i + u + 1))
                if u == 0 and not first:
                    act.wait_ge(*ff_dn(16 * i))
                act.activation(A_HI[:, f, th * HALF:(th + 1) * HALF], AB[:, u % 2, :], ACT.Copy).then_inc(*ff_ahi.by(1))

        turn(0, first=True)
        with act.Fori(1, FFB) as i:
            turn(i)

    def dve_ffn(dve):
        V = nc.vector
        with dve.Fori(0, FFB) as i:
            for u in range(4):
                th, f = u // 2, u % 2
                dve.wait_ge(*ff_silu(4 * i + u + 1))
                V.tensor_tensor(AB[:, u % 2, :], PS[:, 2 * (u % 2) + 1, :], GSB[:, u % 2, :], ALU.mult)\
                    .then_inc(*ff_ab.by(1))
                dve.wait_ge(*ff_ahi(4 * i + u + 1))
                V.tensor_tensor(A_LO[:, f, th * HALF:(th + 1) * HALF], AB[:, u % 2, :],
                                A_HI[:, f, th * HALF:(th + 1) * HALF].bitcast(F32), ALU.subtract).then_inc(*ff_alo.by(1))
            for v in range(16):
                t, c = v // 2, v % 2
                dve.wait_ge(*ff_dn(16 * i + v + 1))
                V.tensor_tensor(X[:, t, c * HALF:(c + 1) * HALF], X[:, t, c * HALF:(c + 1) * HALF],
                                PS[:, 4 + v % 4, :], ALU.add).then_inc(*ff_x.by(1))

    done = lambda name: (mm_done, gemms[name].end)
    tok_to = lambda dram_: (lambda b, a, h, w: dram_[a * P:(a + 1) * P, b * HALF:b * HALF + w])
    ch_to = lambda dram_: (lambda b, a, h, w: dram_[(4 * b + a) * P:(4 * b + a + 1) * P, h * HALF:h * HALF + w])
    last_column_block = lambda name: (bank_dve, gemms[name].free1_dve - TT + 1)
    x_view = rows_of(I["x"][0])

    with nc.Block() as block:
        @block.sync
        def _(sp):
            sp.dma_start(CONST[:, :], I["c_base"]).then_inc(*consts_in.by(16))
            sp_s5_tables(sp)
            sp_weights(sp, weights_before("xk"))
            sp_columns(sp)
            sp_gain(sp, 1, ready=[(xn_full, 2), (s5_out, S5_STORES)])
            sp.dma_start(X[:, :, :], x_view).then_inc(*x_in.by(16))
            sp_weights(sp, weights_before("qk"))
            together(sp_weights_steps(sp, 2 * gemms["gret"].first_block + 4, gemms["qk"].first_block), sp_s5_in(sp))
            sp_weights(sp, weights_before("glu"))
            sp_s5_y(sp)
            wait_stores(sp, "gs5")
            retention = sp_retention(sp)
            first_part(retention)
            together(sp_weights_steps(sp, 2 * gemms["out_ret"].first_block + 4, gemms["glu"].first_block), sp_glu(sp))
            for s in glu_out:
                sp.wait_ge(*s(16 * 8))
            alone(retention)
            sp.wait_ge(*r_lo(TT))
            sp.dma_start(X[:, :, :], x_view).then_inc(*x_in.by(16))
            together(sp_load_operand(sp, st_d),
                     sp_weights_steps(sp, weights_before("out_s5"), gemms["out_ret"].first_block))
            sp_gain(sp, 2)
            sp_weights(sp, weights_before("xq"))
            sp.wait_ge(*bank_dve(gemms["out_s5"].free1_dve))
            sp.wait_ge(*xn_full(turned_base(2) + TT))
            sp.dma_start(rows_of(x1_d), X[:, :, :]).then_inc(*x_out.by(16))
            sp_gain(sp, 3)
            sp_weights(sp, weights_before("xo"))
            sp.wait_ge(*x_out(16))
            sp_attention(sp)
            sp.wait_ge(*xa_lo(TT))
            sp.dma_start(X[:, :, :], rows_of(x1_d)).then_inc(*x_in.by(16))
            sp_weights(sp, weights_before("ptok"))
            sp.wait_ge(*inplace(TT))
            sp_gain(sp, 4)
            sp.dma_start(rows_of(x2_d), X[:, :, :]).then_inc(*x_out.by(16))
            sp_weights(sp, 2 * gemms["pch"].first_block + 4)
            together(sp_weights_steps(sp, 2 * gemms["out2"].first_block + 2, gemms["pch"].first_block), sp_sgu(sp),
                     sp_short_conv(sp))
            together(sp_conv(sp), sp_delta(sp), sp_gla(sp))
            sp.wait_ge(*fin_d.lo(TT))
            sp_weights(sp, len(halves))
            sp.dma_start(X[:, :, :], rows_of(x2_d)).then_inc(*x_in.by(16))
            sp_gain(sp, 5)
            sp_ffn(sp)
            sp.wait_ge(*xn_full(turned_base(5) + TT))
            sp_gain(sp, 6)
            for t in range(TT):
                sp.wait_ge(*inplace(TT + t + 1))
                sp.dma_start(out[0, t * P:(t + 1) * P, :], X[:, t, :]).then_inc(*x_out.by(16))
            sp.wait_ge(*x_out(32 + 16 * TT))

        @block.gpsimd
        def _(pool):
            pool_s5_tables(pool, None)
            pool.wait_ge(*s5_zero_out(16 * (SC - 1)))
            pool.wait_ge(*s5_bt_out(16))
            pool.wait_ge(*s5_r(1))
            pool_split_all(pool)
            pool_ffn(pool)

        @block.scalar
        def _(act):
            act_s5_tables(act)
            act.wait_ge(*s5_cpw(4 * SC))
            act.wait_ge(*s5_r(1))
            act_norm_stats(act, 0, ready=(x_in, 16), tiles=2)
            act_norm_hi(act, 0, free=[(s5_out, S5_STORES)], tiles=2)
            act_gemm_store(act, "xk", lambda b, a, h, w: ka_d[(4 * b + a) * P:(4 * b + a + 1) * P, :])
            act_norm_stats(act, 1, ready=(x_in, 32), root=False)
            act_gemm_store(act, "xv", tok_to(va_d))
            act_norm_root(act, 1)
            act_norm_hi(act, 1, free=[done("xv")])
            act_gemm_store(act, "u", tok_to(u_d))
            together(one_after_other(act_gemm_store_steps(act, "qk", tok_to(qk_d)), 2 * TT,
                                     act_gemm_store_steps(act, "v", tok_to(v_d))), act_s5_in(act))
            act_gemm_store(act, "gret", ch_to(gret_d), func=ACT.Silu)
            act_gemm_store(act, "gs5", ch_to(gs5_d), func=ACT.Silu)
            act_s5_y(act)
            act_split_y(act)
            retention = act_retention(act)
            first_part(retention)
            act_glu(act)
            alone(retention)
            act.wait_ge(*mm_done(gemms["out_ret"].end))
            act_load_operand(act)
            act_norm_stats(act, 2, ready=last_column_block("out_s5"), step=1)
            act_norm_hi(act, 2, free=[done("out_s5")])
            act_gemm_store(act, "xq", ch_to(qa_d))
            together(act_attention_scores(act), act_attention_outputs(act))
            act_norm_stats(act, 3, ready=last_column_block("xo"), step=1)
            act_norm_stats(act, 4, ready=(inplace, 1), step=1)
            act_norm_hi(act, 4, free=[done("xo")])
            act_gemm_store(act, "ptok", lambda b, a, h, w: ptok_d[a * P:(a + 1) * P, PTOK0[b]:PTOK0[b] + w])
            together(act_gemm_store_steps(act, "pch", ch_to(pch_d)), act_sgu(act), act_short_conv(act))
            together(act_conv(act), act_delta_prepare(act), act_delta_head(act), act_delta_tail(act), act_gla(act))
            act_norm_stats(act, 5, ready=last_column_block("out2"), step=1)
            act_norm_hi(act, 5, free=[done("out2")])
            act_ffn(act)
            act_norm_stats(act, 6, ready=(ff_x, 16 * (FFB - 1) + 2), step=2)

        @block.vector
        def _(dve):
            chain = Chain(dve, sem("dve_chain"))
            dve_s5_tables(dve, chain)
            dve_norm_split(dve, 0, chain, tiles=2)
            dve_split_first(dve)
            dve_norm_split(dve, 1, chain)
            dve_s5_in(dve)
            dve_s5_scan(dve)
            dve_s5_y(dve)
            dve_split_y(dve)
            retention = dve_retention(dve, chain)
            first_part(retention)
            dve_glu(dve)
            alone(retention)
            dve.wait_ge(*x_in(48))
            dve_gemm_add(dve, "out_ret")
            dve_load_operand(dve)
            dve_gemm_add(dve, "out_s5")
            dve_norm_split(dve, 2, chain)
            together(dve_attention_scores(dve, chain), dve_attention_outputs(dve))
            dve.wait_ge(*x_in(64))
            dve_gemm_add(dve, "xo")
            dve_norm_inplace(dve, 3, chain)
            dve_norm_split(dve, 4, chain)
            dve.wait_ge(*x_out(32))
            dve.wait_ge(*pc_in(PC_LOADED))
            together(dve_sgu(dve, chain), dve_short_conv(dve, chain))
            together(dve_conv(dve, chain), dve_delta_prepare(dve, chain), dve_delta_head(dve, chain), dve_delta_tail(dve, chain), dve_gla(dve, chain))
            dve.wait_ge(*x_in(80))
            dve_gemm_add(dve, "out2")
            dve_norm_split(dve, 5, chain)
            dve_ffn(dve)
            dve_norm_inplace(dve, 6, chain)

        @block.tensor
        def _(pe):
            pe_s5_tables(pe)
            pe_norm(pe, 0, tiles=2)
            pe_gemm(pe, "xk", ready=[(op_lo_done, 2)])
            pe_gemm(pe, "xv")
            pe_norm(pe, 1)
            pe_gemm(pe, "u", ready=[(op_lo_done, turned_base(1) + TT)])
            together(one_after_other(pe_gemm_steps(pe, "qk"), 2 * TT, pe_gemm_steps(pe, "v")), pe_s5_in(pe))
            pe_gemm(pe, "gret")
            pe_gemm(pe, "gs5")
            pe_s5_y(pe)
            pe_gemm(pe, "glu", ready=[(la_lo, KT)])
            pe_retention(pe)
            pe_gemm(pe, "out_ret", ready=[(r_lo, TT)])
            pe_gemm(pe, "out_s5", ready=[(la_lo, 2 * KT)])
            pe_norm(pe, 2)
            pe_gemm(pe, "xq", ready=[(op_lo_done, turned_base(2) + TT)])
            together(pe_attention_scores(pe), pe_attention_outputs(pe))
            pe_gemm(pe, "xo", ready=[(xa_lo, TT)])
            pe_norm(pe, 4)
            pe_gemm(pe, "ptok", ready=[(op_lo_done, turned_base(4) + TT)])
            together(pe_gemm_steps(pe, "pch"), pe_sgu(pe))
            pe.wait_ge(*bank_act(gemms["pch"].free1_act))
            together(pe_conv(pe), pe_delta_head(pe), pe_delta_tail(pe), pe_gla(pe))
            pe_gemm(pe, "out2", ready=[(fin_d.lo, TT), (fin_g.lo, TT)])
            pe_norm(pe, 5)
            pe_ffn(pe)

    for before, total in SHARED.values():
        assert sems[before].count == total, (before, sems[before].count, total)


INPUTS = [
    "x", "mem", "positions", "norm1_g", "w_in", "ret_gn_g", "s5_a_re", "s5_a_im", "s5_log_dt", "s5_b_re",
    "s5_b_im", "s5_c_re", "s5_c_im", "s5_d", "s5_glu_w", "s5_glu_b", "w_out", "norm2_g", "norm_mem_g", "xa_wq",
    "xa_wk", "xa_wv", "xa_wo", "norm_f_g", "norm1_w_2", "w_in_2", "sgu_ln_w_2", "sgu_ln_b_2",
    "sgu_w_spatial_2", "sgu_b_spatial_2", "sc_conv_w_2", "dn_conv_w_2", "dn_a_log_2", "dn_dt_bias_2",
    "dn_norm_w_2", "gla_w_gate2_2", "gla_gate_bias_2", "gla_norm_w_2", "w_out_2", "norm2_w_2",
    "w_gate_up_2", "w_down_2", "final_norm_w_2",
]


def kernel(**inputs):
    import concourse.bacc as bacc
    from concourse.bass_utils import run_bass_kernel_spmd

    nc = bacc.Bacc("TRN2", target_bir_lowering=False, num_devices=1)
    arrays = {name: np.ascontiguousarray(inputs[name]) for name in INPUTS}
    base, _, ret, place = shape_constants()
    arrays["c_base"], arrays["c_ret"], arrays["c_place"] = base, ret, place
    I = {n: nc.dram_tensor(f"in_{n}", a.shape, mybir.dt.from_np(a.dtype), kind="ExternalInput").ap()
         for n, a in arrays.items()}
    out = nc.dram_tensor("out", (1, L, D), F32, kind="ExternalOutput").ap()
    build(nc, I, out)
    r = run_bass_kernel_spmd(nc, [{f"in_{n}": a for n, a in arrays.items()}], core_ids=[0])
    return r.results[0]["out"]
```
